# Optimizing a Trainium2 kernel written in Bass

```python
import math
import jax, jax.numpy as jnp
from jax import lax
import numpy as np

D_MODEL = 1024
BATCH = 1
SEQ = 256
DEPTH = 2

CHUNK = 64
SSM_WIDTH = D_MODEL // 4
SSM_GROUP = 16
SSM_GROUPS = SSM_WIDTH // SSM_GROUP
SSM_STATE = 64
GMLP_WIDTH = D_MODEL // 4
GMLP_HEADS = 4
GMLP_HEAD_DIM = GMLP_WIDTH // GMLP_HEADS
GMLP_WINDOW = 128
DIFF_WIDTH = D_MODEL // 2
DIFF_HEADS = 4
DIFF_VDIM = DIFF_WIDTH // DIFF_HEADS
DIFF_QK_DIM = DIFF_VDIM // 2
MIX_WIDTH = SSM_WIDTH + GMLP_WIDTH + DIFF_WIDTH
IN_COLS = SSM_WIDTH + 2 * GMLP_WIDTH + 3 * DIFF_WIDTH
D_FF = ((8 * D_MODEL // 3 + 127) // 128) * 128
CONV_WIDTH = 3
ROPE_THETA = 10000.0
Q_BLOCK = 128
EPS = 1e-6


def rms_norm(x, g):
    xf = x.astype(jnp.float32)
    y = xf * lax.rsqrt(jnp.mean(xf * xf, axis=-1, keepdims=True) + EPS)
    return (y * g.astype(jnp.float32)).astype(x.dtype)

def rope_tables(seq):
    half = DIFF_QK_DIM // 2
    inv = ROPE_THETA ** (-jnp.arange(half, dtype=jnp.float32) / half)
    ang = jnp.arange(seq, dtype=jnp.float32)[:, None] * inv[None, :]
    ang = jnp.concatenate([ang, ang], axis=-1)
    return jnp.cos(ang), jnp.sin(ang)

def apply_rope(x, cos, sin):
    x1, x2 = jnp.split(x, 2, axis=-1)
    rot = jnp.concatenate([-x2, x1], axis=-1)
    c = cos[None, :, None, None, :]
    s = sin[None, :, None, None, :]
    return (x.astype(jnp.float32) * c + rot.astype(jnp.float32) * s).astype(x.dtype)

def s5_mixer(u, a_re, a_im, log_dt, b_re, b_im, c_re, c_im, d_skip, w_glu, b_glu):
    bsz, seq, _ = u.shape
    uf = u.astype(jnp.float32).reshape(bsz, seq, SSM_GROUPS, SSM_GROUP)
    lam = lax.complex(a_re.astype(jnp.float32), a_im.astype(jnp.float32))
    dt = jnp.exp(log_dt.astype(jnp.float32))[:, None]
    a_bar = jnp.exp(lam * dt)
    b_mat = lax.complex(b_re.astype(jnp.float32), b_im.astype(jnp.float32))
    b_bar = ((a_bar - 1.0) / lam)[..., None] * b_mat
    bu = jnp.einsum("bsgh,gph->bsgp", uf.astype(jnp.complex64), b_bar)

    def combine(left, right):
        a_l, b_l = left
        a_r, b_r = right
        return a_l * a_r, a_r * b_l + b_r

    a_seq = jnp.broadcast_to(a_bar, (1, seq) + a_bar.shape)
    _, states = lax.associative_scan(combine, (a_seq, bu), axis=1)
    c_mat = lax.complex(c_re.astype(jnp.float32), c_im.astype(jnp.float32))
    y = jnp.real(jnp.einsum("bsgp,ghp->bsgh", states, c_mat))
    y = y + d_skip.astype(jnp.float32).reshape(SSM_GROUPS, SSM_GROUP) * uf
    y = jax.nn.gelu(y.reshape(bsz, seq, SSM_WIDTH))
    y = y * jax.nn.sigmoid(y @ w_glu.astype(jnp.float32) + b_glu.astype(jnp.float32))
    return y.astype(u.dtype)

def spatial_gating(u, v, v_gain, w_s, b_s):
    bsz, seq, _ = u.shape
    v = rms_norm(v, v_gain)
    nwin = seq // GMLP_WINDOW
    v = v.reshape(bsz, nwin, GMLP_WINDOW, GMLP_HEADS, GMLP_HEAD_DIM)
    pos_chunk = jnp.arange(GMLP_WINDOW) // CHUNK
    mask = pos_chunk[None, :] <= pos_chunk[:, None]
    w = jnp.where(mask[None], w_s, 0).astype(v.dtype)
    mixed = jnp.einsum("hij,bnjhc->bnihc", w, v)
    mixed = mixed + b_s.astype(v.dtype).T[None, None, :, :, None]
    return u * mixed.reshape(bsz, seq, GMLP_WIDTH)

def diff_attention(q, k, v, q_gain, k_gain, lam_q1, lam_k1, lam_q2, lam_k2, sub_gain, lambda_init):
    bsz, seq, _ = q.shape
    q = q.reshape(bsz, seq, DIFF_HEADS, 2, DIFF_QK_DIM)
    k = k.reshape(bsz, seq, DIFF_HEADS, 2, DIFF_QK_DIM)
    v = v.reshape(bsz, seq, DIFF_HEADS, DIFF_VDIM)
    q = rms_norm(q, q_gain)
    k = rms_norm(k, k_gain)
    cos, sin = rope_tables(seq)
    q = apply_rope(q, cos, sin)
    k = apply_rope(k, cos, sin)
    lam = (jnp.exp(jnp.sum(lam_q1.astype(jnp.float32) * lam_k1.astype(jnp.float32)))
           - jnp.exp(jnp.sum(lam_q2.astype(jnp.float32) * lam_k2.astype(jnp.float32)))
           + lambda_init)
    nblk = seq // Q_BLOCK
    q_blocks = jnp.moveaxis(q.reshape(bsz, nblk, Q_BLOCK, DIFF_HEADS, 2, DIFF_QK_DIM), 1, 0)
    key_chunk = jnp.arange(seq) // CHUNK
    scale = DIFF_QK_DIM ** -0.5

    def block(args):
        qb, blk = args
        q_chunk = (blk * Q_BLOCK + jnp.arange(Q_BLOCK)) // CHUNK
        mask = key_chunk[None, :] <= q_chunk[:, None]
        s = jnp.einsum("bqhcd,bkhcd->bhcqk", qb, k).astype(jnp.float32) * scale
        s = jnp.where(mask, s, -jnp.inf)
        p = jax.nn.softmax(s, axis=-1)
        w = (p[:, :, 0] - lam * p[:, :, 1]).astype(v.dtype)
        return jnp.einsum("bhqk,bkhe->bqhe", w, v)

    out = lax.map(block, (q_blocks, jnp.arange(nblk)))
    out = jnp.moveaxis(out, 0, 1).reshape(bsz, seq, DIFF_HEADS, DIFF_VDIM)
    out = rms_norm(out, sub_gain) * (1.0 - lambda_init)
    return out.reshape(bsz, seq, DIFF_WIDTH)

def conv_gated_mlp(x, w_up, conv_w, conv_b, w_down):
    seq = x.shape[1]
    h = x @ w_up
    hp = jnp.pad(h, ((0, 0), (CONV_WIDTH - 1, 0), (0, 0)))
    acc = conv_b
    for i in range(CONV_WIDTH):
        acc = acc + conv_w[i] * hp[:, i:i + seq]
    gate, val = jnp.split(acc, 2, axis=-1)
    return (jax.nn.gelu(gate) * val) @ w_down

def first_inputs(seed: int = 0) -> dict:
    key = jax.random.key(seed)
    ks = iter(jax.random.split(key, 40))

    def nrm(shape, std):
        return jax.random.normal(next(ks), shape, jnp.float32) * std

    L, G, P, C = DEPTH, SSM_GROUPS, SSM_STATE, SSM_GROUP
    x = nrm((BATCH, SEQ, D_MODEL), 1.0)
    attn_norm_g = 1.0 + nrm((L, D_MODEL), 0.02)
    w_in = nrm((L, D_MODEL, IN_COLS), D_MODEL ** -0.5)
    ssm_a_re = -0.5 + nrm((L, G, P), 0.01)
    ssm_a_im = jnp.pi * jnp.arange(P, dtype=jnp.float32)[None, None, :] + nrm((L, G, P), 0.01)
    ssm_log_dt = jax.random.uniform(next(ks), (L, G), jnp.float32, math.log(1e-3), math.log(1e-1))
    ssm_b_re = nrm((L, G, P, C), (2 * C) ** -0.5)
    ssm_b_im = nrm((L, G, P, C), (2 * C) ** -0.5)
    ssm_c_re = nrm((L, G, C, P), P ** -0.5)
    ssm_c_im = nrm((L, G, C, P), P ** -0.5)
    ssm_d = nrm((L, SSM_WIDTH), 1.0)
    ssm_w_glu = nrm((L, SSM_WIDTH, SSM_WIDTH), SSM_WIDTH ** -0.5)
    ssm_b_glu = nrm((L, SSM_WIDTH), 0.02)
    gmlp_v_g = 1.0 + nrm((L, GMLP_WIDTH), 0.02)
    gmlp_w_s = nrm((L, GMLP_HEADS, GMLP_WINDOW, GMLP_WINDOW), GMLP_WINDOW ** -0.5)
    gmlp_b_s = 1.0 + nrm((L, GMLP_HEADS, GMLP_WINDOW), 0.02)
    q_norm_g = 1.0 + nrm((L, DIFF_QK_DIM), 0.02)
    k_norm_g = 1.0 + nrm((L, DIFF_QK_DIM), 0.02)
    lambda_q1 = nrm((L, DIFF_QK_DIM), 0.1)
    lambda_k1 = nrm((L, DIFF_QK_DIM), 0.1)
    lambda_q2 = nrm((L, DIFF_QK_DIM), 0.1)
    lambda_k2 = nrm((L, DIFF_QK_DIM), 0.1)
    subln_g = 1.0 + nrm((L, DIFF_VDIM), 0.02)
    w_out = nrm((L, MIX_WIDTH, D_MODEL), MIX_WIDTH ** -0.5)
    ffn_norm_g = 1.0 + nrm((L, D_MODEL), 0.02)
    w_up = nrm((L, D_MODEL, 2 * D_FF), D_MODEL ** -0.5)
    conv_w = nrm((L, CONV_WIDTH, 2 * D_FF), CONV_WIDTH ** -0.5)
    conv_b = nrm((L, 2 * D_FF), 0.02)
    w_down = nrm((L, D_FF, D_MODEL), D_FF ** -0.5)
    return {"x": x, "attn_norm_g": attn_norm_g, "w_in": w_in,
            "ssm_a_re": ssm_a_re, "ssm_a_im": ssm_a_im, "ssm_log_dt": ssm_log_dt,
            "ssm_b_re": ssm_b_re, "ssm_b_im": ssm_b_im, "ssm_c_re": ssm_c_re, "ssm_c_im": ssm_c_im,
            "ssm_d": ssm_d, "ssm_w_glu": ssm_w_glu, "ssm_b_glu": ssm_b_glu,
            "gmlp_v_g": gmlp_v_g, "gmlp_w_s": gmlp_w_s, "gmlp_b_s": gmlp_b_s,
            "q_norm_g": q_norm_g, "k_norm_g": k_norm_g,
            "lambda_q1": lambda_q1, "lambda_k1": lambda_k1, "lambda_q2": lambda_q2, "lambda_k2": lambda_k2,
            "subln_g": subln_g, "w_out": w_out, "ffn_norm_g": ffn_norm_g,
            "w_up": w_up, "conv_w": conv_w, "conv_b": conv_b, "w_down": w_down}

def first_block(x, attn_norm_g, w_in, ssm_a_re, ssm_a_im, ssm_log_dt, ssm_b_re, ssm_b_im,
              ssm_c_re, ssm_c_im, ssm_d, ssm_w_glu, ssm_b_glu, gmlp_v_g, gmlp_w_s, gmlp_b_s,
              q_norm_g, k_norm_g, lambda_q1, lambda_k1, lambda_q2, lambda_k2, subln_g, w_out,
              ffn_norm_g, w_up, conv_w, conv_b, w_down):
    o1 = SSM_WIDTH
    o2 = o1 + GMLP_WIDTH
    o3 = o2 + GMLP_WIDTH
    o4 = o3 + DIFF_WIDTH
    o5 = o4 + DIFF_WIDTH
    h = x
    for layer in range(DEPTH):
        lambda_init = 0.8 - 0.6 * math.exp(-0.3 * layer)
        xn = rms_norm(h, attn_norm_g[layer])
        proj = xn @ w_in[layer]
        u_ssm, u_g, v_g, q, k, v = jnp.split(proj, [o1, o2, o3, o4, o5], axis=-1)
        y_ssm = s5_mixer(u_ssm, ssm_a_re[layer], ssm_a_im[layer], ssm_log_dt[layer],
                         ssm_b_re[layer], ssm_b_im[layer], ssm_c_re[layer], ssm_c_im[layer],
                         ssm_d[layer], ssm_w_glu[layer], ssm_b_glu[layer])
        y_sgu = spatial_gating(u_g, v_g, gmlp_v_g[layer], gmlp_w_s[layer], gmlp_b_s[layer])
        y_diff = diff_attention(q, k, v, q_norm_g[layer], k_norm_g[layer],
                                lambda_q1[layer], lambda_k1[layer], lambda_q2[layer], lambda_k2[layer],
                                subln_g[layer], lambda_init)
        mixed = jnp.concatenate([y_ssm, y_sgu, y_diff], axis=-1)
        h = h + mixed @ w_out[layer]
        xn = rms_norm(h, ffn_norm_g[layer])
        h = h + conv_gated_mlp(xn, w_up[layer], conv_w[layer], conv_b[layer], w_down[layer])
    return h


DEPTH_2 = 1

HEAD_DIM = 64
BRANCH_WIDTH = D_MODEL // 2
A_GROUPS = ((128, 1), (512, 4), (2048, 16))
A_HEADS = BRANCH_WIDTH // HEAD_DIM
B_HEADS = BRANCH_WIDTH // HEAD_DIM
B_KV_HEADS = B_HEADS // 4
M_HEADS = 4
M_HEAD_DIM = BRANCH_WIDTH // M_HEADS
N_MEM = 256
GRID_W = 64
NORM_EPS = 1e-6
NEG_INF = -1e30
N_BRANCHES = 3

A_QKV = 3 * len(A_GROUPS) * A_HEADS * HEAD_DIM
B_Q = B_HEADS * HEAD_DIM
B_KV = B_KV_HEADS * HEAD_DIM
M_Q = M_HEADS * M_HEAD_DIM
SPLIT_SIZES = (A_QKV, B_Q, B_KV, B_KV, M_Q, BRANCH_WIDTH, BRANCH_WIDTH, BRANCH_WIDTH, N_BRANCHES * D_MODEL)
IN_WIDTH = A_QKV + B_Q + 2 * B_KV + M_Q + 3 * BRANCH_WIDTH + N_BRANCHES * D_MODEL


def rms_norm_2(x, g):
    xf = x.astype(jnp.float32)
    y = xf * lax.rsqrt(jnp.mean(xf * xf, axis=-1, keepdims=True) + NORM_EPS)
    return (y * g.astype(jnp.float32)).astype(x.dtype)

def rope(x, pos):
    dr = x.shape[-1]
    half = dr // 2
    inv = jnp.power(ROPE_THETA, -jnp.arange(half, dtype=jnp.float32) * 2.0 / dr)
    ang = pos.astype(jnp.float32)[:, None] * inv[None, :]
    cos = jnp.cos(ang)[:, None, :]
    sin = jnp.sin(ang)[:, None, :]
    xf = x.astype(jnp.float32)
    x1, x2 = xf[..., :half], xf[..., half:]
    return jnp.concatenate([x1 * cos - x2 * sin, x1 * sin + x2 * cos], axis=-1).astype(x.dtype)

def axial_rope(x, row_pos, col_pos):
    half = x.shape[-1] // 2
    return jnp.concatenate([rope(x[..., :half], row_pos), rope(x[..., half:], col_pos)], axis=-1)

def dilated_window_attention(q, k, v, window, dilation):
    b, s, h, dh = q.shape
    half = window // (2 * dilation)
    blk = half
    L = s // dilation
    nb = -(-L // blk)
    lp = nb * blk
    z = b * dilation

    def regroup(t):
        return t.reshape(b, L, dilation, h, dh).transpose(0, 2, 1, 3, 4).reshape(z, L, h, dh)

    qg, kg, vg = regroup(q), regroup(k), regroup(v)
    qb = jnp.pad(qg, ((0, 0), (0, lp - L), (0, 0), (0, 0))).reshape(z, nb, blk, h, dh)

    def band(t):
        tp = jnp.pad(t, ((0, 0), (blk, lp - L + blk), (0, 0), (0, 0))).reshape(z, nb + 2, blk, h, dh)
        return jnp.concatenate([tp[:, :-2], tp[:, 1:-1], tp[:, 2:]], axis=2)

    kw, vw = band(kg), band(vg)
    qpos = jnp.arange(nb)[:, None] * blk + jnp.arange(blk)[None, :]
    kpos = (jnp.arange(nb)[:, None] - 1) * blk + jnp.arange(3 * blk)[None, :]
    valid = ((jnp.abs(qpos[:, :, None] - kpos[:, None, :]) <= half)
             & (kpos[:, None, :] >= 0) & (kpos[:, None, :] < L))
    sc = jnp.einsum('znqhd,znkhd->znhqk', qb, kw).astype(jnp.float32) * (dh ** -0.5)
    sc = jnp.where(valid[None, :, None], sc, NEG_INF)
    m = jnp.max(sc, axis=-1, keepdims=True)
    p = jnp.exp(sc - m)
    l = jnp.sum(p, axis=-1, keepdims=True)
    o = jnp.einsum('znhqk,znkhd->znqhd', (p / l).astype(v.dtype), vw)
    lse = (m + jnp.log(l))[..., 0]
    o = o.reshape(b, dilation, lp, h, dh)[:, :, :L].transpose(0, 2, 1, 3, 4).reshape(b, s, h, dh)
    lse = lse.transpose(0, 1, 3, 2).reshape(b, dilation, lp, h)[:, :, :L]
    lse = lse.transpose(0, 2, 1, 3).reshape(b, s, h)
    return o, lse

def second_inputs(seed: int = 0) -> dict:
    key = jax.random.key(seed)
    ks = jax.random.split(key, 16)
    nrm = jax.random.normal
    f32 = jnp.float32
    return {
        'x': nrm(ks[0], (BATCH, SEQ, D_MODEL), f32),
        'mem': nrm(ks[1], (BATCH, N_MEM, D_MODEL), f32),
        'g_pre': 1.0 + 0.05 * nrm(ks[2], (DEPTH_2, D_MODEL), f32),
        'w_in': nrm(ks[3], (DEPTH_2, D_MODEL, IN_WIDTH), f32) * D_MODEL ** -0.5,
        'b_merge': 0.1 * nrm(ks[4], (DEPTH_2, N_BRANCHES * D_MODEL), f32),
        'q_norm': 1.0 + 0.05 * nrm(ks[5], (DEPTH_2, HEAD_DIM), f32),
        'k_norm': 1.0 + 0.05 * nrm(ks[6], (DEPTH_2, HEAD_DIM), f32),
        'g_mem': 1.0 + 0.05 * nrm(ks[7], (DEPTH_2, D_MODEL), f32),
        'w_mem_kv': nrm(ks[8], (DEPTH_2, D_MODEL, 2 * M_Q), f32) * D_MODEL ** -0.5,
        'w_br_a': nrm(ks[9], (DEPTH_2, BRANCH_WIDTH, D_MODEL), f32) * BRANCH_WIDTH ** -0.5,
        'w_br_b': nrm(ks[10], (DEPTH_2, BRANCH_WIDTH, D_MODEL), f32) * BRANCH_WIDTH ** -0.5,
        'w_br_m': nrm(ks[11], (DEPTH_2, BRANCH_WIDTH, D_MODEL), f32) * BRANCH_WIDTH ** -0.5,
        'w_out': nrm(ks[12], (DEPTH_2, D_MODEL, D_MODEL), f32) * D_MODEL ** -0.5,
        'g_post': 1.0 + 0.05 * nrm(ks[13], (DEPTH_2, D_MODEL), f32),
    }

def second_block(x, mem, g_pre, w_in, b_merge, q_norm, k_norm, g_mem, w_mem_kv, w_br_a, w_br_b, w_br_m, w_out, g_post):
    b, s, d = x.shape
    dt = x.dtype
    pos = jnp.arange(s, dtype=jnp.float32)
    rows = s // GRID_W
    row_pos = jnp.repeat(jnp.arange(rows, dtype=jnp.float32), GRID_W)
    col_pos = (jnp.arange(s) % GRID_W).astype(jnp.float32)
    split_at = np.cumsum(SPLIT_SIZES)[:-1].tolist()
    n_groups = len(A_GROUPS)
    kv_rep = B_HEADS // B_KV_HEADS
    n_q_blocks = s // Q_BLOCK

    for layer in range(DEPTH_2):
        h = rms_norm_2(x, g_pre[layer])
        a_qkv, bq, bk, bv, mq, ga, gb, gm, mg = jnp.split(h @ w_in[layer], split_at, axis=-1)

        a_qkv = a_qkv.reshape(b, s, 3, n_groups * A_HEADS, HEAD_DIM)
        aq = rope(a_qkv[:, :, 0], pos)
        ak = rope(a_qkv[:, :, 1], pos)
        av = a_qkv[:, :, 2]
        outs, lses = [], []
        for gi, (window, dil) in enumerate(A_GROUPS):
            hs = slice(gi * A_HEADS, (gi + 1) * A_HEADS)
            o_g, lse_g = dilated_window_attention(aq[:, :, hs], ak[:, :, hs], av[:, :, hs], window, dil)
            outs.append(o_g)
            lses.append(lse_g)
        wts = jax.nn.softmax(jnp.stack(lses, axis=0), axis=0).astype(dt)
        oa = jnp.einsum('gbsh,gbshd->bshd', wts, jnp.stack(outs, axis=0)).reshape(b, s, BRANCH_WIDTH)

        qb_ = axial_rope(rms_norm_2(bq.reshape(b, s, B_HEADS, HEAD_DIM), q_norm[layer]), row_pos, col_pos)
        kb_ = axial_rope(rms_norm_2(bk.reshape(b, s, B_KV_HEADS, HEAD_DIM), k_norm[layer]), row_pos, col_pos)
        vb_ = bv.reshape(b, s, B_KV_HEADS, HEAD_DIM)
        q_blocks = qb_.reshape(b, n_q_blocks, Q_BLOCK, B_KV_HEADS, kv_rep, HEAD_DIM).transpose(1, 0, 2, 3, 4, 5)

        def attend(qc, kb_=kb_, vb_=vb_):
            sc = jnp.einsum('bqkgd,bskd->bkgqs', qc, kb_).astype(jnp.float32) * (HEAD_DIM ** -0.5)
            p = jax.nn.softmax(sc, axis=-1).astype(vb_.dtype)
            return jnp.einsum('bkgqs,bskd->bqkgd', p, vb_)

        ob = lax.map(attend, q_blocks).transpose(1, 0, 2, 3, 4, 5).reshape(b, s, B_Q)

        kvm = rms_norm_2(mem, g_mem[layer]) @ w_mem_kv[layer]
        n_mem = mem.shape[1]
        km = kvm[..., :M_Q].reshape(b, n_mem, M_HEADS, M_HEAD_DIM)
        vm = kvm[..., M_Q:].reshape(b, n_mem, M_HEADS, M_HEAD_DIM)
        sm = jnp.einsum('bshd,bnhd->bhsn', mq.reshape(b, s, M_HEADS, M_HEAD_DIM), km).astype(jnp.float32)
        pm = jax.nn.softmax(sm * (M_HEAD_DIM ** -0.5), axis=-1).astype(dt)
        om = jnp.einsum('bhsn,bnhd->bshd', pm, vm).reshape(b, s, M_Q)

        ya = (oa * jax.nn.silu(ga)) @ w_br_a[layer]
        yb = (ob * jax.nn.silu(gb)) @ w_br_b[layer]
        ym = (om * jax.nn.silu(gm)) @ w_br_m[layer]
        gates = jax.nn.sigmoid((mg + b_merge[layer]).astype(jnp.float32)).astype(dt).reshape(b, s, N_BRANCHES, d)
        merged = gates[:, :, 0] * ya + gates[:, :, 1] * yb + gates[:, :, 2] * ym
        out = merged @ w_out[layer]
        x = x + rms_norm_2(out, g_post[layer])
    return x


def setup_inputs(seed=0):
    out = dict(first_inputs(seed))
    for name, value in second_inputs(seed + 1).items():
        if name != "x":
            out[name + "_2"] = value
    return out


def reference(
    x, attn_norm_g, w_in, ssm_a_re, ssm_a_im, ssm_log_dt, ssm_b_re, ssm_b_im, ssm_c_re,
    ssm_c_im, ssm_d, ssm_w_glu, ssm_b_glu, gmlp_v_g, gmlp_w_s, gmlp_b_s, q_norm_g, k_norm_g,
    lambda_q1, lambda_k1, lambda_q2, lambda_k2, subln_g, w_out, ffn_norm_g, w_up, conv_w,
    conv_b, w_down, mem_2, g_pre_2, w_in_2, b_merge_2, q_norm_2, k_norm_2, g_mem_2, w_mem_kv_2,
    w_br_a_2, w_br_b_2, w_br_m_2, w_out_2, g_post_2,
):
    x = first_block(
        x, attn_norm_g, w_in, ssm_a_re, ssm_a_im, ssm_log_dt, ssm_b_re, ssm_b_im, ssm_c_re,
        ssm_c_im, ssm_d, ssm_w_glu, ssm_b_glu, gmlp_v_g, gmlp_w_s, gmlp_b_s, q_norm_g, k_norm_g,
        lambda_q1, lambda_k1, lambda_q2, lambda_k2, subln_g, w_out, ffn_norm_g, w_up, conv_w,
        conv_b, w_down,
    )
    return second_block(
        x, mem_2, g_pre_2, w_in_2, b_merge_2, q_norm_2, k_norm_2, g_mem_2, w_mem_kv_2, w_br_a_2,
        w_br_b_2, w_br_m_2, w_out_2, g_post_2,
    )


_drawn_inputs = setup_inputs


def setup_inputs(seed=0):
    import zlib

    import numpy as np

    out = dict(_drawn_inputs(seed))
    spreads = {}
    factors = {'ssm_a_re': 64.0,
     'ssm_a_im': 22.256,
     'ssm_log_dt': 25.032,
     'ssm_b_re': 30.064,
     'ssm_b_im': 31.32,
     'ssm_c_re': 30.632,
     'ssm_c_im': 32.224,
     'ssm_b_glu': 46.296,
     'gmlp_v_g': 5.421,
     'gmlp_b_s': 4.666,
     'q_norm_g': 4.05,
     'k_norm_g': 4.53,
     'lambda_k1': 8.0,
     'subln_g': 3.681,
     'ffn_norm_g': 2.832,
     'b_merge_2': 14.395,
     'q_norm_2': 40.289,
     'k_norm_2': 58.074,
     'g_mem_2': 22.798,
     'conv_b': 2.998,
     'g_pre_2': 3.488,
     'w_br_a_2': 8.0,
     'g_post_2': 8.0}
    for name, (base, spread) in spreads.items():
        noise = np.random.default_rng([zlib.crc32(name.encode()), seed]).standard_normal(out[name].shape)
        drawn = base * np.exp(spread * noise) if base else spread * noise
        out[name] = __import__('jax').numpy.asarray(drawn.astype(out[name].dtype))
    for name, factor in factors.items():
        out[name] = (out[name] * factor).astype(out[name].dtype)
    return out
```

```python
from contextlib import ExitStack
import math

import numpy as np
import concourse.bass as bass
from concourse import mybir

P = 128
TOK, TT = 256, 2
D, KD = 1024, 8
LAYERS = 2
GROUPS, GCH, STATE = 16, 16, 64
ST = GROUPS * STATE // P
QKD, VD, DH = 64, 128, 4
FF = 2816
FT = FF // P
UNITS = FT // 2
HD, AH, NG, BH, MH, MD = 64, 8, 3, 8, 4, 128
EPS = 1e-6
NEG = -1e30
BIG = -3.0e38
RAW, RING = 5, 4

F32, F32R = mybir.dt.float32, mybir.dt.float32r
ALU, ACT, AX = mybir.AluOpType, mybir.ActivationFunctionType, mybir.AxisListType
LAMBDA_INIT = [0.8 - 0.6 * math.exp(-0.3 * l) for l in range(LAYERS)]

CHUNKS = [("km", 8, 512), ("vm", 8, 512)]
for _l in range(LAYERS):
    CHUNKS += [(f"ssm_u{_l}", 8, 256), (f"q{_l}", 8, 512), (f"k{_l}", 8, 512), (f"v{_l}", 8, 512),
               (f"gmlp{_l}", 8, 512), (f"out{_l}_0", 8, 512), (f"out{_l}_1", 8, 512)]
    CHUNKS += [(f"up{_l}_{j}", 8, 512) for j in range(UNITS)]
    CHUNKS += [(f"down{_l}_0", FT, 512), (f"down{_l}_1", FT, 512)]
CHUNKS += [("mq", 8, 512), ("bq", 8, 512), ("bkv", 8, 256), ("gb", 8, 512), ("gm", 8, 512)]
CHUNKS += [(f"a{w}{g}", 8, 512) for w in "qkv" for g in range(NG)] + [("ga", 8, 512)]
CHUNKS += [(f"mg{i}", 8, 512) for i in range(6)]
CHUNKS += [(f"br{b}{n}", 4, 512) for n in range(2) for b in "abm"] + [("wo0", 8, 512), ("wo1", 8, 512)]
NAMES = [c[0] for c in CHUNKS]
PAIRS = [k * n // 1024 for _, k, n in CHUNKS]
FIRST = [sum(PAIRS[:i]) for i in range(len(CHUNKS))]
NPAIRS = sum(PAIRS)


def chunk(name):
    return NAMES.index(name)


def end_pair(name):
    c = chunk(name)
    return FIRST[c] + PAIRS[c]


BRANCH_ORDER = [b + str(n) for n in range(2) for b in "abm"]
A_CHUNKS = [f"a{w}{g}" for w in "qkv" for g in range(NG)] + ["ga"]
SILU_ORDER = ["gb", "gm", "ga"]
EMPTIED = {"km": [("mem_ev", 2)], "vm": [("mem_ev", 4)], "mq": [("mq_ev", 2)], "bq": [("bqn_ready", 2)],
           "bkv": [("bkn_ready", 2), ("bv_ready", 2)]}
for _l in range(LAYERS):
    EMPTIED[f"ssm_u{_l}"] = [("u_ready", _l + 1)]
    EMPTIED[f"q{_l}"] = [("qn_ready", 4 * _l + 2)]
    EMPTIED[f"k{_l}"] = [("qn_ready", 4 * _l + 4)]
    EMPTIED[f"v{_l}"] = [("v_ready", 2 * _l + 2)]
    EMPTIED[f"gmlp{_l}"] = [("vn_ready", 2 * _l + 2), ("ug_ready", 2 * _l + 2)]
    for _n in range(2):
        EMPTIED[f"out{_l}_{_n}"] = [("resid", 8 * _l + 2 * _n + 2)]
        EMPTIED[f"down{_l}_{_n}"] = [("resid", 8 * _l + 4 + 2 * _n + 2)]
        EMPTIED[f"wo{_n}"] = [("wo_ev", 2 * _n + 2)]
    for _j in range(UNITS):
        EMPTIED[f"up{_l}_{_j}"] = [("conv_d", 4 * (UNITS * _l + _j + 1))]
for _n in range(6):
    EMPTIED[A_CHUNKS[_n]] = [("rot_terms", 4 * _n + 4)]
    EMPTIED[f"mg{_n}"] = [("gate_sum", 2 * _n + 2)]
    EMPTIED["br" + BRANCH_ORDER[_n]] = [("y_gated", 2 * _n + 2)]
for _n in range(NG):
    EMPTIED[f"av{_n}"] = [("av_ready", 2 * _n + 2)]
    EMPTIED[SILU_ORDER[_n]] = [("silu_ready", 2 * _n + 2)]
BUF = []
for _n in NAMES:
    BUF.append(0 if _n.startswith("mg") else 1 - BUF[-1] if BUF else 0)


def buf(name):
    return BUF[chunk(name)]


def spans(*items):
    at, out = 0, {}
    for name, n in items:
        out[name] = (at, at + n)
        at += n
    return out, at


COL, NCOL = spans(("are", 16), ("aim", 16), ("ldt", 16), ("gattn", 16), ("gffn", 16), ("dskip", 4),
                  ("bglu", 4), ("bs", 8), ("gpre", 8), ("gmem", 8), ("conv", LAYERS * 2 * FT * 4))
ROW, NROW = spans(("vg", 512), ("qg", 128), ("kg", 128), ("sub", 256), ("qn2", 64), ("kn2", 64))
LAM, NLAM = spans(("lq1", 128), ("lk1", 128), ("lq2", 128), ("lk2", 128))
CST, NCST = spans(("ident", 128), ("cos", 128), ("sin", 128), ("acos", 128), ("asin", 128),
                  ("mdiff", 384))


def build(nc, weights, x, mem, cols, rows, lams, bmerge, consts, amask, bexp, cexp, wst, wglu, out, upto=99):
    with ExitStack() as ctx:
        def sbt(stack, name, shape, dt=F32):
            return stack.enter_context(nc.sbuf_tensor(name, shape, dt))

        sems = {}

        def sem(name):
            if name not in sems:
                sems[name] = ctx.enter_context(nc.semaphore(name))
            return sems[name]

        raw = sbt(ctx, "raw", [P, RAW, 1024])
        whi = sbt(ctx, "whi", [P, RING, 1024], F32R)
        wlo = sbt(ctx, "wlo", [P, RING, 1024], F32R)
        xres = sbt(ctx, "xres", [P, TT, D])
        xn = sbt(ctx, "xn", [P, TT, D])
        xth = sbt(ctx, "xth", [P, KD, TOK], F32R)
        xtl = sbt(ctx, "xtl", [P, KD, TOK], F32R)
        kmT = sbt(ctx, "kmT", [P, MH, TOK])
        vm = sbt(ctx, "vm", [P, TT, 512])
        colv = sbt(ctx, "colv", [P, NCOL])
        rowv = sbt(ctx, "rowv", [P, NROW])
        cst = sbt(ctx, "cst", [P, NCST])
        ssq = sbt(ctx, "ssq", [P, 8, 4])
        ssm1 = sbt(ctx, "ssm1", [P, 8, 2])
        rstd = sbt(ctx, "rstd", [P, 8, 2])
        mhalf = sbt(ctx, "mhalf", [P, 16])
        sp_ = sbt(ctx, "sp_", [P, 24, 16])
        sqs = sbt(ctx, "sqs", [P, 512], mybir.dt.bfloat16)
        gss = sbt(ctx, "gss", [P, LAYERS, TT])
        gr = sbt(ctx, "gr", [P, LAYERS, TT])
        hss = sbt(ctx, "hss", [P, 16])
        hr = sbt(ctx, "hr", [P, 2, 16])
        sqs2 = sbt(ctx, "sqs2", [P, 64])
        hb = sbt(ctx, "hb", [P, 4])
        nlam = sbt(ctx, "nlam", [P, LAYERS])
        lamv = sbt(ctx, "lamv", [P, 8])
        ropeq = sbt(ctx, "ropeq", [P, LAYERS, 4, TT, QKD])

        def col(name, i=0, n=None):
            a, b = COL[name]
            return colv[:, a + i:(a + i + n) if n else b]

        def row(name, i=0, n=None):
            a, b = ROW[name]
            return rowv[:, a + i:(a + i + n) if n else b]

        def cs(name):
            a, b = CST[name]
            return cst[:, a:b]

        ident = cs("ident")

        def wide(ap, n, dim=1):
            a = ap.unsqueeze(dim)
            shape = list(a.shape)
            shape[dim] = n
            return a.to_broadcast(shape)

        one = ExitStack()
        ctx.enter_context(one)
        bex = sbt(one, "bex", [P, 2, ST, P])
        cex = sbt(one, "cex", [P, 2, ST, P])
        tab = sbt(one, "tab", [P, 2, ST, TOK])
        wglus = sbt(one, "wglus", [P, 2, 256])
        wsts = sbt(one, "wsts", [P, 4, P])
        pw = sbt(one, "pw", [P, 5, ST])
        pq = sbt(one, "pq", [P, 2, ST, 32])
        ft = sbt(one, "ft", [P, 4, P])
        mix = ExitStack()
        one.enter_context(mix)
        bu = sbt(mix, "bu", [P, ST, 2, TOK])
        mp = sbt(mix, "mp", [P, 2, 2, TOK])
        md = sbt(mix, "md", [P, 3, 2, TOK])
        uT = sbt(mix, "uT", [P, 2, TOK])
        qT = sbt(mix, "qT", [P, DH, TOK])
        kT = sbt(mix, "kT", [P, DH, TOK])
        v_sb = sbt(mix, "v_sb", [P, TT, 512])
        qn = sbt(mix, "qn", [P, TT, 512])
        hsq = sbt(mix, "hsq", [P, TT, 512])
        ug = sbt(mix, "ug", [P, TT, 256])
        sm = sbt(mix, "sm", [P, 2, 2, TOK])
        pT = sbt(mix, "pT", [P, 2, TT, P])
        st_ = sbt(mix, "st_", [P, 8, 8])
        mix.close()
        ffs = ExitStack()
        one.enter_context(ffs)
        hth = sbt(ffs, "hth", [P, FT, TOK], F32R)
        htl = sbt(ffs, "htl", [P, FT, TOK], F32R)
        acc = sbt(ffs, "acc", [P, 2, 4, TOK])
        gtd = sbt(ffs, "gtd", [P, 2, 2, TOK])
        ffs.close()
        one.close()

        two = ExitStack()
        ctx.enter_context(two)
        sm2 = sbt(two, "sm2", [P, 2, NG * TOK])
        pT2 = sbt(two, "pT2", [P, 2, 2 * NG, P])
        rt = sbt(two, "rt", [P, TT, 512])
        gat = sbt(two, "gat", [P, 3, TT, 512])
        ma = sbt(two, "ma", [P, 4 * TOK])
        brow = sbt(two, "brow", [P, 2, 512])
        sx = sbt(two, "sx", [P, 4, 8])
        tabq = sbt(two, "tabq", [P, 4, TT, HD])
        bm = ExitStack()
        two.enter_context(bm)
        bqT = sbt(bm, "bqT", [P, 4, TOK])
        bkT = sbt(bm, "bkT", [P, 2, TOK])
        bv = sbt(bm, "bv", [P, TT, P])
        mqT = sbt(bm, "mqT", [P, MH, TOK])
        bm.close()
        gt = sbt(two, "gt", [P, TT, 3 * D])
        att = ExitStack()
        two.enter_context(att)
        aqT = sbt(att, "aqT", [P, 2, NG, 4, TOK])
        va = sbt(att, "va", [P, NG, TT, 512])
        att.close()
        oth = sbt(two, "oth", [P, 12, TOK], F32R)
        otl = sbt(two, "otl", [P, 12, TOK], F32R)
        merged = sbt(two, "merged", [P, TT, D])
        gpost = sbt(two, "gpost", [P, D])
        two.close()

        PJ = [ctx.enter_context(nc.psum_tensor(f"PJ{i}", [P, TT, 512], F32)) for i in range(2)]
        S0, S1, T0, T1 = (ctx.enter_context(nc.psum_tensor(n, [P, 512], F32)) for n in ("S0", "S1", "T0", "T1"))
        AUX = [S0, S1, T0, T1]

        raw_landed = [sem(f"raw_landed{i}") for i in range(RAW)]
        hi_ready, lo_ready, pair_used = sem("hi_ready"), sem("lo_ready"), sem("pair_used")
        block = ctx.enter_context(nc.Block())

        NORM_GAIN = [("gmem", 0), ("gattn", 0), ("gffn", 0), ("gattn", 8), ("gffn", 8), ("gpre", 0)]

        def md_vn(h):
            return xn[:, :, 768 + h * 64:768 + (h + 1) * 64]

        def md_g(k):
            return md[:, 0, k, :]

        def merge_tanh(act, i):
            act.wait_ge(sem("gate_sum"), 2 * i + 2)
            act.activation(gt[:, :, 512 * i:512 * i + 512], gt[:, :, 512 * i:512 * i + 512], ACT.Tanh,
                           scale=0.5).then_inc(sem("gate_ready"), 1)

        def gate_sum(dve, i):
            nm = f"mg{i}"
            dve.wait_ge(pair_used, end_pair(nm))
            dve.wait_ge(sem(f"brow_landed{i % 2}"), 16 * (i // 2 + 1))
            for t in range(TT):
                dve.tensor_tensor(gt[:, t, 512 * i:512 * i + 512], PJ[buf(nm)][:, t, :], brow[:, i % 2, :],
                                  ALU.add).then_inc(sem("gate_sum"), 1)

        @block.sync
        def _(sp):
            def small(dst, src, s):
                sp.dma_start(dst, src).then_inc(sem(s), 16)

            small(xn[:], mem.rearrange("(t p) d -> p t d", p=P), "mem_landed")
            small(cst[:], consts, "cst_landed")
            small(colv[:], cols, "col_landed")
            small(xres[:], x.rearrange("(t p) d -> p t d", p=P), "x_landed")
            for p in range(NPAIRS):
                if p >= RAW:
                    sp.wait_ge(lo_ready, p - RAW + 1)
                sp.dma_start(raw[:, p % RAW, :], weights[p]).then_inc(raw_landed[p % RAW], 16)
                if p == 3:
                    small(rowv[:], rows.to_broadcast([P, NROW]), "row_landed")
                    small(bu[:, 0, :, :].rearrange("p c t -> p (c t)"), lams.to_broadcast([P, NLAM]), "lam_landed")
                    small(bex[:], bexp[0], "bex_landed")
                    small(cex[:], cexp[0], "cex_landed")
                    small(wsts[:], wst[0], "wst_landed")
                    small(wglus[:], wglu[0], "wglu_landed")
                if p == FIRST[chunk("up0_0")] + 6:
                    for s in ("y_done", "glu_done", "sgu_done"):
                        sp.wait_ge(sem(s), 1)
                    small(bex[:], bexp[1], "bex_landed")
                    small(cex[:], cexp[1], "cex_landed")
                    small(wsts[:], wst[1], "wst_landed")
                    small(wglus[:], wglu[1], "wglu_landed")
                if p == FIRST[chunk("gb")]:
                    sp.wait_ge(pair_used, end_pair("down1_1"))
                    small(ma[:], amask, "ma_landed")
                for i in range(6):
                    if p == FIRST[chunk(f"mg{i}")]:
                        if i >= 2:
                            sp.wait_ge(sem("gate_sum"), 2 * i - 2)
                        small(brow[:, i % 2, :], bmerge[:, 512 * i:512 * i + 512].to_broadcast([P, 512]), f"brow_landed{i % 2}")
                if p + 1 == NPAIRS or (upto == 1 and p + 1 == FIRST[chunk("mq")]):
                    break
            if upto == 1:
                sp.wait_ge(sem("resid"), 4 * 2 * LAYERS)
                sp.dma_start(out.rearrange("(t p) d -> p t d", p=P), xres[:]).then_inc(sem("out_stored"), 16)
                sp.wait_ge(sem("out_stored"), 16)
                return
            sp.wait_ge(sem("apv_done"), 16)
            small(gpost[:], bmerge[:, 3 * D:4 * D].to_broadcast([P, D]), "gpost_landed")
            for t in range(TT):
                sp.wait_ge(sem("y_ready"), t + 1)
                sp.dma_start(out[t * P:(t + 1) * P, :], xn[:, t, :]).then_inc(sem("out_stored"), 16)
            sp.wait_ge(sem("out_stored"), 32)

        BM = [("b", h, t) for h in range(BH) for t in range(TT)] + [("m", h, t) for h in range(MH) for t in range(TT)]
        F2, F3 = FIRST[chunk("aq0")], FIRST[chunk("mg0")]

        def bm_slots(n):
            return [k for k in range(len(BM) + 2) if 1 + 3 * k // 2 == n]

        def a_slots(n):
            return [k for k in range(AH * TT + 2) if 4 * k // 3 == n]

        @block.tensor
        def _(pe):
            def pair_products(p, kt0, banks, fm, xh, xl, cw, last_k):
                r = p % RING
                n_k = 1024 // cw
                pe.wait_ge(hi_ready, p + 1)
                pe.wait_ge(lo_ready, p + 1)
                for kk in range(n_k):
                    k = kt0 + kk
                    wh, wl = whi[:, r, kk * cw:(kk + 1) * cw], wlo[:, r, kk * cw:(kk + 1) * cw]
                    if fm:
                        for f in range(cw // P):
                            o = banks[f // 2][:, (f % 2) * TOK:(f % 2 + 1) * TOK]
                            a, b = wh[:, f * P:(f + 1) * P], wl[:, f * P:(f + 1) * P]
                            pe.matmul(o, a, xh[:, k, :], start=(k == 0 and f % 2 == 0), stop=False, skip_group_check=True)
                            pe.matmul(o, a, xl[:, k, :], start=False, stop=False, skip_group_check=True)
                            m = pe.matmul(o, b, xh[:, k, :], start=False, stop=(k == last_k), skip_group_check=True)
                    else:
                        for t in range(TT):
                            o = banks[t][:, 0:cw]
                            h, lw = xh[:, k, t * P:(t + 1) * P], xl[:, k, t * P:(t + 1) * P]
                            pe.matmul(o, h, wh, start=(k == 0), stop=False, skip_group_check=True)
                            pe.matmul(o, h, wl, start=False, stop=False, skip_group_check=True)
                            m = pe.matmul(o, lw, wh, start=False, stop=(k == last_k), skip_group_check=True)
                return m

            def project(name, fm=False, xh=xth, xl=xtl, ready=None, pairs=None):
                c = chunk(name)
                _, n_k, cw = CHUNKS[c]
                banks = [PJ[BUF[c]][:, 0, :], PJ[BUF[c]][:, 1, :]]
                before = [i for i in range(c) if BUF[i] == BUF[c]]
                per = 1024 // cw
                for j in (range(PAIRS[c]) if pairs is None else pairs):
                    if j == 0 and before:
                        for s, n in EMPTIED[NAMES[before[-1]]]:
                            pe.wait_ge(sem(s), n)
                    if ready:
                        pe.wait_ge(ready[0], ready[1] + (j + 1) * ready[2])
                    m = pair_products(FIRST[c] + j, j * per, banks, fm, xh, xl, cw, n_k - 1)
                    m.then_inc(pair_used, 1)

            def norm_transposes(n):
                if n == 0:
                    pe.wait_ge(sem("cst_landed"), 16)
                if n >= 1:
                    pe.wait_ge(sem("xt_lo"), 8 * n)
                if n >= 2:
                    aux_free_before_norm(n)
                for t in range(TT):
                    pe.wait_ge(sem("xn_ready"), 2 * n + t + 1)
                    for f in range(KD):
                        o = AUX[f // 2][:, (f % 2) * TOK + t * P:(f % 2) * TOK + (t + 1) * P]
                        m = pe.transpose(o, xn[:, t, f * P:(f + 1) * P], ident)
                        if t == 1 and f % 2 == 1:
                            m.then_inc(sem("xt_tr"), 1)

            def aux_free_before_norm(n):
                if n in (2, 4):
                    l = n // 2 - 1
                    pe.wait_ge(sem("mix_lo"), 4 * (l + 1))

            norm_transposes(0)
            project("km", fm=True, ready=(sem("xt_lo"), 0, 2))
            project("vm")
            norm_transposes(1)

            for l in range(LAYERS):
                if l > 0:
                    norm_transposes(1 + 2 * l)
                xt = (sem("xt_lo"), 8 * (1 + 2 * l), 4)
                project(f"ssm_u{l}", fm=True, ready=xt)
                pe.wait_ge(sem("bex_landed"), 16 * (l + 1))
                pe.wait_ge(sem("u_ready"), l + 1)
                pe.wait_ge(sem("xt_lo"), 8 * (2 + 2 * l))
                for s in range(ST):
                    if s >= 4:
                        pe.wait_ge(sem("bu_ready"), ST * l + s - 3)
                    for c in range(2):
                        m = pe.matmul(AUX[s % 4][:, c * TOK:(c + 1) * TOK], bex[:, c, s, :], uT[:, s // 4, :],
                                      start=(c == 0), stop=True, skip_group_check=True)
                    m.then_inc(sem("bu_done"), 1)
                project(f"q{l}")
                project(f"k{l}")

                def head_transposes(which, banks, n):
                    pe.wait_ge(sem("bu_ready"), ST * (l + 1))
                    pe.wait_ge(sem("rope_ready"), 4 * (2 * l + which + 1))
                    for h in range(DH):
                        for t in range(TT):
                            o = banks[h // 2][:, (h % 2) * TOK + t * P:(h % 2) * TOK + (t + 1) * P]
                            m = pe.transpose(o, xn[:, t, which * 512 + h * P:which * 512 + (h + 1) * P], ident)
                    m.then_inc(sem("qk_tr"), 1)

                head_transposes(0, (S0, S1), 0)
                project(f"v{l}")
                head_transposes(1, (T0, T1), 1)
                project(f"gmlp{l}")

                def scores(s):
                    h, t = divmod(s, TT)
                    n = P * (t + 1)
                    for c, bank in ((0, S0), (1, S1)):
                        m = pe.matmul(bank[:, 0:n], qT[c * QKD:(c + 1) * QKD, h, t * P:(t + 1) * P],
                                      kT[c * QKD:(c + 1) * QKD, h, 0:n], start=True, stop=True, skip_group_check=True)
                    m.then_inc(sem("sc_done"), 1)

                def prob_transposes(s):
                    t = s % TT
                    i = 8 * l + s
                    pe.wait_ge(sem("w_ready"), i + 1)
                    if i >= 2:
                        pe.wait_ge(sem("pt_ev"), i - 1)
                    for k in range(t + 1):
                        m = pe.transpose((T0, T1)[s % 2][:, k * P:(k + 1) * P],
                                         sm[:, s % 2, 1, k * P:(k + 1) * P], ident)
                    m.then_inc(sem("pt_tr"), 1)

                def values(s):
                    h, t = divmod(s, TT)
                    i = 8 * l + s
                    pe.wait_ge(sem("pt_ev"), i + 1)
                    if i >= 2:
                        pe.wait_ge(sem("o_ev"), i - 1)
                    for k in range(t + 1):
                        m = pe.matmul(PJ[buf(f"v{l}")][:, s % 2, 0:P], pT[:, s % 2, k, :],
                                      v_sb[:, k, h * VD:(h + 1) * VD], start=(k == 0), stop=(k == t), skip_group_check=True)
                    m.then_inc(sem("pv_done"), 1)

                pe.wait_ge(sem("qk_ev"), 4 * (l + 1))
                pe.wait_ge(sem("v_ready"), 2 * (l + 1))
                for s in range(8 + 2):
                    if s < 8:
                        if s > 0:
                            pe.wait_ge(sem("sc_read"), 2 * (8 * l + s))
                        scores(s)
                    if 1 <= s <= 8:
                        prob_transposes(s - 1)
                    if s >= 2:
                        values(s - 2)
                pe.wait_ge(sem("vn_ready"), 2 * (l + 1))
                pe.wait_ge(sem("wst_ready"), l + 1)
                pe.wait_ge(sem("pt_ev"), 8 * (l + 1))
                for h in range(4):
                    m = pe.matmul(T0[:, h * P:(h + 1) * P], wsts[:, h, :], md_vn(h), start=(h == 0), stop=True,
                                  skip_group_check=True)
                m.then_inc(sem("sgu_done"), 1)
                pe.wait_ge(sem("o_ev"), 8 * (l + 1))
                pe.wait_ge(sem("cex_ready"), 2 * ST * (l + 1))
                for ct in range(2):
                    for j in range(4):
                        s = 4 * ct + j
                        pe.wait_ge(sem("state_ready"), 2 * (ST * l + s + 1))
                        for c in range(2):
                            m = pe.matmul(T1[:, ct * TOK:(ct + 1) * TOK], cex[:, c, s, :], bu[:, s, c, :],
                                          start=(s == 0 and c == 0), stop=(j == 3 and c == 1), skip_group_check=True)
                m.then_inc(sem("y_done"), 1)
                pe.wait_ge(sem("sc_read"), 2 * 8 * (l + 1))
                pe.wait_ge(sem("sgu_ready"), 4 * (l + 1))
                for f in range(2):
                    for t in range(TT):
                        m = pe.transpose(S0[:, f * TOK + t * P:f * TOK + (t + 1) * P], xn[:, t, 512 + f * P:512 + (f + 1) * P], ident)
                m.then_inc(sem("mix_tr"), 1)
                pe.wait_ge(sem("diff_ready"), 2 * (l + 1))
                for f in range(4):
                    for t in range(TT):
                        bank = (S1, T0)[f // 2]
                        m = pe.transpose(bank[:, (f % 2) * TOK + t * P:(f % 2) * TOK + (t + 1) * P],
                                         xn[:, t, f * P:(f + 1) * P], ident)
                m.then_inc(sem("mix_tr"), 1)
                pe.wait_ge(sem("wglu_landed"), 16 * (l + 1))
                pe.wait_ge(sem("gelu_ready"), 2 * (l + 1))
                pe.wait_ge(sem("mix_lo"), 4 * l + 1)
                for f in range(2):
                    for k in range(2):
                        m = pe.matmul(S0[:, f * TOK:(f + 1) * TOK], wglus[:, k, f * P:(f + 1) * P], md_g(k),
                                      start=(f == 0 and k == 0), stop=(k == 1), skip_group_check=True)
                m.then_inc(sem("glu_done"), 1)
                pe.wait_ge(sem("mix_lo"), 4 * (l + 1))
                project(f"out{l}_0")
                project(f"out{l}_1")
                norm_transposes(2 + 2 * l)
                xt = (sem("xt_lo"), 8 * (2 + 2 * l), 2)
                for j in range(UNITS):
                    project(f"up{l}_{j}", fm=True, ready=xt)
                for i in range(2):
                    project(f"down{l}_{i}", xh=hth, xl=htl, ready=None if i else (sem("ht_lo"), UNITS * l, 1))
            if upto == 1:
                return

            norm_transposes(5)
            project("mq", fm=True, ready=(sem("xt_lo"), 40, 2))
            project("bq")
            project("bkv")
            project("gb")
            pe.wait_ge(sem("brope_ready"), 4)
            for f in range(4):
                for t in range(TT):
                    m = pe.transpose((T0, T1)[f // 2][:, (f % 2) * TOK + t * P:(f % 2) * TOK + (t + 1) * P],
                                     rt[:, t, f * P:(f + 1) * P], ident)
            m.then_inc(sem("b_tr"), 1)
            pe.wait_ge(sem("bkrope_ready"), 8)
            for f in range(2):
                for t in range(TT):
                    m = pe.transpose(S0[:, f * TOK + t * P:f * TOK + (t + 1) * P], xn[:, t, 256 + f * P:256 + (f + 1) * P], ident)
            m.then_inc(sem("b_tr"), 1)
            project("gm")

            def bm_scores(k):
                br, h, t = BM[k]
                if k:
                    pe.wait_ge(sem("bm_exp"), k)
                if br == "b":
                    a, b = (h % 2) * HD, (h % 2 + 1) * HD
                    m = pe.matmul(S0[:, 0:TOK], bqT[a:b, h // 2, t * P:(t + 1) * P], bkT[a:b, h // 4, :], start=True, stop=True)
                else:
                    m = pe.matmul(S0[:, 0:TOK], mqT[:, h, t * P:(t + 1) * P], kmT[:, h, :], start=True, stop=True)
                m.then_inc(sem("bm_sc"), 1)

            def bm_transposes(k):
                pe.wait_ge(sem("bm_exp"), k + 1)
                if k:
                    pe.wait_ge(sem("bm_pt"), k)
                for i in range(2):
                    m = pe.transpose(T0[:, i * P:(i + 1) * P], sm2[:, k % 2, i * P:(i + 1) * P], ident)
                m.then_inc(sem("bm_tr"), 1)

            def bm_values(k):
                br, h, t = BM[k]
                pe.wait_ge(sem("bm_pt"), k + 1)
                if k:
                    pe.wait_ge(sem("bm_out"), k)
                for i in range(2):
                    v = bv[:, i, (h // 4) * HD:(h // 4 + 1) * HD] if br == "b" else vm[:, i, h * MD:(h + 1) * MD]
                    m = pe.matmul(T1[:, 0:HD if br == "b" else MD], pT2[:, k % 2, i, :], v, start=(i == 0), stop=(i == 1))
                m.then_inc(sem("bm_pv"), 1)

            pe.wait_ge(sem("b_ev"), 3)
            pe.wait_ge(sem("bv_ready"), 2)
            pe.wait_ge(sem("mq_ev"), 2)
            for c, nm in enumerate(A_CHUNKS):
                for j in range(4):
                    project(nm, pairs=[j])
                    if 1 <= c <= 6 and j >= 2:
                        rnd = 2 * (c - 1) + j - 2
                        pe.wait_ge(sem("a_rope"), 4 * c)
                        if rnd:
                            pe.wait_ge(sem("a_ev"), rnd)
                        for i in range(2):
                            f = 2 * (j - 2) + i
                            for t in range(TT):
                                m = pe.transpose(S1[:, i * TOK + t * P:i * TOK + (t + 1) * P], rt[:, t, f * P:(f + 1) * P], ident)
                        m.then_inc(sem("a_tr"), 1)
                    for k in bm_slots(4 * c + j):
                        if k < len(BM):
                            bm_scores(k)
                        if 1 <= k <= len(BM):
                            bm_transposes(k - 1)
                        if k >= 2:
                            bm_values(k - 2)

            def a_scores(k):
                h, t = divmod(k, TT)
                a, b = (h % 2) * HD, (h % 2 + 1) * HD
                if k:
                    pe.wait_ge(sem("a_max"), 2 * k)
                for g in range(NG):
                    o = (S0, S0, S1)[g][:, (g % 2) * TOK:(g % 2 + 1) * TOK]
                    m = pe.matmul(o, aqT[a:b, 0, g, h // 2, t * P:(t + 1) * P], aqT[a:b, 1, g, h // 2, :],
                                  start=(g != 1), stop=True, skip_group_check=True)
                m.then_inc(sem("a_sc"), 1)

            def a_transposes(k):
                pe.wait_ge(sem("a_exp"), k + 1)
                if k:
                    pe.wait_ge(sem("a_pt"), 2 * k)
                for i in range(2 * NG):
                    m = pe.transpose((T0, T1)[i // 4][:, (i % 4) * P:(i % 4 + 1) * P], sm2[:, k % 2, i * P:(i + 1) * P], ident)
                m.then_inc(sem("a_ptr"), 1)

            def a_values(k):
                h, t = divmod(k, TT)
                pe.wait_ge(sem("a_pt"), 2 * k + 2)
                if k:
                    pe.wait_ge(sem("a_out"), k)
                for i in range(2 * NG):
                    m = pe.matmul(PJ[1][:, 0, 0:HD], pT2[:, k % 2, i, :], va[:, i // 2, i % 2, h * HD:(h + 1) * HD],
                                  start=(i == 0), stop=(i == 2 * NG - 1))
                m.then_inc(sem("apv_done"), 1)

            for n in range(24):
                project(f"mg{n // 4}", pairs=[n % 4])
                for k in a_slots(n):
                    if k == 0:
                        pe.wait_ge(sem("a_ev"), 12)
                        pe.wait_ge(sem("av_ready"), 6)
                        pe.wait_ge(sem("bm_out"), len(BM))
                        for s, v in EMPTIED["ga"]:
                            pe.wait_ge(sem(s), v)
                    if k < AH * TT:
                        a_scores(k)
                    if 1 <= k <= AH * TT:
                        a_transposes(k - 1)
                    if k >= 2:
                        a_values(k - 2)
            for b in range(3):
                if b == 2:
                    pe.wait_ge(sem("a_out"), AH * TT)
                for f in range(0, 4, 2):
                    i = 2 * b + f // 2
                    pe.wait_ge(sem("a_pt"), 2 * AH * TT)
                    if i >= 4:
                        pe.wait_ge(sem("o_lo"), i - 3)
                    for q in range(2):
                        for t in range(TT):
                            m = pe.transpose(AUX[i % 4][:, q * TOK + t * P:q * TOK + (t + 1) * P],
                                             gat[:, b, t, (f + q) * P:(f + q + 1) * P], ident)
                    m.then_inc(sem("o_tr"), 1)
            for nm in BRANCH_ORDER:
                b = "bma".index(nm[0])
                project("br" + nm, xh=oth[:, 4 * b:4 * b + 4, :], xl=otl[:, 4 * b:4 * b + 4, :],
                        ready=(sem("o_lo"), 2 * b, 1))
            for f in range(KD):
                if f % 2 == 0:
                    pe.wait_ge(sem("o_lo"), 6)
                pe.wait_ge(sem("merged_ready"), 2 if f < 4 else 4)
                for t in range(TT):
                    m = pe.transpose(AUX[f // 2][:, (f % 2) * TOK + t * P:(f % 2) * TOK + (t + 1) * P],
                                     merged[:, t, f * P:(f + 1) * P], ident)
                if f % 2:
                    m.then_inc(sem("m_tr"), 1)
            project("wo0", ready=(sem("m_lo"), 0, 1))
            project("wo1")

        @block.scalar
        def _(act):
            at = [0]

            def hi_upto(n):
                while at[0] < min(n, stop_pair):
                    p = at[0]
                    act.wait_ge(raw_landed[p % RAW], 16 * (p // RAW + 1))
                    if p >= RING:
                        act.wait_ge(pair_used, p - RING + 1)
                    act.activation(whi[:, p % RING, :], raw[:, p % RAW, :], ACT.Copy).then_inc(hi_ready, 1)
                    at[0] += 1

            stop_pair = FIRST[chunk("mq")] if upto == 1 else NPAIRS
            n_sq = [0]

            def squares(n, src, t, half):
                if n_sq[0]:
                    act.wait_ge(sem("ssq_ready"), n_sq[0])
                n_sq[0] += 1
                act.activation(sqs[:, :], src[:, t, half * 512:(half + 1) * 512], ACT.Square,
                               accum_out=ssq[:, n, 2 * t + half:2 * t + half + 1]).then_inc(sem("ssq_ready"), 1)

            def norm_hi(n):
                g, o = NORM_GAIN[n]
                for f in range(KD):
                    if f % 2 == 0:
                        act.wait_ge(sem("xt_tr"), 4 * n + f // 2 + 1)
                    act.activation(xth[:, f, :], AUX[f // 2][:, (f % 2) * TOK:(f % 2 + 1) * TOK], ACT.Copy,
                                   scale=col(g, o + f, 1)).then_inc(sem("xt_hi"), 1)

            hi_upto(2)
            act.wait_ge(sem("mem_landed"), 16)
            for t in range(TT):
                for half in range(2):
                    squares(0, xn, t, half)
            act.wait_ge(sem("x_landed"), 16)
            for t in range(TT):
                for half in range(2):
                    squares(1, xres, t, half)
            act.wait_ge(sem("col_landed"), 16)
            norm_hi(0)
            act.activation(sp_[:, 0, :], col("ldt"), ACT.Exp).then_inc(sem("par_a"), 1)
            hi_upto(end_pair("km") - 2)
            act.wait_ge(sem("par_d"), 1)
            act.activation(sp_[:, 3, :], sp_[:, 1, :], ACT.Exp).then_inc(sem("par_a"), 1)
            act.activation(lamv[:, 2:4], lamv[:, 0:2], ACT.Exp).then_inc(sem("par_a"), 1)
            act.activation(lamv[:, 6:8], lamv[:, 4:6], ACT.Exp).then_inc(sem("par_a"), 1)
            act.activation(sp_[:, 6, :], sp_[:, 5, :], ACT.Sin).then_inc(sem("par_a"), 1)
            act.activation(sp_[:, 7, :], sp_[:, 5, :], ACT.Sin, scale=0.5).then_inc(sem("par_a"), 1)
            hi_upto(end_pair("km") + 1)
            for t in range(TT):
                act.wait_ge(pair_used, end_pair("km"))
                act.copy(kmT[:, 2 * t:2 * t + 2, :], PJ[0][:, t, :]).then_inc(sem("mem_ev"), 1)
            hi_upto(end_pair("vm") + 1)
            for t in range(TT):
                act.wait_ge(pair_used, end_pair("vm"))
                act.copy(vm[:, t, :], PJ[1][:, t, :]).then_inc(sem("mem_ev"), 1)

            for l in range(LAYERS):
                act.wait_ge(pair_used, FIRST[chunk(f"ssm_u{l}")])
                norm_hi(1 + 2 * l)
                hi_upto(end_pair(f"ssm_u{l}") + 2)
                for s in range(ST):
                    act.wait_ge(sem("bu_done"), ST * l + s + 1)
                    act.copy(bu[:, s, :, :], AUX[s % 4][:, :]).then_inc(sem("bu_ready"), 1)
                    if s % 2:
                        hi_upto(end_pair(f"ssm_u{l}") + 3 + s // 2)
                for i, nm in enumerate("qk"):
                    c = chunk(f"{nm}{l}")
                    hi_upto(end_pair(f"{nm}{l}") + 1)
                    act.wait_ge(pair_used, FIRST[c] + PAIRS[c])
                    for t in range(TT):
                        if t == 0 and (i or l):
                            act.wait_ge(sem("hss_ready"), 2 * l + i)
                        act.activation(hsq[:, t, :], PJ[BUF[c]][:, t, :], ACT.Square).then_inc(sem("hsq_ready"), 1)
                    if i == 1:
                        hi_upto(end_pair(f"k{l}") + 3)
                        act.wait_ge(sem("qk_tr"), 2 * l + 1)
                        act.copy(qT[:, 0:2, :], S0[:, :]).then_inc(sem("qk_ev"), 1)
                        act.copy(qT[:, 2:4, :], S1[:, :]).then_inc(sem("qk_ev"), 1)
                c = chunk(f"v{l}")
                hi_upto(end_pair(f"v{l}") + 2)
                act.wait_ge(pair_used, FIRST[c] + PAIRS[c])
                for t in range(TT):
                    m = act.copy(v_sb[:, t, :], PJ[BUF[c]][:, t, :])
                    m.then_inc(sem("v_ready"), 1)
                act.wait_ge(sem("qk_tr"), 2 * l + 2)
                act.copy(kT[:, 0:2, :], T0[:, :]).then_inc(sem("qk_ev"), 1)
                act.copy(kT[:, 2:4, :], T1[:, :]).then_inc(sem("qk_ev"), 1)
                c = chunk(f"gmlp{l}")
                hi_upto(end_pair(f"gmlp{l}") + 2)
                act.wait_ge(pair_used, FIRST[c] + PAIRS[c])
                act.wait_ge(sem("ssq_ready"), n_sq[0])
                for t in range(TT):
                    if t:
                        act.wait_ge(sem("gss_ready"), 2 * l + 1)
                    act.activation(sqs[:, 0:256], PJ[BUF[c]][:, t, 256:512], ACT.Square,
                                   accum_out=gss[:, l, t:t + 1]).then_inc(sem("gss_ready"), 1)

                def exps(s):
                    n = P * (s % TT + 1)
                    act.wait_ge(sem("nb_ready"), 8 * l + s + 1)
                    for c in range(2):
                        act.activation(sm[:, s % 2, c, 0:n], sm[:, s % 2, c, 0:n], ACT.Exp, bias=st_[:, s, 2 + c:3 + c],
                                       scale=QKD ** -0.5, accum_out=st_[:, s, 4 + c:5 + c]).then_inc(sem("exp_done"), 1)

                def prob_evac(s):
                    n = P * (s % TT + 1)
                    act.wait_ge(sem("pt_tr"), 8 * l + s + 1)
                    act.copy(pT[:, s % 2, 0:s % TT + 1, :], (T0, T1)[s % 2][:, 0:n]).then_inc(sem("pt_ev"), 1)

                def out_evac(s):
                    h, t = divmod(s, TT)
                    act.wait_ge(sem("pv_done"), 8 * l + s + 1)
                    act.activation(xn[:, t, h * VD:(h + 1) * VD], PJ[buf(f"v{l}")][:, s % 2, 0:P], ACT.Copy,
                                   scale=st_[:, s, 6:7]).then_inc(sem("o_ev"), 1)

                for s in range(8 + 2):
                    if s < 8:
                        exps(s)
                    if 1 <= s <= 8:
                        prob_evac(s - 1)
                    if s >= 2:
                        out_evac(s - 2)
                    if s == 4:
                        hi_upto(end_pair(f"gmlp{l}") + RING)
                for t in range(TT):
                    act.wait_ge(sem("o_ev"), 8 * (l + 1))
                    act.activation(hsq[:, t, :], xn[:, t, 0:512], ACT.Square).then_inc(sem("osq_ready"), 1)
                act.wait_ge(sem("ypre_ready"), 2 * (l + 1))
                for f in range(2):
                    act.activation(md[:, 0, f, :], md[:, 1, f, :], ACT.Gelu_apprx_tanh).then_inc(sem("gelu_ready"), 1)
                act.wait_ge(sem("mix_tr"), 2 * l + 1)
                act.wait_ge(pair_used, end_pair(f"gmlp{l}"))
                act.copy(xth[:, 2:4, :], S0[:, :]).then_inc(sem("mix_hi"), 1)
                act.wait_ge(sem("mix_tr"), 2 * l + 2)
                act.copy(xth[:, 4:6, :], S1[:, :]).then_inc(sem("mix_hi"), 1)
                act.copy(xth[:, 6:8, :], T0[:, :]).then_inc(sem("mix_hi"), 1)
                act.wait_ge(sem("glu_done"), l + 1)
                for f in range(2):
                    act.activation(md[:, 1, f, :], S0[:, f * TOK:(f + 1) * TOK], ACT.Tanh, scale=0.5,
                                   bias=hb[:, 2 * l + f:2 * l + f + 1]).then_inc(sem("tanh_ready"), 1)
                act.wait_ge(sem("glu_prod"), l + 1)
                act.activation(xth[:, 0:2, :], md[:, 2, :, :], ACT.Copy, scale=0.5).then_inc(sem("mix_hi"), 1)
                for i in range(2):
                    nm = f"out{l}_{i}"
                    hi_upto(end_pair(nm) + (1 if i == 0 else RING))
                    for t in range(TT):
                        act.wait_ge(sem("resid"), 8 * l + 2 * i + t + 1)
                        squares(2 + 2 * l, xres, t, i)
                act.wait_ge(pair_used, end_pair(f"out{l}_1"))
                norm_hi(2 + 2 * l)

                def unit_first(j):
                    c = chunk(f"up{l}_{j}")
                    act.wait_ge(pair_used, FIRST[c] + PAIRS[c])
                    if UNITS * l + j >= 2:
                        act.wait_ge(sem("gated"), UNITS * l + j - 1)
                    for i in range(4):
                        k = conv_col(l, j, i)
                        act.activation(acc[:, j % 2, i, :], PJ[BUF[c]][:, i // 2, (i % 2) * TOK:(i % 2 + 1) * TOK],
                                       ACT.Identity, scale=colv[:, k + 2:k + 3], bias=colv[:, k + 3:k + 4]).then_inc(sem("conv_a"), 1)

                def unit_gelu(j):
                    act.wait_ge(sem("conv_d"), 4 * (UNITS * l + j + 1))
                    act.activation(acc[:, j % 2, 0:2, :], acc[:, j % 2, 0:2, :], ACT.Gelu_apprx_tanh).then_inc(sem("ffn_gelu"), 1)

                def unit_hi(j):
                    act.wait_ge(sem("gated"), UNITS * l + j + 1)
                    act.copy(hth[:, 2 * j:2 * j + 2, :], gtd[:, j % 2, :, :]).then_inc(sem("ht_hi"), 1)

                for j in range(UNITS + 1):
                    if j < UNITS:
                        hi_upto(end_pair(f"up{l}_{j}") + 3)
                        unit_first(j)
                    if j > 0:
                        unit_hi(j - 1)
                    if j < UNITS:
                        unit_gelu(j)
                for i in range(2):
                    nm = f"down{l}_{i}"
                    hi_upto(end_pair(nm) + (1 if i == 0 else RING))
                    for t in range(TT):
                        if l == LAYERS - 1 and upto == 1:
                            continue
                        act.wait_ge(sem("resid"), 8 * l + 4 + 2 * i + t + 1)
                        squares(3 + 2 * l, xres, t, i)
            if upto == 1:
                return

            act.wait_ge(pair_used, FIRST[chunk("mq")])
            norm_hi(5)
            hi_upto(end_pair("mq") + 1)
            act.wait_ge(pair_used, end_pair("mq"))
            for t in range(TT):
                act.copy(mqT[:, 2 * t:2 * t + 2, :], PJ[buf("mq")][:, t, :]).then_inc(sem("mq_ev"), 1)
            hi_upto(end_pair("bq") + 1)
            act.wait_ge(pair_used, end_pair("bq"))
            for t in range(TT):
                act.activation(sm2[:, t, 0:512], PJ[buf("bq")][:, t, :], ACT.Square).then_inc(sem("bsq_ready"), 1)
            hi_upto(end_pair("bkv") + 1)
            act.wait_ge(pair_used, end_pair("bkv"))
            for t in range(TT):
                act.activation(pT2[:, t, 0, :], PJ[buf("bkv")][:, t, 0:P], ACT.Square).then_inc(sem("bksq_ready"), 1)
                act.copy(bv[:, t, :], PJ[buf("bkv")][:, t, P:2 * P]).then_inc(sem("bv_ready"), 1)

            def gate_tanh(nm, th):
                i = SILU_ORDER.index(nm)
                act.wait_ge(pair_used, end_pair(nm))
                if i == 1:
                    act.wait_ge(sem("silu_ready"), 2)
                for t in range(TT):
                    act.activation(th[:, t, 0:512], PJ[buf(nm)][:, t, :], ACT.Tanh, scale=0.5).then_inc(sem("th_ready"), 1)

            hi_upto(end_pair("gb") + 2)
            act.wait_ge(sem("bhss_ready"), 1)
            gate_tanh("gb", sm2)
            act.wait_ge(sem("b_tr"), 1)
            act.copy(bqT[:, 0:2, :], T0[:, :]).then_inc(sem("b_ev"), 1)
            act.copy(bqT[:, 2:4, :], T1[:, :]).then_inc(sem("b_ev"), 1)
            act.wait_ge(sem("b_tr"), 2)
            act.copy(bkT[:, :, :], S0[:, :]).then_inc(sem("b_ev"), 1)
            hi_upto(end_pair("gm") + 2)
            gate_tanh("gm", sm2)
            for c, nm in enumerate(A_CHUNKS):
                for j in range(4):
                    n = 4 * c + j
                    hi_upto(F2 + n + 3)
                    if j == 1 and c >= 7:
                        g = c - 7
                        act.wait_ge(pair_used, end_pair(f"av{g}"))
                        for t in range(TT):
                            act.copy(va[:, g, t, :], PJ[buf(f"av{g}")][:, t, :]).then_inc(sem("av_ready"), 1)
                    if 1 <= c <= 6 and j >= 2:
                        rnd = 2 * (c - 1) + j - 2
                        act.wait_ge(sem("a_tr"), rnd + 1)
                        w, g = divmod(c - 1, NG)
                        act.copy(aqT[:, w, g, 2 * (j - 2):2 * (j - 2) + 2, :], S1[:, :]).then_inc(sem("a_ev"), 1)
                    for k in bm_slots(n):
                        if k < len(BM):
                            br, h, t = BM[k]
                            act.wait_ge(sem("bm_nb"), k + 1)
                            if k == 0:
                                act.wait_ge(sem("silu_ready"), 4)
                            if k >= 2:
                                act.wait_ge(sem("bm_tr"), k - 1)
                            act.activation(sm2[:, k % 2, 0:TOK], S0[:, 0:TOK], ACT.Exp, bias=sx[:, k % 4, 1:2],
                                           scale=(HD if br == "b" else MD) ** -0.5,
                                           accum_out=sx[:, k % 4, 2:3]).then_inc(sem("bm_exp"), 1)
                        if 1 <= k <= len(BM):
                            act.wait_ge(sem("bm_tr"), k)
                            if k >= 3:
                                act.wait_ge(sem("bm_pv"), k - 2)
                            act.copy(pT2[:, (k - 1) % 2, 0:2, :], T0[:, 0:TOK]).then_inc(sem("bm_pt"), 1)
            hi_upto(F3 + 2)
            act.wait_ge(sem("a_tr"), 12)
            gate_tanh("ga", rt)
            for n in range(24):
                hi_upto(F3 + n + 3)
                for k in a_slots(n):
                    if k < AH * TT:
                        act.wait_ge(sem("a_nb"), k + 1)
                        act.activation(sm2[:, k % 2, :], sm2[:, k % 2, :], ACT.Exp, bias=sx[:, k % 4, 1:2], scale=HD ** -0.5,
                                       accum_out=sx[:, k % 4, 2:3]).then_inc(sem("a_exp"), 1)
                    if 1 <= k <= AH * TT:
                        act.wait_ge(sem("a_ptr"), k)
                        if k >= 3:
                            act.wait_ge(sem("apv_done"), k - 2)
                        act.copy(pT2[:, (k - 1) % 2, 0:4, :], T0[:, :]).then_inc(sem("a_pt"), 1)
                        act.copy(pT2[:, (k - 1) % 2, 4:6, :], T1[:, 0:TOK]).then_inc(sem("a_pt"), 1)
                if n % 4 == 1 and n > 4:
                    merge_tanh(act, n // 4 - 1)
            merge_tanh(act, 5)
            hi_upto(F3 + 24 + RING)
            for i in range(6):
                act.wait_ge(sem("o_tr"), i + 1)
                act.activation(oth[:, 2 * i:2 * i + 2, :], AUX[i % 4][:, :], ACT.Copy, scale=0.5).then_inc(sem("o_hi"), 1)
            hi_upto(FIRST[chunk("wo0")] + 3)
            for i in range(4):
                act.wait_ge(sem("m_tr"), i + 1)
                act.activation(xth[:, 2 * i:2 * i + 2, :], AUX[i][:, :], ACT.Copy, scale=0.5).then_inc(sem("m_hi"), 1)
            for i in range(2):
                nm = f"wo{i}"
                hi_upto(end_pair(nm) + 1)
                act.wait_ge(pair_used, end_pair(nm))
                for t in range(TT):
                    act.wait_ge(sem("ssq_ready"), n_sq[0])
                    n_sq[0] += 1
                    act.activation(sqs[:, :], PJ[buf(nm)][:, t, :], ACT.Square,
                                   accum_out=ssq[:, 6, 2 * t + i:2 * t + i + 1]).then_inc(sem("ssq_ready"), 1)

        @block.gpsimd
        def _(pool):
            pool.memset(mhalf[:], -0.5).then_inc(sem("mhalf_ready"), 1)
            pool.wait_ge(sem("mhalf_ready"), 1)

            steps = [0]

            def link(ins):
                steps[0] += 1
                ins.then_inc(sem("pool_chain"), 1)
                pool.wait_ge(sem("pool_chain"), steps[0])

            def power(out_, in_, n, width, signal):
                link(pool.tensor_scalar(out_, in_, 1.0 / width, EPS, ALU.mult, ALU.add))
                pool.tensor_tensor(out_, out_, mhalf[:, 0:n], ALU.pow).then_inc(sem(signal), 1)

            def norm_rstd(n):
                pool.wait_ge(sem("ssq_ready"), 4 * (n + 1))
                link(pool.tensor_tensor(ssm1[:, n, :], ssq[:, n, 0:4:2], ssq[:, n, 1:4:2], ALU.add))
                power(rstd[:, n, :], ssm1[:, n, :], 2, D, "rstd_ready")

            def tables(l):
                lo8 = slice(8 * l, 8 * l + 8)
                c1, s1 = sp_[:, 8, lo8], sp_[:, 6, lo8]
                pool.memset(tab[:, 0, :, 0:1], 1.0).then_inc(sem("pool_chain"), 1)
                pool.memset(tab[:, 1, :, 0:1], 0.0).then_inc(sem("pool_chain"), 1)
                pool.tensor_copy(pw[:, 0, :], c1).then_inc(sem("pool_chain"), 1)
                pool.tensor_copy(pw[:, 1, :], s1).then_inc(sem("pool_chain"), 1)
                steps[0] += 4
                pool.wait_ge(sem("pool_chain"), steps[0])
                n = 1
                while n < TOK:
                    m = min(n, 32)
                    for a in range(0, n, m):
                        c, s = tab[:, 0, :, a:a + m], tab[:, 1, :, a:a + m]
                        C, S = wide(pw[:, 0, :], m, 2), wide(pw[:, 1, :], m, 2)
                        t1, t2 = pq[:, 0, :, 0:m], pq[:, 1, :, 0:m]
                        for first, second, op, o in ((C, S, ALU.subtract, 0), (S, C, ALU.add, 1)):
                            pool.tensor_tensor(t1, c, first, ALU.mult).then_inc(sem("pool_chain"), 1)
                            pool.tensor_tensor(t2, s, second, ALU.mult).then_inc(sem("pool_chain"), 1)
                            steps[0] += 2
                            pool.wait_ge(sem("pool_chain"), steps[0])
                            link(pool.tensor_tensor(tab[:, o, :, n + a:n + a + m], t1, t2, op))
                    link(pool.tensor_tensor(pw[:, 2, :], pw[:, 0, :], pw[:, 0, :], ALU.mult))
                    link(pool.tensor_tensor(pw[:, 3, :], pw[:, 1, :], pw[:, 1, :], ALU.mult))
                    link(pool.tensor_tensor(pw[:, 4, :], pw[:, 0, :], pw[:, 1, :], ALU.mult))
                    link(pool.tensor_tensor(pw[:, 0, :], pw[:, 2, :], pw[:, 3, :], ALU.subtract))
                    link(pool.tensor_tensor(pw[:, 1, :], pw[:, 4, :], pw[:, 4, :], ALU.add))
                    n *= 2

            def fold_coefficient(l):
                pool.wait_ge(sem("cex_landed"), 16 * (l + 1))
                lo8 = slice(8 * l, 8 * l + 8)
                for s in range(ST):
                    cr, ci, nci, ncr = (sp_[:, r, 8 * l + s:8 * l + s + 1] for r in (9, 10, 11, 12))
                    re, im = cex[:, 0, s, :], cex[:, 1, s, :]
                    a, b, c, d = (ft[:, i, :] for i in range(4))
                    for o, i_, k in ((a, re, cr), (b, im, nci), (c, re, nci), (d, im, ncr)):
                        pool.tensor_scalar(o, i_, k, None, ALU.mult).then_inc(sem("pool_chain"), 1)
                        steps[0] += 1
                    pool.wait_ge(sem("pool_chain"), steps[0])
                    pool.tensor_tensor(re, a, b, ALU.add).then_inc(sem("cex_ready"), 1)
                    pool.tensor_tensor(im, c, d, ALU.add).then_inc(sem("cex_ready"), 1)
                    pool.wait_ge(sem("cex_ready"), 2 * (ST * l + s + 1))

            def pre_rotate(l, s):
                pool.wait_ge(sem("bu_ready"), ST * l + s + 1)
                if ST * l + s:
                    pool.wait_ge(sem("pre_rot"), 2 * (ST * l + s))
                cc, ss = wide(tab[:, 0, s, :], 2), wide(tab[:, 1, s, :], 2)
                pool.tensor_tensor(mp[:, 0, :, :], bu[:, s, :, :], cc, ALU.mult).then_inc(sem("pool_chain"), 1)
                pool.tensor_tensor(mp[:, 1, :, :], bu[:, s, :, :], ss, ALU.mult).then_inc(sem("pool_chain"), 1)
                steps[0] += 2
                pool.wait_ge(sem("pool_chain"), steps[0])
                pool.tensor_tensor(bu[:, s, 0, :], mp[:, 0, 0, :], mp[:, 1, 1, :], ALU.add).then_inc(sem("pre_rot"), 1)
                pool.tensor_tensor(bu[:, s, 1, :], mp[:, 0, 1, :], mp[:, 1, 0, :], ALU.subtract).then_inc(sem("pre_rot"), 1)

            norm_rstd(0)
            norm_rstd(1)
            pool.wait_ge(sem("par_done"), 1)
            tables(0)
            fold_coefficient(0)
            for l in range(LAYERS):
                if l > 0:
                    norm_rstd(1 + 2 * l)

                for s in range(ST):
                    pre_rotate(l, s)
                    if s in (3, 7):
                        pool.wait_ge(sem("hss_ready"), 2 * l + s // 4 + 1)
                        power(hr[:, s // 4, 0:16], hss[:, :], 16, QKD, "hr_ready")
                    if s == 7:
                        pool.wait_ge(sem("gss_ready"), 2 * (l + 1))
                        power(gr[:, l, :], gss[:, l, :], 2, 256, "gr_ready")
                pool.wait_ge(sem("oss_ready"), l + 1)
                power(hr[:, 0, 0:8], hss[:, 0:8], 8, VD, "or_ready")
                norm_rstd(2 + 2 * l)
                for j in range(UNITS):
                    pool.wait_ge(sem("ffn_gelu"), UNITS * l + j + 1)
                    if j >= 2 or l:
                        pool.wait_ge(sem("ht_lo"), UNITS * l + j - 1)
                    pool.tensor_tensor(gtd[:, j % 2, :, :], acc[:, j % 2, 0:2, :], acc[:, j % 2, 2:4, :],
                                       ALU.mult).then_inc(sem("gated"), 1)
                    if j == 1 and l + 1 < LAYERS:
                        pass
                if l + 1 < LAYERS:
                    tables(l + 1)
                    fold_coefficient(l + 1)
            if upto == 1:
                return

            norm_rstd(5)
            pool.wait_ge(sem("bhss_ready"), 1)
            power(hr[:, 0, 0:16], hss[:, 0:16], 16, HD, "bhr_ready")
            pool.wait_ge(sem("bhss_ready"), 2)
            power(hr[:, 1, 0:4], hss[:, 0:4], 4, HD, "bhr_ready")
            for c in range(6):
                if c:
                    pool.wait_ge(sem("a_tr"), 2 * c)
                else:
                    pool.wait_ge(sem("b_tr"), 1)
                for t in range(TT):
                    pool.wait_ge(sem("rot_terms"), 4 * c + 2 * t + 2)
                    c8, s8 = (xn[:, t, i * 512:(i + 1) * 512].rearrange("p (g d) -> p g d", g=8) for i in range(2))
                    o8 = rt[:, t, :].rearrange("p (g d) -> p g d", g=8)
                    pool.tensor_tensor(o8[:, :, 0:32], c8[:, :, 0:32], s8[:, :, 32:64], ALU.subtract).then_inc(sem("a_rope"), 1)
                    pool.tensor_tensor(o8[:, :, 32:64], c8[:, :, 32:64], s8[:, :, 0:32], ALU.add).then_inc(sem("a_rope"), 1)
            for i in range(6):
                b, n = BRANCH_ORDER[i][0], int(BRANCH_ORDER[i][1])
                if b == "a":
                    continue
                for t in range(TT):
                    pool.wait_ge(sem("y_gated"), 2 * i + t + 1)
                    m = merged[:, t, 512 * n:512 * n + 512]
                    at = ("abm".index(b)) * D + 512 * n
                    if b == "m":
                        pool.wait_ge(sem("merged_b"), 2 * n + t + 1)
                    pool.tensor_tensor(m, m, gt[:, t, at:at + 512], ALU.add).then_inc(sem("merged_b" if b == "b" else "merged_ready"), 1)
            norm_rstd(6)

        @block.vector
        def _(dve):
            at = [0]
            steps = [0]
            stop_pair = FIRST[chunk("mq")] if upto == 1 else NPAIRS

            def link(ins):
                steps[0] += 1
                ins.then_inc(sem("dve_chain"), 1)
                dve.wait_ge(sem("dve_chain"), steps[0])

            def lo_upto(n):
                while at[0] < min(n, stop_pair):
                    p = at[0]
                    dve.wait_ge(hi_ready, p + 1)
                    dve.tensor_tensor(wlo[:, p % RING, :], raw[:, p % RAW, :], whi[:, p % RING, :].bitcast(F32),
                                      ALU.subtract).then_inc(lo_ready, 1)
                    at[0] += 1

            def norm_scale(n, src):
                dve.wait_ge(sem("rstd_ready"), n + 1)
                for t in range(TT):
                    dve.tensor_scalar(xn[:, t, :], src[:, t, :], rstd[:, n, t:t + 1], None, ALU.mult).then_inc(sem("xn_ready"), 1)

            def norm_lo(n):
                g, o = NORM_GAIN[n]
                for f in range(KD):
                    dve.wait_ge(sem("xt_hi"), KD * n + f // 2 * 2 + 2)
                    dve.scalar_tensor_tensor(out=xtl[:, f, :], in0=AUX[f // 2][:, (f % 2) * TOK:(f % 2 + 1) * TOK],
                                             scalar=col(g, o + f, 1), in1=xth[:, f, :].bitcast(F32),
                                             op0=ALU.mult, op1=ALU.subtract).then_inc(sem("xt_lo"), 1)

            norm_scale(0, xn)
            lo_upto(2)
            norm_lo(0)
            v = [sp_[:, i, :] for i in range(24)]
            dve.wait_ge(sem("row_landed"), 16)
            dve.wait_ge(sem("par_a"), 1)
            link(dve.tensor_tensor(v[1], col("are"), v[0], ALU.mult))
            link(dve.tensor_tensor(v[2], col("aim"), v[0], ALU.mult))
            link(dve.tensor_scalar(v[4], v[2], 1.0 / (2 * math.pi), None, ALU.mult))
            link(dve.tensor_scalar(v[4], v[4], 12582912.0, None, ALU.add))
            link(dve.tensor_scalar(v[4], v[4], -12582912.0, None, ALU.add))
            c1 = 6.28125
            c2 = round((2 * math.pi - c1) * 2 ** 21) / 2 ** 21
            c3 = 2 * math.pi - c1 - c2
            src_ = v[2]
            for cc in (c1, c2, c3):
                link(dve.scalar_tensor_tensor(out=v[5], in0=v[4], scalar=-cc, in1=src_, op0=ALU.mult, op1=ALU.add))
                src_ = v[5]
            link(dve.tensor_scalar(v[5], v[5], 3.1415925, -3.1415925, ALU.min, ALU.max))
            dve.wait_ge(sem("lam_landed"), 16)
            lamrow = bu[:, 0, :, :].rearrange("p c t -> p (c t)")
            for l in range(LAYERS):
                for i, (a, b) in enumerate((("lq1", "lk1"), ("lq2", "lk2"))):
                    ra, rb = (lamrow[:, LAM[z][0] + 64 * l:LAM[z][0] + 64 * l + 64] for z in (a, b))
                    link(dve.tensor_tensor_reduce(sqs2[:, :], ra, rb, 1.0, 0.0,
                                                  ALU.mult, ALU.add, lamv[:, 4 * i + l:4 * i + l + 1]))
            dve.sem_inc(sem("par_d"), 1)
            lo_upto(end_pair("km") - 3)
            cosv = cs("cos").rearrange("p (t d) -> p t d", t=TT)
            sinv = cs("sin").rearrange("p (t d) -> p t d", t=TT)
            for l in range(LAYERS):
                for i, (g, tb) in enumerate((("qg", cosv), ("qg", sinv), ("kg", cosv), ("kg", sinv))):
                    link(dve.tensor_tensor(ropeq[:, l, i, :, :], tb, wide(row(g, 64 * l, 64), TT), ALU.mult))
                link(dve.tensor_scalar(row("sub", VD * l, VD), row("sub", VD * l, VD), 1.0 - LAMBDA_INIT[l], None, ALU.mult))
            dve.wait_ge(sem("col_landed"), 16)
            link(dve.tensor_scalar(hb[:, :], col("bglu"), 0.5, None, ALU.mult))
            dve.wait_ge(sem("par_a"), 6)
            for l in range(LAYERS):
                link(dve.tensor_tensor(nlam[:, l:l + 1], lamv[:, 6 + l:7 + l], lamv[:, 2 + l:3 + l], ALU.subtract))
                link(dve.tensor_scalar(nlam[:, l:l + 1], nlam[:, l:l + 1], -LAMBDA_INIT[l], None, ALU.add))
            are, aim = col("are"), col("aim")
            link(dve.tensor_tensor(v[13], v[7], v[7], ALU.mult))
            link(dve.tensor_scalar(v[8], v[13], -2.0, 1.0, ALU.mult, ALU.add))
            link(dve.tensor_tensor(v[14], v[3], v[8], ALU.mult))
            link(dve.tensor_tensor(v[15], v[3], v[6], ALU.mult))
            link(dve.tensor_scalar(v[14], v[14], -1.0, None, ALU.add))
            link(dve.tensor_tensor(v[16], are, are, ALU.mult))
            link(dve.tensor_tensor(v[17], aim, aim, ALU.mult))
            link(dve.tensor_tensor(v[16], v[16], v[17], ALU.add))
            link(dve.reciprocal(v[16], v[16]))
            link(dve.tensor_tensor(v[17], v[14], are, ALU.mult))
            link(dve.tensor_tensor(v[18], v[15], aim, ALU.mult))
            link(dve.tensor_tensor(v[17], v[17], v[18], ALU.add))
            link(dve.tensor_tensor(v[9], v[17], v[16], ALU.mult))
            link(dve.tensor_tensor(v[17], v[15], are, ALU.mult))
            link(dve.tensor_tensor(v[18], v[14], aim, ALU.mult))
            link(dve.tensor_tensor(v[17], v[17], v[18], ALU.subtract))
            link(dve.tensor_tensor(v[10], v[17], v[16], ALU.mult))
            link(dve.tensor_scalar(v[11], v[10], -1.0, None, ALU.mult))
            link(dve.tensor_scalar(v[12], v[9], -1.0, None, ALU.mult))
            dve.sem_inc(sem("par_done"), 1)
            lo_upto(end_pair("km") + 1)
            lo_upto(end_pair("vm") - 2)

            for l in range(LAYERS):
                dve.wait_ge(sem("wst_landed"), 16 * (l + 1))
                dve.memset(wsts[64:128, :, 0:64], 0.0).then_inc(sem("wst_ready"), 1)
                dve.wait_ge(sem("xt_tr"), 4 * (1 + 2 * l))
                norm_scale(1 + 2 * l, xres)
                if l == 0:
                    lo_upto(end_pair("vm") + 1)
                norm_lo(1 + 2 * l)
                lo_upto(end_pair(f"ssm_u{l}") + 1)
                c = chunk(f"ssm_u{l}")
                dve.wait_ge(pair_used, FIRST[c] + PAIRS[c])
                dve.tensor_copy(uT[:, :, :], PJ[BUF[c]][:, 0, :]).then_inc(sem("u_ready"), 1)
                lo_upto(end_pair(f"ssm_u{l}") + 3)

                def qk_norm_rope(i, nm):
                    c = chunk(f"{nm}{l}")
                    pj = PJ[BUF[c]]
                    lo_upto(end_pair(f"{nm}{l}") + 1)
                    dve.wait_ge(sem("hsq_ready"), 4 * l + 2 * i + 2)
                    if i or l:
                        dve.wait_ge(sem("hr_ready"), 2 * l + i)
                    for t in range(TT):
                        m = dve.tensor_reduce(hss[:, 8 * t:8 * t + 8], hsq[:, t, :].rearrange("p (g d) -> p g d", g=8), AX.X, ALU.add)
                        if t == 0:
                            steps[0] += 1
                            m.then_inc(sem("dve_chain"), 1)
                            dve.wait_ge(sem("dve_chain"), steps[0])
                    m.then_inc(sem("hss_ready"), 1)
                    lo_upto(end_pair(f"{nm}{l}") + 2)
                    dve.wait_ge(sem("hr_ready"), 2 * l + i + 1)
                    for t in range(TT):
                        g8 = pj[:, t, :].rearrange("p (g d) -> p g d", g=8)
                        dve.tensor_tensor(qn[:, t, :].rearrange("p (g d) -> p g d", g=8), g8,
                                          wide(hr[:, i, 8 * t:8 * t + 8], QKD, 2), ALU.mult).then_inc(sem("qn_ready"), 1)
                    dve.wait_ge(sem("qn_ready"), 2 * (2 * l + i + 1))
                    for t in range(TT):
                        q8 = qn[:, t, :].rearrange("p (g d) -> p g d", g=8)
                        t2 = hsq[:, t, :].rearrange("p (g d) -> p g d", g=8)
                        o8 = xn[:, t, 512 * i:512 * i + 512].rearrange("p (g d) -> p g d", g=8)
                        cg, sg = (wide(ropeq[:, l, 2 * i + j, t, :], 8) for j in range(2))
                        dve.tensor_tensor(t2, q8, sg, ALU.mult).then_inc(sem("dve_chain"), 1)
                        dve.tensor_tensor(q8, q8, cg, ALU.mult).then_inc(sem("dve_chain"), 1)
                        steps[0] += 2
                        dve.wait_ge(sem("dve_chain"), steps[0])
                        dve.tensor_tensor(o8[:, :, 0:32], q8[:, :, 0:32], t2[:, :, 32:64], ALU.subtract).then_inc(sem("rope_ready"), 1)
                        dve.tensor_tensor(o8[:, :, 32:64], q8[:, :, 32:64], t2[:, :, 0:32], ALU.add).then_inc(sem("rope_ready"), 1)

                def ssm_scan(s):
                    dve.wait_ge(sem("pre_rot"), 2 * (ST * l + s + 1))
                    if ST * l + s:
                        dve.wait_ge(sem("state_ready"), 2 * (ST * l + s))
                    r = sp_[:, 3, 8 * l + s:8 * l + s + 1].to_broadcast([P, TOK])
                    for c in range(2):
                        dve.tensor_tensor_scan(md[:, 0, c, :], r, bu[:, s, c, :], 0.0, ALU.mult, ALU.add).then_inc(sem("dve_chain"), 1)
                    steps[0] += 2
                    dve.wait_ge(sem("dve_chain"), steps[0])
                    cc, ss = wide(tab[:, 0, s, :], 2), wide(tab[:, 1, s, :], 2)
                    dve.tensor_tensor(md[:, 1, :, :], md[:, 0, :, :], cc, ALU.mult).then_inc(sem("dve_chain"), 1)
                    dve.tensor_tensor(md[:, 2, :, :], md[:, 0, :, :], ss, ALU.mult).then_inc(sem("dve_chain"), 1)
                    steps[0] += 2
                    dve.wait_ge(sem("dve_chain"), steps[0])
                    dve.tensor_tensor(bu[:, s, 0, :], md[:, 1, 0, :], md[:, 2, 1, :], ALU.subtract).then_inc(sem("state_ready"), 1)
                    dve.tensor_tensor(bu[:, s, 1, :], md[:, 1, 1, :], md[:, 2, 0, :], ALU.add).then_inc(sem("state_ready"), 1)

                qk_norm_rope(0, "q")
                lo_upto(end_pair(f"q{l}") + 3)
                ssm_scan(0)
                qk_norm_rope(1, "k")
                lo_upto(end_pair(f"k{l}") + 3)
                ssm_scan(1)
                lo_upto(end_pair(f"v{l}") + 1)
                ssm_scan(2)
                lo_upto(end_pair(f"gmlp{l}"))
                ssm_scan(3)
                c = chunk(f"gmlp{l}")
                dve.wait_ge(sem("gr_ready"), l + 1)
                dve.wait_ge(sem("qk_tr"), 2 * (l + 1))
                for t in range(TT):
                    dve.scalar_tensor_tensor(out=xn[:, t, 768:1024], in0=PJ[BUF[c]][:, t, 256:512], scalar=gr[:, l, t:t + 1],
                                             in1=row("vg", 256 * l, 256), op0=ALU.mult, op1=ALU.mult).then_inc(sem("vn_ready"), 1)
                    dve.tensor_copy(ug[:, t, :], PJ[BUF[c]][:, t, 0:256]).then_inc(sem("ug_ready"), 1)

                def mask_max(s):
                    h, t = divmod(s, TT)
                    n = P * (t + 1)
                    mk = cs("mdiff")[:, 0:128] if t == 0 else cs("mdiff")[:, 128:384]
                    dve.wait_ge(sem("sc_done"), 8 * l + s + 1)
                    if 8 * l + s >= 2:
                        dve.wait_ge(sem("pt_tr"), 8 * l + s - 1)
                    for c, bank in ((0, S0), (1, S1)):
                        dve.tensor_tensor_reduce(sm[:, s % 2, c, 0:n], bank[:, 0:n], mk, 1.0, BIG, ALU.add, ALU.max,
                                                 st_[:, s, c:c + 1]).then_inc(sem("sc_read"), 1)
                    dve.wait_ge(sem("sc_read"), 2 * (8 * l + s + 1))
                    dve.tensor_scalar(st_[:, s, 2:4], st_[:, s, 0:2], -(QKD ** -0.5), None, ALU.mult).then_inc(sem("nb_ready"), 1)

                def combine(s):
                    n = P * (s % TT + 1)
                    dve.wait_ge(sem("exp_done"), 2 * (8 * l + s + 1))
                    link(dve.reciprocal(st_[:, s, 6:8], st_[:, s, 4:6]))
                    link(dve.scalar_tensor_tensor(out=st_[:, s, 7:8], in0=st_[:, s, 7:8], scalar=st_[:, s, 4:5],
                                                  in1=nlam[:, l:l + 1], op0=ALU.mult, op1=ALU.mult))
                    dve.scalar_tensor_tensor(out=sm[:, s % 2, 1, 0:n], in0=sm[:, s % 2, 1, 0:n], scalar=st_[:, s, 7:8],
                                             in1=sm[:, s % 2, 0, 0:n], op0=ALU.mult, op1=ALU.add).then_inc(sem("w_ready"), 1)

                for s in range(9):
                    if s < 8:
                        mask_max(s)
                    if s in (1, 3, 5, 7):
                        ssm_scan(4 + s // 2)
                    if s > 0:
                        combine(s - 1)
                    if s == 5:
                        lo_upto(end_pair(f"gmlp{l}") + RING)
                dve.wait_ge(sem("sgu_done"), l + 1)
                for h in range(4):
                    dve.scalar_tensor_tensor(out=xn[:, :, 512 + h * 64:576 + h * 64],
                                             in0=T0[:, h * P:(h + 1) * P].rearrange("p (t d) -> p t d", t=TT),
                                             scalar=col("bs", 4 * l + h, 1), in1=ug[:, :, h * 64:(h + 1) * 64],
                                             op0=ALU.add, op1=ALU.mult).then_inc(sem("sgu_ready"), 1)
                dve.wait_ge(sem("y_done"), l + 1)
                for f in range(2):
                    dve.scalar_tensor_tensor(out=md[:, 1, f, :], in0=uT[:, f, :], scalar=col("dskip", 2 * l + f, 1),
                                             in1=T1[:, f * TOK:(f + 1) * TOK], op0=ALU.mult, op1=ALU.add).then_inc(sem("ypre_ready"), 1)
                dve.wait_ge(sem("osq_ready"), 2 * (l + 1))
                dve.wait_ge(sem("hr_ready"), 2 * (l + 1))
                dve.tensor_reduce(hss[:, 0:8], hsq[:, :, :].rearrange("p t (g d) -> p (t g) d", g=4), AX.X, ALU.add)\
                   .then_inc(sem("oss_ready"), 1)
                dve.wait_ge(sem("mix_tr"), 2 * l + 1)
                dve.wait_ge(sem("mix_hi"), 4 * l + 1)
                dve.tensor_tensor(xtl[:, 2:4, :], S0[:, :].rearrange("p (f d) -> p f d", f=2), xth[:, 2:4, :].bitcast(F32),
                                  ALU.subtract).then_inc(sem("mix_lo"), 1)
                dve.wait_ge(sem("or_ready"), l + 1)
                a8 = xn[:, :, 0:512]
                for t in range(TT):
                    a4 = xn[:, t, 0:512].rearrange("p (g d) -> p g d", g=4)
                    link(dve.tensor_tensor(a4, a4, wide(hr[:, 0, 4 * t:4 * t + 4], VD, 2), ALU.mult))
                    dve.tensor_tensor(a4, a4, wide(row("sub", VD * l, VD), 4), ALU.mult).then_inc(sem("diff_ready"), 1)
                dve.wait_ge(sem("mix_hi"), 4 * l + 3)
                for i, bank in enumerate((S1, T0)):
                    dve.tensor_tensor(xtl[:, 4 + 2 * i:6 + 2 * i, :], bank[:, :].rearrange("p (f d) -> p f d", f=2),
                                      xth[:, 4 + 2 * i:6 + 2 * i, :].bitcast(F32), ALU.subtract).then_inc(sem("mix_lo"), 1)
                dve.wait_ge(sem("tanh_ready"), 2 * (l + 1))
                dve.scalar_tensor_tensor(out=md[:, 2, :, :], in0=md[:, 1, :, :], scalar=1.0, in1=md[:, 0, :, :],
                                         op0=ALU.add, op1=ALU.mult).then_inc(sem("glu_prod"), 1)
                dve.wait_ge(sem("mix_hi"), 4 * (l + 1))
                dve.scalar_tensor_tensor(out=xtl[:, 0:2, :], in0=md[:, 2, :, :], scalar=0.5, in1=xth[:, 0:2, :].bitcast(F32),
                                         op0=ALU.mult, op1=ALU.subtract).then_inc(sem("mix_lo"), 1)

                def residual(nm, i, ahead):
                    c = chunk(nm)
                    lo_upto(end_pair(nm) + ahead)
                    dve.wait_ge(pair_used, FIRST[c] + PAIRS[c])
                    for t in range(TT):
                        dve.tensor_tensor(xres[:, t, 512 * i:512 * i + 512], PJ[BUF[c]][:, t, :],
                                          xres[:, t, 512 * i:512 * i + 512], ALU.add).then_inc(sem("resid"), 1)
                residual(f"out{l}_0", 0, 1)
                residual(f"out{l}_1", 1, RING)
                norm_scale(2 + 2 * l, xres)
                norm_lo(2 + 2 * l)

                def unit_taps(j):
                    c = chunk(f"up{l}_{j}")
                    n0 = 4 * (UNITS * l + j)
                    for tap, sh in ((1, 1), (0, 2)):
                        for i in range(4):
                            k = conv_col(l, j, i)
                            if tap == 1:
                                dve.wait_ge(sem("conv_a"), n0 + i // 2 * 2 + 2)
                            else:
                                dve.wait_ge(sem("conv_m"), n0 + i + 1)
                            dve.scalar_tensor_tensor(
                                out=acc[:, j % 2, i, sh:TOK],
                                in0=PJ[BUF[c]][:, i // 2, (i % 2) * TOK:(i % 2 + 1) * TOK - sh],
                                scalar=colv[:, k + tap:k + tap + 1], in1=acc[:, j % 2, i, sh:TOK],
                                op0=ALU.mult, op1=ALU.add).then_inc(sem("conv_m" if tap == 1 else "conv_d"), 1)

                def unit_lo(j):
                    dve.wait_ge(sem("ht_hi"), UNITS * l + j + 1)
                    dve.tensor_tensor(htl[:, 2 * j:2 * j + 2, :], gtd[:, j % 2, :, :], hth[:, 2 * j:2 * j + 2, :].bitcast(F32),
                                      ALU.subtract).then_inc(sem("ht_lo"), 1)

                for j in range(UNITS + 1):
                    if j < UNITS:
                        lo_upto(end_pair(f"up{l}_{j}") + 2)
                        unit_taps(j)
                    if j > 0:
                        unit_lo(j - 1)
                residual(f"down{l}_0", 0, 1)
                residual(f"down{l}_1", 1, RING)
            if upto == 1:
                return

            norm_scale(5, xres)
            norm_lo(5)
            lo_upto(end_pair("mq") + 1)
            aco, asi = (cs(z).rearrange("p (t d) -> p t d", t=TT) for z in ("acos", "asin"))
            for i, (g, tb) in enumerate((("qn2", aco), ("qn2", asi), ("kn2", aco), ("kn2", asi))):
                dve.tensor_tensor(tabq[:, i, :, :], tb, wide(row(g), TT), ALU.mult).then_inc(sem("tabq_ready"), 1)
            lo_upto(end_pair("bq") + 1)

            def head_norm_rope(heads, squares_, source, sq_sem, n_sq, which, temp, outs, sems_):
                w = heads * HD
                dve.wait_ge(sem(sq_sem), n_sq)
                for t in range(TT):
                    m = dve.tensor_reduce(hss[:, heads * t:heads * t + heads], squares_(t).rearrange("p (g d) -> p g d", g=heads),
                                          AX.X, ALU.add)
                    if t == 0:
                        link(m)
                m.then_inc(sem("bhss_ready"), 1)
                dve.wait_ge(sem("bhr_ready"), which + 1)
                dve.wait_ge(sem("tabq_ready"), 4)
                for t in range(TT):
                    g8 = source(t).rearrange("p (g d) -> p g d", g=heads)
                    x8 = temp(t, 0).rearrange("p (g d) -> p g d", g=heads)
                    dve.tensor_tensor(x8, g8, wide(hr[:, which, heads * t:heads * t + heads], HD, 2), ALU.mult).then_inc(sem(sems_[0]), 1)
                dve.wait_ge(sem(sems_[0]), 2)
                for t in range(TT):
                    x8 = temp(t, 0).rearrange("p (g d) -> p g d", g=heads)
                    t8 = temp(t, 1).rearrange("p (g d) -> p g d", g=heads)
                    link(dve.tensor_tensor(t8, x8, wide(tabq[:, 2 * which + 1, t, :], heads), ALU.mult))
                    link(dve.tensor_tensor(x8, x8, wide(tabq[:, 2 * which, t, :], heads), ALU.mult))
                    x16 = temp(t, 0).rearrange("p (g d) -> p g d", g=2 * heads)
                    t16 = temp(t, 1).rearrange("p (g d) -> p g d", g=2 * heads)
                    for o in outs(t, x16, t16):
                        o16, xx, tt_ = o
                        dve.tensor_tensor(o16[:, :, 0:16], xx[:, :, 0:16], tt_[:, :, 16:32], ALU.subtract).then_inc(sem(sems_[1]), 1)
                        dve.tensor_tensor(o16[:, :, 16:32], xx[:, :, 16:32], tt_[:, :, 0:16], ALU.add).then_inc(sem(sems_[1]), 1)

            head_norm_rope(BH, lambda t: sm2[:, t, 0:512], lambda t: PJ[buf("bq")][:, t, :], "bsq_ready", 2, 0,
                           lambda t, i: xn[:, t, 512 * i:512 * i + 512],
                           lambda t, x, z: [(rt[:, t, :].rearrange("p (g d) -> p g d", g=16), x, z)],
                           ("bqn_ready", "brope_ready"))
            lo_upto(end_pair("bkv") + 1)

            def twice(t, x, z):
                out_ = []
                for h in range(2):
                    for c in range(2):
                        a = 256 + P * h + HD * c
                        out_.append((xn[:, t, a:a + HD].rearrange("p (g d) -> p g d", g=2), x[:, 2 * h:2 * h + 2, :], z[:, 2 * h:2 * h + 2, :]))
                return out_

            dve.wait_ge(sem("brope_ready"), 4)
            dve.wait_ge(sem("bv_ready"), 2)
            head_norm_rope(2, lambda t: pT2[:, t, 0, :], lambda t: PJ[buf("bkv")][:, t, 0:P], "bksq_ready", 2, 1,
                           lambda t, i: xn[:, t, P * i:P * i + P], twice, ("bkn_ready", "bkrope_ready"))

            def silu(nm, th):
                i = SILU_ORDER.index(nm)
                for t in range(TT):
                    dve.wait_ge(sem("th_ready"), 2 * i + t + 1)
                    dve.scalar_tensor_tensor(out=gat[:, i, t, :], in0=th[:, t, 0:512], scalar=1.0, in1=PJ[buf(nm)][:, t, :],
                                             op0=ALU.add, op1=ALU.mult).then_inc(sem("silu_ready"), 1)

            lo_upto(end_pair("gb") + 2)
            silu("gb", sm2)
            lo_upto(end_pair("gm") + 2)
            silu("gm", sm2)

            def rot_terms(c):
                nm = A_CHUNKS[c]
                dve.wait_ge(pair_used, end_pair(nm))
                if c:
                    dve.wait_ge(sem("a_rope"), 4 * c)
                else:
                    dve.wait_ge(sem("b_tr"), 2)
                for t in range(TT):
                    g8 = PJ[buf(nm)][:, t, :].rearrange("p (g d) -> p g d", g=8)
                    for i, tb in enumerate((cosv, sinv)):
                        o8 = xn[:, t, i * 512:(i + 1) * 512].rearrange("p (g d) -> p g d", g=8)
                        dve.tensor_tensor(o8, g8, wide(tb[:, t, :], 8), ALU.mult).then_inc(sem("rot_terms"), 1)

            for c, nm in enumerate(A_CHUNKS):
                for j in range(4):
                    n = 4 * c + j
                    lo_upto(F2 + n + 3)
                    if j == 0 and 1 <= c <= 6:
                        rot_terms(c - 1)
                    for k in bm_slots(n):
                        if k < len(BM):
                            br, h, t = BM[k]
                            dve.wait_ge(sem("bm_sc"), k + 1)
                            if k >= 4:
                                dve.wait_ge(sem("bm_out"), k - 3)
                            link(dve.tensor_reduce(sx[:, k % 4, 0:1], S0[:, 0:TOK], AX.X, ALU.max))
                            dve.tensor_scalar(sx[:, k % 4, 1:2], sx[:, k % 4, 0:1], -((HD if br == "b" else MD) ** -0.5), None,
                                              ALU.mult).then_inc(sem("bm_nb"), 1)
                        if k >= 1 and k - 1 < len(BM):
                            dve.wait_ge(sem("bm_exp"), k)
                            dve.reciprocal(sx[:, (k - 1) % 4, 3:4], sx[:, (k - 1) % 4, 2:3]).then_inc(sem("bm_rl"), 1)
                        if k >= 2:
                            k2 = k - 2
                            br, h, t = BM[k2]
                            w = HD if br == "b" else MD
                            o = gat[:, "bm".index(br), t, h * w:(h + 1) * w]
                            dve.wait_ge(sem("bm_pv"), k2 + 1)
                            dve.wait_ge(sem("bm_rl"), k2 + 1)
                            dve.scalar_tensor_tensor(out=o, in0=T1[:, 0:w], scalar=sx[:, k2 % 4, 3:4], in1=o,
                                                     op0=ALU.mult, op1=ALU.mult).then_inc(sem("bm_out"), 1)
            lo_upto(F3 + 2)
            silu("ga", rt)
            dve.wait_ge(sem("ma_landed"), 16)
            for n in range(24):
                lo_upto(F3 + n + 3)
                if n % 4 == 0 and n:
                    gate_sum(dve, n // 4 - 1)
                for k in a_slots(n):
                    if k < AH * TT:
                        h, t = divmod(k, TT)
                        dve.wait_ge(sem("a_sc"), k + 1)
                        if k >= 2:
                            dve.wait_ge(sem("a_ptr"), k - 1)
                        if k >= 4:
                            dve.wait_ge(sem("a_out"), k - 3)
                        mk = ma[:, t * TOK:].rearrange("p (g n) -> p g n", n=TOK)[:, 0:3 - t:2 - t, :]
                        dve.tensor_tensor_reduce(sm2[:, k % 2, 0:512].rearrange("p (g n) -> p g n", g=2),
                                                 S0[:, :].rearrange("p (g n) -> p g n", g=2), mk, 1.0, BIG, ALU.add, ALU.max,
                                                 sx[:, k % 4, 4:5]).then_inc(sem("a_max"), 1)
                        dve.tensor_tensor_reduce(sm2[:, k % 2, 512:768], S1[:, 0:TOK], ma[:, 3 * TOK:4 * TOK], 1.0, BIG, ALU.add,
                                                 ALU.max, sx[:, k % 4, 5:6]).then_inc(sem("a_max"), 1)
                        dve.wait_ge(sem("a_max"), 2 * k + 2)
                        link(dve.tensor_tensor(sx[:, k % 4, 0:1], sx[:, k % 4, 4:5], sx[:, k % 4, 5:6], ALU.max))
                        dve.tensor_scalar(sx[:, k % 4, 1:2], sx[:, k % 4, 0:1], -(HD ** -0.5), None, ALU.mult).then_inc(sem("a_nb"), 1)
                    if k >= 1 and k - 1 < AH * TT:
                        dve.wait_ge(sem("a_exp"), k)
                        dve.reciprocal(sx[:, (k - 1) % 4, 3:4], sx[:, (k - 1) % 4, 2:3]).then_inc(sem("a_rl"), 1)
                    if k >= 2:
                        h, t = divmod(k - 2, TT)
                        o = gat[:, 2, t, h * HD:(h + 1) * HD]
                        dve.wait_ge(sem("apv_done"), k - 1)
                        dve.wait_ge(sem("a_rl"), k - 1)
                        dve.scalar_tensor_tensor(out=o, in0=PJ[1][:, 0, 0:HD], scalar=sx[:, (k - 2) % 4, 3:4], in1=o,
                                                 op0=ALU.mult, op1=ALU.mult).then_inc(sem("a_out"), 1)
            gate_sum(dve, 5)
            lo_upto(F3 + 24 + RING)
            for i in range(6):
                dve.wait_ge(sem("o_hi"), i + 1)
                dve.scalar_tensor_tensor(out=otl[:, 2 * i:2 * i + 2, :], in0=AUX[i % 4][:, :].rearrange("p (f n) -> p f n", f=2),
                                         scalar=0.5, in1=oth[:, 2 * i:2 * i + 2, :].bitcast(F32),
                                         op0=ALU.mult, op1=ALU.subtract).then_inc(sem("o_lo"), 1)
            for i, b in enumerate(BRANCH_ORDER):
                nm = "br" + b
                n = int(b[1])
                lo_upto(min(end_pair(nm) + 2, FIRST[chunk("wo0")] + 3))
                dve.wait_ge(pair_used, end_pair(nm))
                dve.wait_ge(sem("gate_ready"), 6)
                at_ = "abm".index(b[0]) * D + 512 * n
                for t in range(TT):
                    g = gt[:, t, at_:at_ + 512]
                    o = merged[:, t, 512 * n:512 * n + 512] if b[0] == "a" else g
                    dve.scalar_tensor_tensor(out=o, in0=g, scalar=1.0, in1=PJ[buf(nm)][:, t, :],
                                             op0=ALU.add, op1=ALU.mult).then_inc(sem("y_gated"), 1)
            for i in range(4):
                dve.wait_ge(sem("m_hi"), i + 1)
                dve.scalar_tensor_tensor(out=xtl[:, 2 * i:2 * i + 2, :], in0=AUX[i][:, :].rearrange("p (f n) -> p f n", f=2),
                                         scalar=0.5, in1=xth[:, 2 * i:2 * i + 2, :].bitcast(F32),
                                         op0=ALU.mult, op1=ALU.subtract).then_inc(sem("m_lo"), 1)
            for i in range(2):
                nm = f"wo{i}"
                lo_upto(end_pair(nm) + 1)
                dve.wait_ge(sem("ssq_ready"), 4 * 6 + 2 * i + 2)
                for t in range(TT):
                    dve.tensor_copy(xn[:, t, 512 * i:512 * i + 512], PJ[buf(nm)][:, t, :]).then_inc(sem("wo_ev"), 1)
            dve.wait_ge(sem("rstd_ready"), 7)
            dve.wait_ge(sem("gpost_landed"), 16)
            dve.wait_ge(sem("wo_ev"), 4)
            for t in range(TT):
                link(dve.scalar_tensor_tensor(out=xn[:, t, :], in0=xn[:, t, :], scalar=rstd[:, 6, t:t + 1], in1=gpost[:, :],
                                              op0=ALU.mult, op1=ALU.mult))
                dve.tensor_tensor(xn[:, t, :], xn[:, t, :], xres[:, t, :], ALU.add).then_inc(sem("y_ready"), 1)

def conv_col(l, j, i):
    tile = 2 * j + i % 2 + (FT if i >= 2 else 0)
    return COL["conv"][0] + (l * 2 * FT + tile) * 4


def rope_table(pos, half, width):
    inv = 10000.0 ** (-np.arange(half, dtype=np.float64) / half)
    a = pos[:, None] * inv[None, :]
    a = np.concatenate([a, a], axis=1)
    return np.cos(a), np.sin(a)


def by_partition(a):
    return np.ascontiguousarray(a.reshape(TT, P, -1).transpose(1, 0, 2).reshape(P, -1))


def constants():
    pos = np.arange(TOK)
    cos, sin = rope_table(pos, 32, 64)
    rc, rs = rope_table(pos // 64, 16, 32)
    cc, cs_ = rope_table(pos % 64, 16, 32)
    own = pos[:, None] // 64
    diff = np.where(pos[None, :] // 64 <= own, 0.0, NEG)
    parts = [np.eye(P), by_partition(cos), by_partition(sin), by_partition(np.concatenate([rc, cc], 1)),
             by_partition(np.concatenate([rs, cs_], 1)), diff[0:128, 0:128], diff[128:256, 0:256]]
    return np.concatenate(parts, axis=1).astype(np.float32)


def window_masks():
    q, k = np.arange(TOK)[:, None], np.arange(TOK)[None, :]
    near = np.abs(q - k) <= 64
    parts = [near[0:P], near[P:]] + [((q - k) % d == 0)[0:P] for d in (4, 16)]
    return np.where(np.concatenate(parts, axis=1), 0.0, NEG).astype(np.float32)


def layout(i):
    def cut(w, n):
        return w.reshape(w.shape[0] // P, P, w.shape[1])

    tiles = {}
    for l in range(LAYERS):
        w = i["w_in"][l]
        at = 0
        for nm, n in (("ssm_u", 256), ("gmlp", 512), ("q", 512), ("k", 512), ("v", 512)):
            tiles[f"{nm}{l}"] = w[:, at:at + n]
            at += n
        for j in range(2):
            tiles[f"out{l}_{j}"] = i["w_out"][l][:, 512 * j:512 * j + 512]
            tiles[f"down{l}_{j}"] = i["w_down"][l][:, 512 * j:512 * j + 512]
        for j in range(UNITS):
            up = i["w_up"][l]
            tiles[f"up{l}_{j}"] = np.concatenate([up[:, 256 * j:256 * j + 256], up[:, FF + 256 * j:FF + 256 * j + 256]], 1)
    w = i["w_in_2"][0]
    at = 0
    for nm, n in [(f"a{c}{g}", 512) for c in "qkv" for g in range(NG)] + \
            [("bq", 512), ("bkv", 256), ("mq", 512), ("ga", 512), ("gb", 512), ("gm", 512)] + [(f"mg{j}", 512) for j in range(6)]:
        tiles[nm] = w[:, at:at + n]
        at += n
    tiles["km"], tiles["vm"] = i["w_mem_kv_2"][0][:, 0:512], i["w_mem_kv_2"][0][:, 512:1024]
    for j in range(2):
        for b in "abm":
            tiles[f"br{b}{j}"] = i[f"w_br_{b}_2"][0][:, 512 * j:512 * j + 512]
        tiles[f"wo{j}"] = i["w_out_2"][0][:, 512 * j:512 * j + 512]
    weights = np.empty((NPAIRS, P, 1024), np.float32)
    for (nm, k, n), first, pairs in zip(CHUNKS, FIRST, PAIRS):
        per = 1024 // n
        weights[first:first + pairs] = tiles[nm].reshape(pairs, per, P, n).transpose(0, 2, 1, 3).reshape(pairs, P, 1024)

    cols = np.zeros((P, NCOL), np.float32)

    def put(name, a, at=0):
        a = a.reshape(-1, P).T
        cols[:, COL[name][0] + at:COL[name][0] + at + a.shape[1]] = a

    put("are", i["ssm_a_re"])
    put("aim", i["ssm_a_im"])
    put("ldt", np.repeat(i["ssm_log_dt"].reshape(-1), STATE))
    put("gattn", i["attn_norm_g"])
    put("gffn", i["ffn_norm_g"])
    put("dskip", i["ssm_d"])
    put("bglu", i["ssm_b_glu"])
    put("bs", i["gmlp_b_s"])
    put("gpre", i["g_pre_2"])
    put("gmem", i["g_mem_2"])
    conv = np.concatenate([i["conv_w"], i["conv_b"][:, None, :]], axis=1)
    put("conv", conv.reshape(LAYERS, 4, 2 * FT, P).transpose(0, 2, 1, 3))
    rows = np.zeros((1, NROW), np.float32)
    for name, src in (("vg", "gmlp_v_g"), ("qg", "q_norm_g"), ("kg", "k_norm_g"), ("sub", "subln_g"),
                      ("qn2", "q_norm_2"), ("kn2", "k_norm_2")):
        a, b = ROW[name]
        rows[0, a:b] = i[src].reshape(-1)
    bexp = np.zeros((LAYERS, P, 2, ST, P), np.float32)
    cexp = np.zeros((LAYERS, P, 2, ST, P), np.float32)
    for c, (b, m) in enumerate((("ssm_b_re", "ssm_c_re"), ("ssm_b_im", "ssm_c_im"))):
        for g in range(GROUPS):
            s, half, ch = g // 2, (g % 2) * STATE, (g % 8) * GCH
            bexp[:, ch:ch + GCH, c, s, half:half + STATE] = i[b][:, g].transpose(0, 2, 1)
            cexp[:, half:half + STATE, c, s, ch:ch + GCH] = i[m][:, g].transpose(0, 2, 1)
    return {
        "weights": weights, "x": i["x"].reshape(TOK, D), "mem": i["mem_2"].reshape(TOK, D), "cols": cols, "rows": rows,
        "lams": np.concatenate([i[f"lambda_{z}"].reshape(1, -1) for z in ("q1", "k1", "q2", "k2")], axis=1),
        "bmerge": np.concatenate([i["b_merge_2"].reshape(1, -1), i["g_post_2"].reshape(1, -1)], axis=1),
        "consts": constants(), "amask": window_masks(), "bexp": bexp, "cexp": cexp,
        "wst": np.ascontiguousarray(i["gmlp_w_s"].transpose(0, 3, 1, 2)),
        "wglu": np.ascontiguousarray(i["ssm_w_glu"].reshape(LAYERS, 2, P, 256).transpose(0, 2, 1, 3)),
    }


def kernel(**inputs):
    import concourse.bacc as bacc
    from concourse.bass_utils import run_bass_kernel_spmd

    nc = bacc.Bacc("TRN2", target_bir_lowering=False, num_devices=1)
    arrays = {f"{k}_in": np.ascontiguousarray(v) for k, v in layout({k: np.asarray(v) for k, v in inputs.items()}).items()}
    args = {k[:-3]: nc.dram_tensor(k, a.shape, mybir.dt.from_np(a.dtype), kind="ExternalInput").ap() for k, a in arrays.items()}
    out = nc.dram_tensor("y_out", (TOK, D), F32, kind="ExternalOutput").ap()
    build(nc, out=out, **args)
    r = run_bass_kernel_spmd(nc, [arrays], core_ids=[0])
    return r.results[0]["y_out"].reshape(1, TOK, D)
```

```python
from contextlib import ExitStack
import math

import numpy as np
import concourse.bass as bass
from concourse import mybir

P = 128
TOK, TT = 256, 2
D, KD = 1024, 8
LAYERS = 2
GROUPS, GCH, STATE = 16, 16, 64
ST = GROUPS * STATE // P
QKD, VD, DH = 64, 128, 4
FF = 2816
FT = FF // P
UNITS = FT // 2
HD, AH, NG, BH, MH, MD = 64, 8, 3, 8, 4, 128
EPS = 1e-6
NEG = -1e30
BIG = -3.0e38
RAW, RING = 5, 5

F32, F32R = mybir.dt.float32, mybir.dt.float32r
ALU, ACT, AX = mybir.AluOpType, mybir.ActivationFunctionType, mybir.AxisListType
LAMBDA_INIT = [0.8 - 0.6 * math.exp(-0.3 * l) for l in range(LAYERS)]

CHUNKS = [("km", 8, 512), ("vm", 8, 512)]
for _l in range(LAYERS):
    CHUNKS += [(f"ssm_u{_l}", 8, 256), (f"q{_l}", 8, 512), (f"k{_l}", 8, 512), (f"v{_l}", 8, 512),
               (f"gmlp{_l}", 8, 512), (f"out{_l}_0", 8, 512), (f"out{_l}_1", 8, 512)]
    CHUNKS += [(f"up{_l}_{j}", 8, 512) for j in range(UNITS)]
    CHUNKS += [(f"down{_l}_0", FT, 512), (f"down{_l}_1", FT, 512)]
CHUNKS += [("mq", 8, 512), ("bq", 8, 512), ("bkv", 8, 256), ("gb", 8, 512), ("gm", 8, 512)]
CHUNKS += [(f"a{w}{g}", 8, 512) for w in "qkv" for g in range(NG)] + [("ga", 8, 512)]
CHUNKS += [(f"mg{i}", 8, 512) for i in range(6)]
CHUNKS += [(f"br{b}{n}", 4, 512) for n in range(2) for b in "abm"] + [("wo0", 8, 512), ("wo1", 8, 512)]
NAMES = [c[0] for c in CHUNKS]
PAIRS = [k * n // 1024 for _, k, n in CHUNKS]
FIRST = [sum(PAIRS[:i]) for i in range(len(CHUNKS))]
NPAIRS = sum(PAIRS)


def chunk(name):
    return NAMES.index(name)


def end_pair(name):
    c = chunk(name)
    return FIRST[c] + PAIRS[c]


BRANCH_ORDER = [b + str(n) for n in range(2) for b in "abm"]
A_CHUNKS = [f"a{w}{g}" for w in "qkv" for g in range(NG)] + ["ga"]
SILU_ORDER = ["gb", "gm", "ga"]
EMPTIED = {"km": [("mem_ev", 2)], "vm": [("mem_ev", 4)], "mq": [("mq_ev", 2)], "bq": [("bqn_ready", 2)],
           "bkv": [("bkn_ready", 2), ("bv_ready", 2)]}
for _l in range(LAYERS):
    EMPTIED[f"ssm_u{_l}"] = [("u_ready", _l + 1)]
    EMPTIED[f"q{_l}"] = [("qn_ready", 4 * _l + 2)]
    EMPTIED[f"k{_l}"] = [("qn_ready", 4 * _l + 4)]
    EMPTIED[f"v{_l}"] = [("v_ready", 2 * _l + 2)]
    EMPTIED[f"gmlp{_l}"] = [("vn_ready", 2 * _l + 2), ("ug_ready", 2 * _l + 2)]
    for _n in range(2):
        EMPTIED[f"out{_l}_{_n}"] = [("resid", 8 * _l + 2 * _n + 2)]
        EMPTIED[f"down{_l}_{_n}"] = [("resid", 8 * _l + 4 + 2 * _n + 2)]
        EMPTIED[f"wo{_n}"] = [("wo_ev", 2 * _n + 2)]
    for _j in range(UNITS):
        EMPTIED[f"up{_l}_{_j}"] = [("conv_d", 4 * (UNITS * _l + _j + 1))]
for _n in range(6):
    EMPTIED[A_CHUNKS[_n]] = [("rot_terms", 4 * _n + 4)]
    EMPTIED[f"mg{_n}"] = [("gate_sum", 2 * _n + 2)]
    EMPTIED["br" + BRANCH_ORDER[_n]] = [("y_gated", 2 * _n + 2)]
for _n in range(NG):
    EMPTIED[f"av{_n}"] = [("av_ready", 2 * _n + 2)]
    EMPTIED[SILU_ORDER[_n]] = [("silu_ready", 2 * _n + 2)]
BUF = []
for _n in NAMES:
    BUF.append(1 - BUF[-1] if BUF else 0)


def buf(name):
    return BUF[chunk(name)]


def spans(*items):
    at, out = 0, {}
    for name, n in items:
        out[name] = (at, at + n)
        at += n
    return out, at


COL, NCOL = spans(("are", 16), ("aim", 16), ("ldt", 16), ("gattn", 16), ("gffn", 16), ("dskip", 4),
                  ("bglu", 4), ("bs", 8), ("gpre", 8), ("gmem", 8), ("conv", LAYERS * 2 * FT * 4))
ROW, NROW = spans(("vg", 512), ("qg", 128), ("kg", 128), ("sub", 256), ("qn2", 64), ("kn2", 64))
LAM, NLAM = spans(("lq1", 128), ("lk1", 128), ("lq2", 128), ("lk2", 128))
CST, NCST = spans(("ident", 128), ("cos", 128), ("sin", 128), ("acos", 128), ("asin", 128),
                  ("mdiff", 384))


def build(nc, weights, x, mem, cols, rows, lams, bmerge, consts, amask, bexp, cexp, wst, wglu, out, upto=99):
    with ExitStack() as ctx:
        def sbt(stack, name, shape, dt=F32):
            return stack.enter_context(nc.sbuf_tensor(name, shape, dt))

        sems = {}

        def sem(name):
            if name not in sems:
                sems[name] = ctx.enter_context(nc.semaphore(name))
            return sems[name]

        raw = sbt(ctx, "raw", [P, RAW, 1024])
        whi = sbt(ctx, "whi", [P, RING, 1024], F32R)
        wlo = sbt(ctx, "wlo", [P, RING, 1024], F32R)
        xres = sbt(ctx, "xres", [P, TT, D])
        xn = sbt(ctx, "xn", [P, TT, D])
        xth = sbt(ctx, "xth", [P, KD, TOK], F32R)
        xtl = sbt(ctx, "xtl", [P, KD, TOK], F32R)
        kmT = sbt(ctx, "kmT", [P, MH, TOK])
        vm = sbt(ctx, "vm", [P, TT, 512])
        colv = sbt(ctx, "colv", [P, NCOL])
        rowv = sbt(ctx, "rowv", [P, NROW])
        cst = sbt(ctx, "cst", [P, NCST])
        ssq = sbt(ctx, "ssq", [P, 8, 4])
        ssm1 = sbt(ctx, "ssm1", [P, 8, 2])
        rstd = sbt(ctx, "rstd", [P, 8, 2])
        mhalf = sbt(ctx, "mhalf", [P, 16])
        sqs = sbt(ctx, "sqs", [P, 512], mybir.dt.bfloat16)
        gss = sbt(ctx, "gss", [P, LAYERS, TT])
        gr = sbt(ctx, "gr", [P, LAYERS, TT])
        hss = sbt(ctx, "hss", [P, 16])
        hr = sbt(ctx, "hr", [P, 2, 16])
        sqs2 = sbt(ctx, "sqs2", [P, 64])
        hb = sbt(ctx, "hb", [P, 4])
        nlam = sbt(ctx, "nlam", [P, LAYERS])
        lamv = sbt(ctx, "lamv", [P, 8])

        def col(name, i=0, n=None):
            a, b = COL[name]
            return colv[:, a + i:(a + i + n) if n else b]

        def row(name, i=0, n=None):
            a, b = ROW[name]
            return rowv[:, a + i:(a + i + n) if n else b]

        def cs(name):
            a, b = CST[name]
            return cst[:, a:b]

        ident = cs("ident")

        def wide(ap, n, dim=1):
            a = ap.unsqueeze(dim)
            shape = list(a.shape)
            shape[dim] = n
            return a.to_broadcast(shape)

        one = ExitStack()
        ctx.enter_context(one)
        bex = sbt(one, "bex", [P, 2, 2, P])
        cex = sbt(one, "cex", [P, 2, ST, 32])
        sp_ = sbt(one, "sp_", [P, 24, 16])
        ropeq = sbt(one, "ropeq", [P, 4, TT, QKD])
        identb = sbt(one, "identb", [P, P], mybir.dt.bfloat16)
        maskb = sbt(one, "maskb", [P, TT, 512], mybir.dt.bfloat16)
        tab = sbt(one, "tab", [P, 2, ST, TOK])
        wglus = sbt(one, "wglus", [P, 2, 256])
        wsts = sbt(one, "wsts", [P, 4, P])
        pw = sbt(one, "pw", [P, 5, ST])
        ta = sbt(one, "ta", [P, 2, ST, 16])
        tb = sbt(one, "tb", [P, 2, ST, 16])
        tq = sbt(one, "tq", [P, 2, ST, 8])
        mix = ExitStack()
        one.enter_context(mix)
        bu = sbt(mix, "bu", [P, ST, 2, TOK])
        mp = sbt(mix, "mp", [P, 2, 2, TOK])
        md = sbt(mix, "md", [P, 3, 2, TOK])
        uT = sbt(mix, "uT", [P, 2, TOK])
        qT = sbt(mix, "qT", [P, DH, TOK])
        kT = sbt(mix, "kT", [P, DH, TOK])
        v_sb = sbt(mix, "v_sb", [P, TT, 512])
        qn = sbt(mix, "qn", [P, TT, 512])
        hsq = sbt(mix, "hsq", [P, TT, 512])
        ug = sbt(mix, "ug", [P, TT, 256])
        sm = sbt(mix, "sm", [P, 2, 2, 512])
        pT = sbt(mix, "pT", [P, 2, 4, P])
        st_ = sbt(mix, "st_", [P, 3, 8, 4])
        mix.close()
        ffs = ExitStack()
        one.enter_context(ffs)
        hth = sbt(ffs, "hth", [P, FT, TOK], F32R)
        htl = sbt(ffs, "htl", [P, FT, TOK], F32R)
        acc = sbt(ffs, "acc", [P, 2, 4, TOK])
        gtd = sbt(ffs, "gtd", [P, 2, 2, TOK])
        ffs.close()
        one.close()

        two = ExitStack()
        ctx.enter_context(two)
        sm2 = sbt(two, "sm2", [P, 2, NG * TOK])
        pT2 = sbt(two, "pT2", [P, 2, 2 * NG, P])
        rt = sbt(two, "rt", [P, TT, 512])
        brow = rt
        gat = sbt(two, "gat", [P, 3, TT, 512])
        ma = sbt(two, "ma", [P, 4 * TOK])
        sx = sbt(two, "sx", [P, 4, 8])
        tabq = sbt(two, "tabq", [P, 4, TT, HD])
        bm = ExitStack()
        two.enter_context(bm)
        bqT = sbt(bm, "bqT", [P, 4, TOK])
        bkT = sbt(bm, "bkT", [P, 2, TOK])
        bv = sbt(bm, "bv", [P, TT, P])
        mqT = sbt(bm, "mqT", [P, MH, TOK])
        bm.close()
        gt = sbt(two, "gt", [P, TT, 3 * D])
        att = ExitStack()
        two.enter_context(att)
        aqT = sbt(att, "aqT", [P, 2, NG, 4, TOK])
        va = sbt(att, "va", [P, NG, TT, 512])
        att.close()
        oth = sbt(two, "oth", [P, 12, TOK], F32R)
        otl = sbt(two, "otl", [P, 12, TOK], F32R)
        merged = sbt(two, "merged", [P, TT, D])
        gpost = sbt(two, "gpost", [P, D])
        two.close()

        PJ = [ctx.enter_context(nc.psum_tensor(f"PJ{i}", [P, TT, 512], F32)) for i in range(2)]
        S0, S1, T0, T1 = (ctx.enter_context(nc.psum_tensor(n, [P, 512], F32)) for n in ("S0", "S1", "T0", "T1"))
        AUX = [S0, S1, T0, T1]
        OBANKS = [S0, T0, T1, S1]

        raw_landed = [sem(f"raw_landed{i}") for i in range(RAW)]
        hi_ready, lo_ready, pair_used = sem("hi_ready"), sem("lo_ready"), sem("pair_used")
        block = ctx.enter_context(nc.Block())

        NORM_GAIN = [("gmem", 0), ("gattn", 0), ("gffn", 0), ("gattn", 8), ("gffn", 8), ("gpre", 0)]

        def md_vn(h):
            return xn[:, :, 768 + h * 64:768 + (h + 1) * 64]

        def md_g(k):
            return md[:, 0, k, :]

        def merge_tanh(act, i):
            act.wait_ge(sem("gate_sum"), 2 * i + 2)
            act.activation(gt[:, :, 512 * i:512 * i + 512], gt[:, :, 512 * i:512 * i + 512], ACT.Tanh,
                           scale=0.5).then_inc(sem("gate_ready"), 1)

        def gate_sum(dve, i):
            nm = f"mg{i}"
            dve.wait_ge(pair_used, end_pair(nm))
            dve.wait_ge(sem(f"brow_landed{i % 2}"), 16 * (i // 2 + 1))
            for t in range(TT):
                dve.tensor_tensor(gt[:, t, 512 * i:512 * i + 512], PJ[buf(nm)][:, t, :], brow[:, i % 2, :],
                                  ALU.add).then_inc(sem("gate_sum"), 1)

        def table_base(pool, link, l):
            lo8 = slice(8 * l, 8 * l + 8)
            link(pool.tensor_copy(pw[:, 0, :], sp_[:, 8, lo8]))
            link(pool.tensor_copy(pw[:, 1, :], sp_[:, 6, lo8]))

        def table_factor(pool, link, tt_):
            link(pool.memset(tt_[:, 0, :, 0:1], 1.0))
            link(pool.memset(tt_[:, 1, :, 0:1], 0.0))
            n = 1
            while n < 16:
                c, s_ = tt_[:, 0, :, 0:n], tt_[:, 1, :, 0:n]
                C, S = wide(pw[:, 0, :], n, 2), wide(pw[:, 1, :], n, 2)
                for u, w, op, o in ((C, S, ALU.subtract, 0), (S, C, ALU.add, 1)):
                    link(pool.tensor_tensor(tq[:, 0, :, 0:n], c, u, ALU.mult))
                    link(pool.tensor_tensor(tq[:, 1, :, 0:n], s_, w, ALU.mult))
                    link(pool.tensor_tensor(tt_[:, o, :, n:2 * n], tq[:, 0, :, 0:n], tq[:, 1, :, 0:n], op))
                link(pool.tensor_tensor(pw[:, 2, :], pw[:, 0, :], pw[:, 0, :], ALU.mult))
                link(pool.tensor_tensor(pw[:, 3, :], pw[:, 1, :], pw[:, 1, :], ALU.mult))
                link(pool.tensor_tensor(pw[:, 4, :], pw[:, 0, :], pw[:, 1, :], ALU.mult))
                link(pool.tensor_tensor(pw[:, 0, :], pw[:, 2, :], pw[:, 3, :], ALU.subtract))
                link(pool.tensor_tensor(pw[:, 1, :], pw[:, 4, :], pw[:, 4, :], ALU.add))
                n *= 2

        def table_product(pool, link, l, s, tmp):
            av = [wide(ta[:, i, s:s + 2, :], 16, 3) for i in range(2)]
            bv_ = [wide(tb[:, i, s:s + 2, :], 16, 2) for i in range(2)]
            o = [tab[:, i, s:s + 2, :].rearrange("p s (a b) -> p s a b", a=16) for i in range(2)]
            for k, first, second, op in ((0, (av[0], bv_[0]), (av[1], bv_[1]), ALU.subtract),
                                         (1, (av[1], bv_[0]), (av[0], bv_[1]), ALU.add)):
                pool.tensor_tensor(o[k], *first, ALU.mult).then_inc(sem("tab_p"), 1)
                pool.tensor_tensor(tmp[:, k], *second, ALU.mult).then_inc(sem("tab_p"), 1)
                pool.wait_ge(sem("tab_p"), 16 * l + 2 * s + 2 * k + 2)
                pool.tensor_tensor(o[k], o[k], tmp[:, k], op).then_inc(sem("tab_ready"), 1)
            pool.wait_ge(sem("tab_ready"), 8 * l + s + 2)

        def fold_coefficient(eng, link, l, cf):
            eng.wait_ge(sem("cex_landed"), 16 * (l + 1))
            cr, ci, nci, ncr = (wide(sp_[:, r, 8 * l:8 * l + 8], 32, 2) for r in (9, 10, 11, 12))
            re, im = cex[:, 0, :, :], cex[:, 1, :, :]
            for o, (i_, k) in enumerate(((re, cr), (im, nci), (re, nci), (im, ncr))):
                link(eng.tensor_tensor(cf[:, o, :, :], i_, k, ALU.mult))
            eng.tensor_tensor(re, cf[:, 0, :, :], cf[:, 1, :, :], ALU.add).then_inc(sem("cex_ready"), 1)
            eng.tensor_tensor(im, cf[:, 2, :, :], cf[:, 3, :, :], ALU.add).then_inc(sem("cex_ready"), 1)

        @block.sync
        def _(sp):
            def small(dst, src, s):
                sp.dma_start(dst, src).then_inc(sem(s), 16)

            for t in range(TT):
                small(xn[:, t, :], mem[t * P:(t + 1) * P, :], f"mem_landed{t}")
            small(cst[:], consts, "cst_landed")
            small(colv[:], cols, "col_landed")
            for p in range(NPAIRS):
                if p >= RAW:
                    sp.wait_ge(lo_ready, p - RAW + 1)
                sp.dma_start(raw[:, p % RAW, :], weights[p]).then_inc(raw_landed[p % RAW], 16)
                if p == 2:
                    small(xres[:], x.rearrange("(t p) d -> p t d", p=P), "x_landed")
                if p == 3:
                    small(rowv[:], rows.to_broadcast([P, NROW]), "row_landed")
                    small(bu[:, 0, :, :].rearrange("p c t -> p (c t)"), lams.to_broadcast([P, NLAM]), "lam_landed")
                    small(bex[:], bexp[0], "bex_landed")
                    small(cex[:], cexp[0], "cex_landed")
                    small(wsts[:], wst[0], "wst_landed")
                    small(wglus[:], wglu[0], "wglu_landed")
                if p == FIRST[chunk("up0_0")] + 6:
                    for s in ("y_done", "glu_done", "sgu_done"):
                        sp.wait_ge(sem(s), 1)
                    small(bex[:], bexp[1], "bex_landed")
                    small(cex[:], cexp[1], "cex_landed")
                    small(wsts[:], wst[1], "wst_landed")
                    small(wglus[:], wglu[1], "wglu_landed")
                if p == FIRST[chunk("gb")]:
                    sp.wait_ge(pair_used, end_pair("down1_1"))
                    small(ma[:], amask, "ma_landed")
                for i in range(6):
                    if p == (FIRST[chunk("mg1")] + 3 if i < 2 else FIRST[chunk(f"mg{i}")] + 2):
                        if i >= 2:
                            sp.wait_ge(sem("gate_sum"), 2 * i - 2)
                        else:
                            sp.wait_ge(sem("silu_ready"), 6)
                        small(brow[:, i % 2, :], bmerge[:, 512 * i:512 * i + 512].to_broadcast([P, 512]), f"brow_landed{i % 2}")
                if p + 1 == NPAIRS or (upto == 1 and p + 1 == FIRST[chunk("mq")]):
                    break
            if upto == 1:
                sp.wait_ge(sem("resid"), 4 * 2 * LAYERS)
                sp.dma_start(out.rearrange("(t p) d -> p t d", p=P), xres[:]).then_inc(sem("out_stored"), 16)
                sp.wait_ge(sem("out_stored"), 16)
                return
            sp.wait_ge(sem("apv_done"), 16)
            small(gpost[:], bmerge[:, 3 * D:4 * D].to_broadcast([P, D]), "gpost_landed")
            for t in range(TT):
                sp.wait_ge(sem("y_ready"), t + 1)
                sp.dma_start(out[t * P:(t + 1) * P, :], xn[:, t, :]).then_inc(sem("out_stored"), 16)
            sp.wait_ge(sem("out_stored"), 32)

        POOL_POST = (5, 7)

        def post_rotate(eng, l, s, products):
            mine = [x for x in range(ST) if (x in POOL_POST) == (s in POOL_POST)]
            name = "state_ready_pool" if s in POOL_POST else "state_ready"
            before = len(mine) * l + mine.index(s)
            if before:
                eng.wait_ge(sem(name), 2 * before)
            cc, ss = wide(tab[:, 0, s, :], 2), wide(tab[:, 1, s, :], 2)
            eng.tensor_tensor(products[:, 0, :, :], bu[:, s, :, :], cc, ALU.mult).then_inc(sem(name + "_p"), 1)
            eng.tensor_tensor(products[:, 1, :, :], bu[:, s, :, :], ss, ALU.mult).then_inc(sem(name + "_p"), 1)
            eng.wait_ge(sem(name + "_p"), 2 * before + 2)
            eng.tensor_tensor(bu[:, s, 0, :], products[:, 0, 0, :], products[:, 1, 1, :], ALU.subtract).then_inc(sem(name), 1)
            eng.tensor_tensor(bu[:, s, 1, :], products[:, 0, 1, :], products[:, 1, 0, :], ALU.add).then_inc(sem(name), 1)

        DB = [(0, (0, 1, 2, 3)), (1, (0, 1)), (1, (2, 3))]
        DBANKS = [(S0, S1), (T0, T1), (S0, S1)]
        EXPS = [8, 12, 16]

        BM = [("b", h, t) for h in range(BH) for t in range(TT)] + [("m", h, t) for h in range(MH) for t in range(TT)]
        F2, F3 = FIRST[chunk("aq0")], FIRST[chunk("mg0")]

        def bm_slots(n):
            return [k for k in range(len(BM) + 2) if 1 + 3 * k // 2 == n]

        def a_slots(n):
            return [k for k in range(AH * TT + 2) if 4 * k // 3 == n]

        @block.tensor
        def _(pe):
            def pair_products(p, kt0, banks, fm, xh, xl, cw, last_k):
                r = p % RING
                n_k = 1024 // cw
                pe.wait_ge(hi_ready, p + 1)
                pe.wait_ge(lo_ready, p + 1)
                for kk in range(n_k):
                    k = kt0 + kk
                    wh, wl = whi[:, r, kk * cw:(kk + 1) * cw], wlo[:, r, kk * cw:(kk + 1) * cw]
                    if fm:
                        for f in range(cw // P):
                            o = banks[f // 2][:, (f % 2) * TOK:(f % 2 + 1) * TOK]
                            a, b = wh[:, f * P:(f + 1) * P], wl[:, f * P:(f + 1) * P]
                            pe.matmul(o, a, xh[:, k, :], start=(k == 0 and f % 2 == 0), stop=False, skip_group_check=True)
                            pe.matmul(o, a, xl[:, k, :], start=False, stop=False, skip_group_check=True)
                            m = pe.matmul(o, b, xh[:, k, :], start=False, stop=(k == last_k), skip_group_check=True)
                    else:
                        for t in range(TT):
                            o = banks[t][:, 0:cw]
                            h, lw = xh[:, k, t * P:(t + 1) * P], xl[:, k, t * P:(t + 1) * P]
                            pe.matmul(o, h, wh, start=(k == 0), stop=False, skip_group_check=True)
                            pe.matmul(o, h, wl, start=False, stop=False, skip_group_check=True)
                            m = pe.matmul(o, lw, wh, start=False, stop=(k == last_k), skip_group_check=True)
                return m

            def project(name, fm=False, xh=xth, xl=xtl, ready=None, pairs=None):
                c = chunk(name)
                _, n_k, cw = CHUNKS[c]
                banks = [PJ[BUF[c]][:, 0, :], PJ[BUF[c]][:, 1, :]]
                before = [i for i in range(c) if BUF[i] == BUF[c]]
                per = 1024 // cw
                for j in (range(PAIRS[c]) if pairs is None else pairs):
                    if j == 0 and before:
                        for s, n in EMPTIED[NAMES[before[-1]]]:
                            pe.wait_ge(sem(s), n)
                    if ready:
                        pe.wait_ge(ready[0], ready[1] + (j + 1) * ready[2])
                    m = pair_products(FIRST[c] + j, j * per, banks, fm, xh, xl, cw, n_k - 1)
                    m.then_inc(pair_used, 1)

            def norm_transposes(n):
                if n == 0:
                    pe.wait_ge(sem("cst_landed"), 16)
                if n >= 1:
                    pe.wait_ge(sem("xt_lo"), 8 * n)
                if n >= 2:
                    aux_free_before_norm(n)
                for t in range(TT):
                    pe.wait_ge(sem("xn_ready"), 2 * n + t + 1)
                    for f in range(KD):
                        o = AUX[f // 2][:, (f % 2) * TOK + t * P:(f % 2) * TOK + (t + 1) * P]
                        m = pe.transpose(o, xn[:, t, f * P:(f + 1) * P], ident)
                        if t == 1 and f % 2 == 1:
                            m.then_inc(sem("xt_tr"), 1)

            def aux_free_before_norm(n):
                if n in (2, 4):
                    l = n // 2 - 1
                    pe.wait_ge(sem("mix_lo"), 4 * (l + 1))

            norm_transposes(0)
            project("km", fm=True, ready=(sem("xt_lo"), 0, 2))
            project("vm")
            norm_transposes(1)

            for l in range(LAYERS):
                if l > 0:
                    norm_transposes(1 + 2 * l)
                xt = (sem("xt_lo"), 8 * (1 + 2 * l), 4)
                project(f"ssm_u{l}", fm=True, ready=xt)
                pe.wait_ge(sem("bex_landed"), 16 * (l + 1))
                pe.wait_ge(sem("u_ready"), l + 1)
                pe.wait_ge(sem("xt_lo"), 8 * (2 + 2 * l))
                for s in range(ST):
                    if s >= 4:
                        pe.wait_ge(sem("bu_ready"), ST * l + s - 3)
                    q = slice(32 * (s % 4), 32 * (s % 4) + 32)
                    for c in range(2):
                        m = pe.matmul(AUX[s % 4][:, c * TOK:(c + 1) * TOK], bex[q, c, s // 4, :], uT[q, s // 4, :],
                                      start=(c == 0), stop=True, skip_group_check=True)
                    m.then_inc(sem("bu_done"), 1)
                project(f"q{l}")
                project(f"k{l}")

                def head_transposes(which, banks, n):
                    pe.wait_ge(sem("bu_ready"), ST * (l + 1))
                    pe.wait_ge(sem("rope_ready"), 4 * (2 * l + which + 1))
                    for h in range(DH):
                        for t in range(TT):
                            o = banks[h // 2][:, (h % 2) * TOK + t * P:(h % 2) * TOK + (t + 1) * P]
                            m = pe.transpose(o, xn[:, t, which * 512 + h * P:which * 512 + (h + 1) * P], ident)
                    m.then_inc(sem("qk_tr"), 1)

                head_transposes(0, (S0, S1), 0)
                project(f"v{l}")
                head_transposes(1, (T0, T1), 1)
                project(f"gmlp{l}", pairs=[0, 1])

                def scores(b):
                    t, heads = DB[b]
                    n = P * (t + 1)
                    if b == 2:
                        pe.wait_ge(sem("da_exp"), 16 * l + EXPS[0])
                    for c, bank in enumerate(DBANKS[b]):
                        pe.matmul(bank[:, :], identb[:, :], maskb[:, t, :], start=True, stop=False, skip_group_check=True)
                    for i, h in enumerate(heads):
                        for c, bank in enumerate(DBANKS[b]):
                            m = pe.matmul(bank[:, i * n:(i + 1) * n], qT[c * QKD:(c + 1) * QKD, h, t * P:(t + 1) * P],
                                          kT[c * QKD:(c + 1) * QKD, h, 0:n], start=False, stop=True, skip_group_check=True)
                    m.then_inc(sem("da_sc"), 1)

                def prob_transposes(b):
                    pe.wait_ge(sem("da_w"), 3 * l + b + 1)
                    if b == 2:
                        pe.wait_ge(sem("da_pt"), 3 * l + 1)
                    for i in range(4):
                        m = pe.transpose(PJ[buf(f"v{l}")][:, b % 2, i * P:(i + 1) * P], sm[:, b % 2, 1, i * P:(i + 1) * P], ident)
                    m.then_inc(sem("da_tr"), 1)

                def values(b):
                    t, heads = DB[b]
                    pe.wait_ge(sem("da_pt"), 3 * l + b + 1)
                    for i, h in enumerate(heads):
                        for k in range(t + 1):
                            m = pe.matmul(PJ[buf(f"gmlp{l}")][:, t, h * VD:(h + 1) * VD], pT[:, b % 2, i * (t + 1) + k, :],
                                          v_sb[:, k, h * VD:(h + 1) * VD], start=(k == 0), stop=(k == t), skip_group_check=True)
                    m.then_inc(sem("da_pv"), 1)

                pe.wait_ge(sem("qk_ev"), 4 * (l + 1))
                pe.wait_ge(sem("v_ready"), 2 * (l + 1))
                if l == 0:
                    pe.wait_ge(sem("maskb_ready"), 3)
                scores(0)
                scores(1)
                project(f"gmlp{l}", pairs=[2, 3])
                scores(2)
                prob_transposes(0)
                for s, n in EMPTIED[f"gmlp{l}"]:
                    pe.wait_ge(sem(s), n)
                values(0)
                prob_transposes(1)
                values(1)
                prob_transposes(2)
                values(2)
                pe.wait_ge(sem("vn_ready"), 2 * (l + 1))
                pe.wait_ge(sem("wst_ready"), l + 1)
                pe.wait_ge(sem("da_exp"), 16 * (l + 1))
                for h in range(4):
                    m = pe.matmul(T0[:, h * P:(h + 1) * P], wsts[:, h, :], md_vn(h), start=(h == 0), stop=True,
                                  skip_group_check=True)
                m.then_inc(sem("sgu_done"), 1)
                pe.wait_ge(sem("cex_ready"), 2 * (l + 1))
                for ct in range(2):
                    for j in range(4):
                        s = 4 * ct + j
                        mine = [x for x in range(ST) if (x in POOL_POST) == (s in POOL_POST)]
                        pe.wait_ge(sem("state_ready_pool" if s in POOL_POST else "state_ready"), 2 * (len(mine) * l + mine.index(s) + 1))
                        for c in range(2):
                            m = pe.matmul(T1[32 * j:32 * j + 32, ct * TOK:(ct + 1) * TOK], cex[:, c, s, :], bu[:, s, c, :],
                                          start=(c == 0), stop=(c == 1), skip_group_check=True)
                m.then_inc(sem("y_done"), 1)
                pe.wait_ge(sem("sgu_ready"), 4 * (l + 1))
                for f in range(2):
                    for t in range(TT):
                        m = pe.transpose(S0[:, f * TOK + t * P:f * TOK + (t + 1) * P], xn[:, t, 512 + f * P:512 + (f + 1) * P], ident)
                m.then_inc(sem("mix_tr"), 1)
                pe.wait_ge(sem("diff_ready"), 2 * (l + 1))
                for f in range(4):
                    for t in range(TT):
                        bank = (S1, T0)[f // 2]
                        m = pe.transpose(bank[:, (f % 2) * TOK + t * P:(f % 2) * TOK + (t + 1) * P],
                                         xn[:, t, f * P:(f + 1) * P], ident)
                m.then_inc(sem("mix_tr"), 1)
                pe.wait_ge(sem("wglu_landed"), 16 * (l + 1))
                pe.wait_ge(sem("gelu_ready"), 2 * (l + 1))
                pe.wait_ge(sem("mix_lo"), 4 * l + 1)
                for f in range(2):
                    for k in range(2):
                        m = pe.matmul(S0[:, f * TOK:(f + 1) * TOK], wglus[:, k, f * P:(f + 1) * P], md_g(k),
                                      start=(f == 0 and k == 0), stop=(k == 1), skip_group_check=True)
                m.then_inc(sem("glu_done"), 1)
                pe.wait_ge(sem("mix_lo"), 4 * (l + 1))
                project(f"out{l}_0")
                project(f"out{l}_1")
                norm_transposes(2 + 2 * l)
                xt = (sem("xt_lo"), 8 * (2 + 2 * l), 2)
                for j in range(UNITS):
                    project(f"up{l}_{j}", fm=True, ready=xt)
                for i in range(2):
                    project(f"down{l}_{i}", xh=hth, xl=htl, ready=None if i else (sem("ht_lo"), UNITS * l, 1))
            if upto == 1:
                return

            norm_transposes(5)
            project("mq", fm=True, ready=(sem("xt_lo"), 40, 2))
            project("bq")
            project("bkv")
            project("gb")
            pe.wait_ge(sem("brope_ready"), 4)
            for f in range(4):
                for t in range(TT):
                    m = pe.transpose((T0, T1)[f // 2][:, (f % 2) * TOK + t * P:(f % 2) * TOK + (t + 1) * P],
                                     rt[:, t, f * P:(f + 1) * P], ident)
            m.then_inc(sem("b_tr"), 1)
            pe.wait_ge(sem("bkrope_ready"), 8)
            for f in range(2):
                for t in range(TT):
                    m = pe.transpose(S0[:, f * TOK + t * P:f * TOK + (t + 1) * P], xn[:, t, 256 + f * P:256 + (f + 1) * P], ident)
            m.then_inc(sem("b_tr"), 1)
            project("gm")

            def bm_scores(k):
                br, h, t = BM[k]
                if k:
                    pe.wait_ge(sem("bm_exp"), k)
                if br == "b":
                    a, b = (h % 2) * HD, (h % 2 + 1) * HD
                    m = pe.matmul(S0[:, 0:TOK], bqT[a:b, h // 2, t * P:(t + 1) * P], bkT[a:b, h // 4, :], start=True, stop=True)
                else:
                    m = pe.matmul(S0[:, 0:TOK], mqT[:, h, t * P:(t + 1) * P], kmT[:, h, :], start=True, stop=True)
                m.then_inc(sem("bm_sc"), 1)

            def bm_transposes(k):
                pe.wait_ge(sem("bm_exp"), k + 1)
                if k:
                    pe.wait_ge(sem("bm_pt"), k)
                for i in range(2):
                    m = pe.transpose(T0[:, i * P:(i + 1) * P], sm2[:, k % 2, i * P:(i + 1) * P], ident)
                m.then_inc(sem("bm_tr"), 1)

            def bm_values(k):
                br, h, t = BM[k]
                pe.wait_ge(sem("bm_pt"), k + 1)
                if k:
                    pe.wait_ge(sem("bm_out"), k)
                for i in range(2):
                    v = bv[:, i, (h // 4) * HD:(h // 4 + 1) * HD] if br == "b" else vm[:, i, h * MD:(h + 1) * MD]
                    m = pe.matmul(T1[:, 0:HD if br == "b" else MD], pT2[:, k % 2, i, :], v, start=(i == 0), stop=(i == 1))
                m.then_inc(sem("bm_pv"), 1)

            pe.wait_ge(sem("b_ev"), 3)
            pe.wait_ge(sem("bv_ready"), 2)
            pe.wait_ge(sem("mq_ev"), 2)
            for c, nm in enumerate(A_CHUNKS):
                for j in range(4):
                    project(nm, pairs=[j])
                    if 1 <= c <= 6 and j >= 2:
                        rnd = 2 * (c - 1) + j - 2
                        pe.wait_ge(sem("a_rope"), 4 * c)
                        if rnd:
                            pe.wait_ge(sem("a_ev"), rnd)
                        for i in range(2):
                            f = 2 * (j - 2) + i
                            for t in range(TT):
                                m = pe.transpose(S1[:, i * TOK + t * P:i * TOK + (t + 1) * P], rt[:, t, f * P:(f + 1) * P], ident)
                        m.then_inc(sem("a_tr"), 1)
                    for k in bm_slots(4 * c + j):
                        if k < len(BM):
                            bm_scores(k)
                        if 1 <= k <= len(BM):
                            bm_transposes(k - 1)
                        if k >= 2:
                            bm_values(k - 2)

            def a_scores(k):
                h, t = divmod(k, TT)
                a, b = (h % 2) * HD, (h % 2 + 1) * HD
                if k:
                    pe.wait_ge(sem("a_max"), 2 * k)
                if k >= 3:
                    pe.wait_ge(sem("a_out"), k - 2)
                for g in range(NG):
                    o = (S0, S0, S1)[g][:, (g % 2) * TOK:(g % 2 + 1) * TOK]
                    m = pe.matmul(o, aqT[a:b, 0, g, h // 2, t * P:(t + 1) * P], aqT[a:b, 1, g, h // 2, :],
                                  start=(g != 1), stop=True, skip_group_check=True)
                m.then_inc(sem("a_sc"), 1)

            def a_transposes(k):
                pe.wait_ge(sem("a_exp"), k + 1)
                if k:
                    pe.wait_ge(sem("a_pt"), 2 * k)
                for i in range(2 * NG):
                    m = pe.transpose((T0, T1)[i // 4][:, (i % 4) * P:(i % 4 + 1) * P], sm2[:, k % 2, i * P:(i + 1) * P], ident)
                m.then_inc(sem("a_ptr"), 1)

            def a_values(k):
                h, t = divmod(k, TT)
                pe.wait_ge(sem("a_pt"), 2 * k + 2)
                if k:
                    pe.wait_ge(sem("a_out"), k)
                pe.wait_ge(sem("a_max"), 2 * min(k + 2, AH * TT))
                for i in range(2 * NG):
                    m = pe.matmul(S1[:, TOK:TOK + HD], pT2[:, k % 2, i, :], va[:, i // 2, i % 2, h * HD:(h + 1) * HD],
                                  start=(i == 0), stop=(i == 2 * NG - 1))
                m.then_inc(sem("apv_done"), 1)

            for n in range(24):
                project(f"mg{n // 4}", pairs=[n % 4])
                for k in a_slots(n):
                    if k == 0:
                        pe.wait_ge(sem("a_ev"), 12)
                        pe.wait_ge(sem("av_ready"), 6)
                        pe.wait_ge(sem("bm_out"), len(BM))
                    if k >= 2:
                        a_values(k - 2)
                    if k < AH * TT:
                        a_scores(k)
                    if 1 <= k <= AH * TT:
                        a_transposes(k - 1)
            for b in range(3):
                for f in range(0, 4, 2):
                    i = 2 * b + f // 2
                    pe.wait_ge(sem("a_pt"), 2 * AH * TT)
                    if i == 3:
                        pe.wait_ge(sem("a_out"), AH * TT)
                    if i >= 4:
                        pe.wait_ge(sem("o_lo"), i - 3)
                    for q in range(2):
                        for t in range(TT):
                            m = pe.transpose(OBANKS[i % 4][:, q * TOK + t * P:q * TOK + (t + 1) * P],
                                             gat[:, b, t, (f + q) * P:(f + q + 1) * P], ident)
                    m.then_inc(sem("o_tr"), 1)
            for nm in BRANCH_ORDER:
                b = "bma".index(nm[0])
                project("br" + nm, xh=oth[:, 4 * b:4 * b + 4, :], xl=otl[:, 4 * b:4 * b + 4, :],
                        ready=(sem("o_lo"), 2 * b, 1))
            for f in range(KD):
                if f % 2 == 0:
                    pe.wait_ge(sem("o_lo"), 6)
                pe.wait_ge(sem("merged_ready"), 2 if f < 4 else 4)
                for t in range(TT):
                    m = pe.transpose(AUX[f // 2][:, (f % 2) * TOK + t * P:(f % 2) * TOK + (t + 1) * P],
                                     merged[:, t, f * P:(f + 1) * P], ident)
                if f % 2:
                    m.then_inc(sem("m_tr"), 1)
            project("wo0", ready=(sem("m_lo"), 0, 1))
            project("wo1")

        @block.scalar
        def _(act):
            at = [0]

            def hi_upto(n):
                while at[0] < min(n, stop_pair):
                    p = at[0]
                    act.wait_ge(raw_landed[p % RAW], 16 * (p // RAW + 1))
                    if p >= RING:
                        act.wait_ge(pair_used, p - RING + 1)
                    act.activation(whi[:, p % RING, :], raw[:, p % RAW, :], ACT.Copy).then_inc(hi_ready, 1)
                    at[0] += 1

            stop_pair = FIRST[chunk("mq")] if upto == 1 else NPAIRS
            n_sq = [0]

            def squares(n, src, t, half):
                if n_sq[0]:
                    act.wait_ge(sem("ssq_ready"), n_sq[0])
                n_sq[0] += 1
                act.activation(sqs[:, :], src[:, t, half * 512:(half + 1) * 512], ACT.Square,
                               accum_out=ssq[:, n, 2 * t + half:2 * t + half + 1]).then_inc(sem("ssq_ready"), 1)

            def norm_hi(n):
                g, o = NORM_GAIN[n]
                for f in range(KD):
                    if f % 2 == 0:
                        act.wait_ge(sem("xt_tr"), 4 * n + f // 2 + 1)
                    act.activation(xth[:, f, :], AUX[f // 2][:, (f % 2) * TOK:(f % 2 + 1) * TOK], ACT.Copy,
                                   scale=col(g, o + f, 1)).then_inc(sem("xt_hi"), 1)

            for t in range(TT):
                act.wait_ge(sem(f"mem_landed{t}"), 16)
                for half in range(2):
                    squares(0, xn, t, half)
            hi_upto(2)
            act.wait_ge(sem("x_landed"), 16)
            for t in range(TT):
                for half in range(2):
                    squares(1, xres, t, half)
            act.wait_ge(sem("col_landed"), 16)
            norm_hi(0)
            act.activation(sp_[:, 0, :], col("ldt"), ACT.Exp).then_inc(sem("par_a"), 1)
            hi_upto(end_pair("km") - 2)
            act.wait_ge(sem("par_d"), 1)
            act.activation(sp_[:, 3, :], sp_[:, 1, :], ACT.Exp).then_inc(sem("par_a"), 1)
            act.activation(lamv[:, 2:4], lamv[:, 0:2], ACT.Exp).then_inc(sem("par_a"), 1)
            act.activation(lamv[:, 6:8], lamv[:, 4:6], ACT.Exp).then_inc(sem("par_a"), 1)
            act.activation(sp_[:, 6, :], sp_[:, 5, :], ACT.Sin).then_inc(sem("par_a"), 1)
            act.activation(sp_[:, 7, :], sp_[:, 5, :], ACT.Sin, scale=0.5).then_inc(sem("par_a"), 1)
            hi_upto(end_pair("km") + 1)
            for t in range(TT):
                act.wait_ge(pair_used, end_pair("km"))
                act.copy(kmT[:, 2 * t:2 * t + 2, :], PJ[0][:, t, :]).then_inc(sem("mem_ev"), 1)
            hi_upto(end_pair("vm") + 1)
            for t in range(TT):
                act.wait_ge(pair_used, end_pair("vm"))
                act.copy(vm[:, t, :], PJ[1][:, t, :]).then_inc(sem("mem_ev"), 1)

            for l in range(LAYERS):
                act.wait_ge(pair_used, FIRST[chunk(f"ssm_u{l}")])
                norm_hi(1 + 2 * l)
                hi_upto(end_pair(f"ssm_u{l}") + 2)
                if l == 0:
                    act.wait_ge(sem("par_d"), 1)
                for s in range(ST):
                    act.wait_ge(sem("bu_done"), ST * l + s + 1)
                    act.copy(bu[:, s, :, :], AUX[s % 4][:, :]).then_inc(sem("bu_ready"), 1)
                    if s % 2:
                        hi_upto(end_pair(f"ssm_u{l}") + 3 + s // 2)
                for i, nm in enumerate("qk"):
                    c = chunk(f"{nm}{l}")
                    hi_upto(end_pair(f"{nm}{l}") + 4)
                    act.wait_ge(pair_used, FIRST[c] + PAIRS[c])
                    for t in range(TT):
                        if t == 0 and (i or l):
                            act.wait_ge(sem("hss_ready"), 2 * l + i)
                            act.wait_ge(sem("rope_ready"), 4 * (2 * l + i))
                        act.activation(hsq[:, t, :], PJ[BUF[c]][:, t, :], ACT.Square).then_inc(sem("hsq_ready"), 1)
                    if i == 1:
                        hi_upto(end_pair(f"k{l}") + 5)
                        act.wait_ge(sem("qk_tr"), 2 * l + 1)
                        act.copy(qT[:, 0:2, :], S0[:, :]).then_inc(sem("qk_ev"), 1)
                        act.copy(qT[:, 2:4, :], S1[:, :]).then_inc(sem("qk_ev"), 1)
                c = chunk(f"v{l}")
                hi_upto(end_pair(f"v{l}") + 4)
                act.wait_ge(pair_used, FIRST[c] + PAIRS[c])
                for t in range(TT):
                    m = act.copy(v_sb[:, t, :], PJ[BUF[c]][:, t, :])
                    m.then_inc(sem("v_ready"), 1)
                act.wait_ge(sem("qk_tr"), 2 * l + 2)
                act.copy(kT[:, 0:2, :], T0[:, :]).then_inc(sem("qk_ev"), 1)
                act.copy(kT[:, 2:4, :], T1[:, :]).then_inc(sem("qk_ev"), 1)
                c = chunk(f"gmlp{l}")
                hi_upto(end_pair(f"gmlp{l}") + 2)
                act.wait_ge(pair_used, FIRST[c] + PAIRS[c])
                act.wait_ge(sem("ssq_ready"), n_sq[0])
                for t in range(TT):
                    if t:
                        act.wait_ge(sem("gss_ready"), 2 * l + 1)
                    act.activation(sqs[:, 0:256], PJ[BUF[c]][:, t, 256:512], ACT.Square,
                                   accum_out=gss[:, l, t:t + 1]).then_inc(sem("gss_ready"), 1)

                def exps(b):
                    t, heads = DB[b]
                    n = P * (t + 1)
                    act.wait_ge(sem("da_nb"), 3 * l + b + 1)
                    if b == 2:
                        act.wait_ge(sem("da_tr"), 3 * l + 1)
                    for c, bank in enumerate(DBANKS[b]):
                        for i in range(len(heads)):
                            act.activation(sm[:, b % 2, c, i * n:(i + 1) * n], bank[:, i * n:(i + 1) * n], ACT.Exp,
                                           bias=st_[:, b, 2 + c, i:i + 1], scale=QKD ** -0.5,
                                           accum_out=st_[:, b, 4 + c, i:i + 1]).then_inc(sem("da_exp"), 1)

                def prob_evac(b):
                    act.wait_ge(sem("da_tr"), 3 * l + b + 1)
                    if b == 2:
                        act.wait_ge(sem("da_pv"), 3 * l + 1)
                    act.copy(pT[:, b % 2, :, :], PJ[buf(f"v{l}")][:, b % 2, :]).then_inc(sem("da_pt"), 1)

                exps(0)
                hi_upto(end_pair(f"gmlp{l}") + 3)
                exps(1)
                hi_upto(end_pair(f"gmlp{l}") + 4)
                prob_evac(0)
                exps(2)
                prob_evac(1)
                prob_evac(2)
                hi_upto(end_pair(f"gmlp{l}") + RING)
                for t in range(TT):
                    act.wait_ge(sem("da_o"), 2 * l + t + 1)
                    act.activation(hsq[:, t, :], xn[:, t, 0:512], ACT.Square).then_inc(sem("osq_ready"), 1)
                act.wait_ge(sem("ypre_ready"), 2 * (l + 1))
                for f in range(2):
                    act.activation(md[:, 0, f, :], md[:, 1, f, :], ACT.Gelu_apprx_tanh).then_inc(sem("gelu_ready"), 1)
                act.wait_ge(sem("mix_tr"), 2 * l + 1)
                act.wait_ge(pair_used, end_pair(f"gmlp{l}"))
                act.copy(xth[:, 2:4, :], S0[:, :]).then_inc(sem("mix_hi"), 1)
                act.wait_ge(sem("mix_tr"), 2 * l + 2)
                act.copy(xth[:, 4:6, :], S1[:, :]).then_inc(sem("mix_hi"), 1)
                act.copy(xth[:, 6:8, :], T0[:, :]).then_inc(sem("mix_hi"), 1)
                act.wait_ge(sem("glu_done"), l + 1)
                for f in range(2):
                    act.activation(md[:, 1, f, :], S0[:, f * TOK:(f + 1) * TOK], ACT.Tanh, scale=0.5,
                                   bias=hb[:, 2 * l + f:2 * l + f + 1]).then_inc(sem("tanh_ready"), 1)
                act.wait_ge(sem("glu_prod"), l + 1)
                act.activation(xth[:, 0:2, :], md[:, 2, :, :], ACT.Copy, scale=0.5).then_inc(sem("mix_hi"), 1)
                for i in range(2):
                    nm = f"out{l}_{i}"
                    hi_upto(end_pair(nm) + (1 if i == 0 else RING))
                    for t in range(TT):
                        act.wait_ge(sem("resid"), 8 * l + 2 * i + t + 1)
                        squares(2 + 2 * l, xres, t, i)
                act.wait_ge(pair_used, end_pair(f"out{l}_1"))
                norm_hi(2 + 2 * l)

                def unit_first(j):
                    c = chunk(f"up{l}_{j}")
                    act.wait_ge(pair_used, FIRST[c] + PAIRS[c])
                    if UNITS * l + j >= 2:
                        act.wait_ge(sem("gated"), UNITS * l + j - 1)
                    for i in range(4):
                        k = conv_col(l, j, i)
                        act.activation(acc[:, j % 2, i, :], PJ[BUF[c]][:, i // 2, (i % 2) * TOK:(i % 2 + 1) * TOK],
                                       ACT.Identity, scale=colv[:, k + 2:k + 3], bias=colv[:, k + 3:k + 4]).then_inc(sem("conv_a"), 1)

                def unit_gelu(j):
                    act.wait_ge(sem("conv_d"), 4 * (UNITS * l + j + 1))
                    act.activation(acc[:, j % 2, 0:2, :], acc[:, j % 2, 0:2, :], ACT.Gelu_apprx_tanh).then_inc(sem("ffn_gelu"), 1)

                def unit_hi(j):
                    act.wait_ge(sem("gated"), UNITS * l + j + 1)
                    act.copy(hth[:, 2 * j:2 * j + 2, :], gtd[:, j % 2, :, :]).then_inc(sem("ht_hi"), 1)

                for j in range(UNITS + 1):
                    if j < UNITS:
                        hi_upto(end_pair(f"up{l}_{j}") + 3)
                        unit_first(j)
                        hi_upto(end_pair(f"up{l}_{j}") + 4)
                    if j > 0:
                        unit_hi(j - 1)
                        if j < UNITS:
                            hi_upto(end_pair(f"up{l}_{j}") + 5)
                    if j < UNITS:
                        unit_gelu(j)
                for i in range(2):
                    nm = f"down{l}_{i}"
                    hi_upto(end_pair(nm) + (1 if i == 0 else RING))
                    for t in range(TT):
                        if l == LAYERS - 1 and upto == 1:
                            continue
                        act.wait_ge(sem("resid"), 8 * l + 4 + 2 * i + t + 1)
                        squares(3 + 2 * l, xres, t, i)
            if upto == 1:
                return

            act.wait_ge(pair_used, FIRST[chunk("mq")])
            norm_hi(5)
            hi_upto(end_pair("mq") + 1)
            act.wait_ge(pair_used, end_pair("mq"))
            for t in range(TT):
                act.copy(mqT[:, 2 * t:2 * t + 2, :], PJ[buf("mq")][:, t, :]).then_inc(sem("mq_ev"), 1)
            hi_upto(end_pair("bq") + 1)
            act.wait_ge(pair_used, end_pair("bq"))
            for t in range(TT):
                act.activation(sm2[:, t, 0:512], PJ[buf("bq")][:, t, :], ACT.Square).then_inc(sem("bsq_ready"), 1)
            hi_upto(end_pair("bkv") + 1)
            act.wait_ge(pair_used, end_pair("bkv"))
            for t in range(TT):
                act.activation(pT2[:, t, 0, :], PJ[buf("bkv")][:, t, 0:P], ACT.Square).then_inc(sem("bksq_ready"), 1)
                act.copy(bv[:, t, :], PJ[buf("bkv")][:, t, P:2 * P]).then_inc(sem("bv_ready"), 1)

            def gate_tanh(nm, th):
                i = SILU_ORDER.index(nm)
                act.wait_ge(pair_used, end_pair(nm))
                if i == 1:
                    act.wait_ge(sem("silu_ready"), 2)
                for t in range(TT):
                    act.activation(th[:, t, 0:512], PJ[buf(nm)][:, t, :], ACT.Tanh, scale=0.5).then_inc(sem("th_ready"), 1)

            hi_upto(end_pair("gb") + 2)
            act.wait_ge(sem("bhss_ready"), 1)
            gate_tanh("gb", sm2)
            act.wait_ge(sem("b_tr"), 1)
            act.copy(bqT[:, 0:2, :], T0[:, :]).then_inc(sem("b_ev"), 1)
            act.copy(bqT[:, 2:4, :], T1[:, :]).then_inc(sem("b_ev"), 1)
            act.wait_ge(sem("b_tr"), 2)
            act.copy(bkT[:, :, :], S0[:, :]).then_inc(sem("b_ev"), 1)
            hi_upto(end_pair("gm") + 2)
            gate_tanh("gm", sm2)
            for c, nm in enumerate(A_CHUNKS):
                for j in range(4):
                    n = 4 * c + j
                    hi_upto(F2 + n + 3)
                    if j == 1 and c >= 7:
                        g = c - 7
                        act.wait_ge(pair_used, end_pair(f"av{g}"))
                        for t in range(TT):
                            act.copy(va[:, g, t, :], PJ[buf(f"av{g}")][:, t, :]).then_inc(sem("av_ready"), 1)
                    if 1 <= c <= 6 and j >= 2:
                        rnd = 2 * (c - 1) + j - 2
                        act.wait_ge(sem("a_tr"), rnd + 1)
                        w, g = divmod(c - 1, NG)
                        act.copy(aqT[:, w, g, 2 * (j - 2):2 * (j - 2) + 2, :], S1[:, :]).then_inc(sem("a_ev"), 1)
                    for k in bm_slots(n):
                        if k < len(BM):
                            br, h, t = BM[k]
                            act.wait_ge(sem("bm_nb"), k + 1)
                            if k == 0:
                                act.wait_ge(sem("silu_ready"), 4)
                            if k >= 2:
                                act.wait_ge(sem("bm_tr"), k - 1)
                            act.activation(sm2[:, k % 2, 0:TOK], S0[:, 0:TOK], ACT.Exp, bias=sx[:, k % 4, 1:2],
                                           scale=(HD if br == "b" else MD) ** -0.5,
                                           accum_out=sx[:, k % 4, 2:3]).then_inc(sem("bm_exp"), 1)
                        if 1 <= k <= len(BM):
                            act.wait_ge(sem("bm_tr"), k)
                            if k >= 3:
                                act.wait_ge(sem("bm_pv"), k - 2)
                            act.copy(pT2[:, (k - 1) % 2, 0:2, :], T0[:, 0:TOK]).then_inc(sem("bm_pt"), 1)
            hi_upto(F3 + 2)
            act.wait_ge(sem("a_tr"), 12)
            gate_tanh("ga", rt)
            for n in range(24):
                hi_upto(F3 + n + 3)
                for k in a_slots(n):
                    if k < AH * TT:
                        act.wait_ge(sem("a_nb"), k + 1)
                        act.activation(sm2[:, k % 2, :], sm2[:, k % 2, :], ACT.Exp, bias=sx[:, k % 4, 1:2], scale=HD ** -0.5,
                                       accum_out=sx[:, k % 4, 2:3]).then_inc(sem("a_exp"), 1)
                    if 1 <= k <= AH * TT:
                        act.wait_ge(sem("a_ptr"), k)
                        if k >= 3:
                            act.wait_ge(sem("apv_done"), k - 2)
                        act.copy(pT2[:, (k - 1) % 2, 0:4, :], T0[:, :]).then_inc(sem("a_pt"), 1)
                        act.copy(pT2[:, (k - 1) % 2, 4:6, :], T1[:, 0:TOK]).then_inc(sem("a_pt"), 1)
                if n % 4 == 1 and n > 4:
                    merge_tanh(act, n // 4 - 1)
            merge_tanh(act, 5)
            hi_upto(F3 + 24 + RING)
            for i in range(6):
                act.wait_ge(sem("o_tr"), i + 1)
                act.activation(oth[:, 2 * i:2 * i + 2, :], OBANKS[i % 4][:, :], ACT.Copy, scale=0.5).then_inc(sem("o_hi"), 1)
            hi_upto(FIRST[chunk("wo0")] + 3)
            for i in range(4):
                act.wait_ge(sem("m_tr"), i + 1)
                act.activation(xth[:, 2 * i:2 * i + 2, :], AUX[i][:, :], ACT.Copy, scale=0.5).then_inc(sem("m_hi"), 1)
            for i in range(2):
                nm = f"wo{i}"
                hi_upto(end_pair(nm) + 1)
                act.wait_ge(pair_used, end_pair(nm))
                for t in range(TT):
                    act.wait_ge(sem("ssq_ready"), n_sq[0])
                    n_sq[0] += 1
                    act.activation(sqs[:, :], PJ[buf(nm)][:, t, :], ACT.Square,
                                   accum_out=ssq[:, 6, 2 * t + i:2 * t + i + 1]).then_inc(sem("ssq_ready"), 1)

        @block.gpsimd
        def _(pool):
            pool.memset(mhalf[:], -0.5).then_inc(sem("mhalf_ready"), 1)
            pool.wait_ge(sem("mhalf_ready"), 1)

            steps = [0]

            def link(ins):
                steps[0] += 1
                ins.then_inc(sem("pool_chain"), 1)
                pool.wait_ge(sem("pool_chain"), steps[0])

            def power(out_, in_, n, width, signal):
                link(pool.tensor_scalar(out_, in_, 1.0 / width, EPS, ALU.mult, ALU.add))
                pool.tensor_tensor(out_, out_, mhalf[:, 0:n], ALU.pow).then_inc(sem(signal), 1)

            def norm_rstd(n):
                pool.wait_ge(sem("ssq_ready"), 4 * (n + 1))
                link(pool.tensor_tensor(ssm1[:, n, :], ssq[:, n, 0:4:2], ssq[:, n, 1:4:2], ALU.add))
                power(rstd[:, n, :], ssm1[:, n, :], 2, D, "rstd_ready")

            HR_AFTER = ((0, 3), (3, 5))
            def pre_rotate(l, s):
                pool.wait_ge(sem("bu_ready"), ST * l + s + 1)
                if ST * l + s:
                    pool.wait_ge(sem("pre_rot"), 2 * (ST * l + s))
                if l and s == 0:
                    pool.wait_ge(sem("state_ready_pool"), 2 * len(POOL_POST) * l)
                cc, ss = wide(tab[:, 0, s, :], 2), wide(tab[:, 1, s, :], 2)
                pool.tensor_tensor(mp[:, 0, :, :], bu[:, s, :, :], cc, ALU.mult).then_inc(sem("pool_chain"), 1)
                pool.tensor_tensor(mp[:, 1, :, :], bu[:, s, :, :], ss, ALU.mult).then_inc(sem("pool_chain"), 1)
                steps[0] += 2
                pool.wait_ge(sem("pool_chain"), steps[0])
                pool.tensor_tensor(bu[:, s, 0, :], mp[:, 0, 0, :], mp[:, 1, 1, :], ALU.add).then_inc(sem("pre_rot"), 1)
                pool.tensor_tensor(bu[:, s, 1, :], mp[:, 0, 1, :], mp[:, 1, 0, :], ALU.subtract).then_inc(sem("pre_rot"), 1)

            norm_rstd(0)
            norm_rstd(1)
            pool.wait_ge(sem("par_done"), 1)
            fold_coefficient(pool, link, 0, v_sb[:, :, :].rearrange("p t (o a b) -> p (t o) a b", o=2, b=32))
            table_base(pool, link, 0)
            table_factor(pool, link, tb)
            table_factor(pool, link, ta)
            for s in range(0, ST, 2):
                table_product(pool, link, 0, s, v_sb[:, :, :].rearrange("p k (c a b) -> p k c a b", c=2, a=16))
            for l in range(LAYERS):
                if l > 0:
                    norm_rstd(1 + 2 * l)

                for s in range(ST):
                    pre_rotate(l, s)
                    if s in HR_AFTER[l]:
                        pool.wait_ge(sem("hss_ready"), 2 * l + 1 + HR_AFTER[l].index(s))
                        power(hr[:, HR_AFTER[l].index(s), 0:16], hss[:, :], 16, QKD, "hr_ready")
                    if s == 7:
                        pool.wait_ge(sem("gss_ready"), 2 * (l + 1))
                        power(gr[:, l, :], gss[:, l, :], 2, 256, "gr_ready")
                for s in POOL_POST:
                    pool.wait_ge(sem("scanned"), 2 * (ST * l + s + 1))
                    pool.wait_ge(sem("pre_rot"), 2 * ST * (l + 1))
                    post_rotate(pool, l, s, mp)
                pool.wait_ge(sem("oss_ready"), l + 1)
                power(hr[:, 0, 0:8], hss[:, 0:8], 8, VD, "or_ready")
                norm_rstd(2 + 2 * l)
                for j in range(UNITS):
                    pool.wait_ge(sem("ffn_gelu"), UNITS * l + j + 1)
                    if j >= 2 or l:
                        pool.wait_ge(sem("ht_lo"), UNITS * l + j - 1)
                    pool.tensor_tensor(gtd[:, j % 2, :, :], acc[:, j % 2, 0:2, :], acc[:, j % 2, 2:4, :],
                                       ALU.mult).then_inc(sem("gated"), 1)
                    if l + 1 < LAYERS:
                        if j == 1:
                            table_base(pool, link, l + 1)
                            table_factor(pool, link, tb)
                        if j == 2:
                            table_factor(pool, link, ta)
                        if 3 <= j < 3 + ST // 2:
                            table_product(pool, link, l + 1, 2 * (j - 3),
                                          xn[:, 0, :].rearrange("p (k c a b) -> p k c a b", k=2, c=2, a=16))
                        if j == 3 + ST // 2:
                            fold_coefficient(pool, link, l + 1, xn[:, 0, :].rearrange("p (o a b) -> p o a b", o=4, b=32))
            if upto == 1:
                return

            norm_rstd(5)
            pool.wait_ge(sem("bhss_ready"), 1)
            power(hr[:, 0, 0:16], hss[:, 0:16], 16, HD, "bhr_ready")
            pool.wait_ge(sem("bhss_ready"), 2)
            power(hr[:, 1, 0:4], hss[:, 0:4], 4, HD, "bhr_ready")
            for c in range(6):
                if c:
                    pool.wait_ge(sem("a_tr"), 2 * c)
                else:
                    pool.wait_ge(sem("b_tr"), 1)
                for t in range(TT):
                    pool.wait_ge(sem("rot_terms"), 4 * c + 2 * t + 2)
                    c8, s8 = (xn[:, t, i * 512:(i + 1) * 512].rearrange("p (g d) -> p g d", g=8) for i in range(2))
                    o8 = rt[:, t, :].rearrange("p (g d) -> p g d", g=8)
                    pool.tensor_tensor(o8[:, :, 0:32], c8[:, :, 0:32], s8[:, :, 32:64], ALU.subtract).then_inc(sem("a_rope"), 1)
                    pool.tensor_tensor(o8[:, :, 32:64], c8[:, :, 32:64], s8[:, :, 0:32], ALU.add).then_inc(sem("a_rope"), 1)
            for i in range(6):
                b, n = BRANCH_ORDER[i][0], int(BRANCH_ORDER[i][1])
                if b == "a":
                    continue
                for t in range(TT):
                    pool.wait_ge(sem("y_gated"), 2 * i + t + 1)
                    m = merged[:, t, 512 * n:512 * n + 512]
                    at = ("abm".index(b)) * D + 512 * n
                    if b == "m":
                        pool.wait_ge(sem("merged_b"), 2 * n + t + 1)
                    pool.tensor_tensor(m, m, gt[:, t, at:at + 512], ALU.add).then_inc(sem("merged_b" if b == "b" else "merged_ready"), 1)
            norm_rstd(6)

        @block.vector
        def _(dve):
            at = [0]
            steps = [0]
            stop_pair = FIRST[chunk("mq")] if upto == 1 else NPAIRS

            def link(ins):
                steps[0] += 1
                ins.then_inc(sem("dve_chain"), 1)
                dve.wait_ge(sem("dve_chain"), steps[0])

            def lo_upto(n):
                while at[0] < min(n, stop_pair):
                    p = at[0]
                    dve.wait_ge(hi_ready, p + 1)
                    dve.tensor_tensor(wlo[:, p % RING, :], raw[:, p % RAW, :], whi[:, p % RING, :].bitcast(F32),
                                      ALU.subtract).then_inc(lo_ready, 1)
                    at[0] += 1

            def norm_scale(n, src):
                dve.wait_ge(sem("rstd_ready"), n + 1)
                for t in range(TT):
                    dve.tensor_scalar(xn[:, t, :], src[:, t, :], rstd[:, n, t:t + 1], None, ALU.mult).then_inc(sem("xn_ready"), 1)

            def norm_lo(n):
                g, o = NORM_GAIN[n]
                for f in range(KD):
                    dve.wait_ge(sem("xt_hi"), KD * n + f // 2 * 2 + 2)
                    dve.scalar_tensor_tensor(out=xtl[:, f, :], in0=AUX[f // 2][:, (f % 2) * TOK:(f % 2 + 1) * TOK],
                                             scalar=col(g, o + f, 1), in1=xth[:, f, :].bitcast(F32),
                                             op0=ALU.mult, op1=ALU.subtract).then_inc(sem("xt_lo"), 1)

            norm_scale(0, xn)
            lo_upto(2)
            norm_lo(0)
            v = [sp_[:, i, :] for i in range(24)]
            dve.wait_ge(sem("row_landed"), 16)
            dve.wait_ge(sem("par_a"), 1)
            link(dve.tensor_tensor(v[1], col("are"), v[0], ALU.mult))
            link(dve.tensor_tensor(v[2], col("aim"), v[0], ALU.mult))
            link(dve.tensor_scalar(v[4], v[2], 1.0 / (2 * math.pi), None, ALU.mult))
            link(dve.tensor_scalar(v[4], v[4], 12582912.0, None, ALU.add))
            link(dve.tensor_scalar(v[4], v[4], -12582912.0, None, ALU.add))
            c1 = 6.28125
            c2 = round((2 * math.pi - c1) * 2 ** 21) / 2 ** 21
            c3 = 2 * math.pi - c1 - c2
            src_ = v[2]
            for cc in (c1, c2, c3):
                link(dve.scalar_tensor_tensor(out=v[5], in0=v[4], scalar=-cc, in1=src_, op0=ALU.mult, op1=ALU.add))
                src_ = v[5]
            link(dve.tensor_scalar(v[5], v[5], 3.1415925, -3.1415925, ALU.min, ALU.max))
            dve.wait_ge(sem("lam_landed"), 16)
            lamrow = bu[:, 0, :, :].rearrange("p c t -> p (c t)")
            for l in range(LAYERS):
                for i, (a, b) in enumerate((("lq1", "lk1"), ("lq2", "lk2"))):
                    ra, rb = (lamrow[:, LAM[z][0] + 64 * l:LAM[z][0] + 64 * l + 64] for z in (a, b))
                    link(dve.tensor_tensor_reduce(sqs2[:, :], ra, rb, 1.0, 0.0,
                                                  ALU.mult, ALU.add, lamv[:, 4 * i + l:4 * i + l + 1]))
            dve.sem_inc(sem("par_d"), 1)
            lo_upto(end_pair("km") - 3)
            dve.wait_ge(sem("cst_landed"), 16)
            dve.tensor_copy(identb[:, :], ident).then_inc(sem("maskb_ready"), 1)
            for t, k in ((0, 4), (1, 2)):
                dve.tensor_copy(maskb[:, t, :].rearrange("p (h n) -> p h n", h=k),
                                wide(cs("mdiff")[:, 0:128] if t == 0 else cs("mdiff")[:, 128:384], k)).then_inc(sem("maskb_ready"), 1)
            cosv = cs("cos").rearrange("p (t d) -> p t d", t=TT)
            sinv = cs("sin").rearrange("p (t d) -> p t d", t=TT)
            for l in range(LAYERS):
                link(dve.tensor_scalar(row("sub", VD * l, VD), row("sub", VD * l, VD), 1.0 - LAMBDA_INIT[l], None, ALU.mult))
            dve.wait_ge(sem("col_landed"), 16)
            link(dve.tensor_scalar(hb[:, :], col("bglu"), 0.5, None, ALU.mult))
            dve.wait_ge(sem("par_a"), 6)
            for l in range(LAYERS):
                link(dve.tensor_tensor(nlam[:, l:l + 1], lamv[:, 6 + l:7 + l], lamv[:, 2 + l:3 + l], ALU.subtract))
                link(dve.tensor_scalar(nlam[:, l:l + 1], nlam[:, l:l + 1], -LAMBDA_INIT[l], None, ALU.add))
            are, aim = col("are"), col("aim")
            link(dve.tensor_tensor(v[13], v[7], v[7], ALU.mult))
            link(dve.tensor_scalar(v[8], v[13], -2.0, 1.0, ALU.mult, ALU.add))
            link(dve.tensor_tensor(v[14], v[3], v[8], ALU.mult))
            link(dve.tensor_tensor(v[15], v[3], v[6], ALU.mult))
            link(dve.tensor_scalar(v[14], v[14], -1.0, None, ALU.add))
            link(dve.tensor_tensor(v[16], are, are, ALU.mult))
            link(dve.tensor_tensor(v[17], aim, aim, ALU.mult))
            link(dve.tensor_tensor(v[16], v[16], v[17], ALU.add))
            link(dve.reciprocal(v[16], v[16]))
            link(dve.tensor_tensor(v[17], v[14], are, ALU.mult))
            link(dve.tensor_tensor(v[18], v[15], aim, ALU.mult))
            link(dve.tensor_tensor(v[17], v[17], v[18], ALU.add))
            link(dve.tensor_tensor(v[9], v[17], v[16], ALU.mult))
            link(dve.tensor_tensor(v[17], v[15], are, ALU.mult))
            link(dve.tensor_tensor(v[18], v[14], aim, ALU.mult))
            link(dve.tensor_tensor(v[17], v[17], v[18], ALU.subtract))
            link(dve.tensor_tensor(v[10], v[17], v[16], ALU.mult))
            link(dve.tensor_scalar(v[11], v[10], -1.0, None, ALU.mult))
            link(dve.tensor_scalar(v[12], v[9], -1.0, None, ALU.mult))
            dve.sem_inc(sem("par_done"), 1)
            
            lo_upto(end_pair("km") + 1)
            lo_upto(end_pair("vm") - 2)

            for l in range(LAYERS):
                for i, (g, tb_) in enumerate((("qg", cosv), ("qg", sinv), ("kg", cosv), ("kg", sinv))):
                    link(dve.tensor_tensor(ropeq[:, i, :, :], tb_, wide(row(g, 64 * l, 64), TT), ALU.mult))
                dve.wait_ge(sem("wst_landed"), 16 * (l + 1))
                dve.memset(wsts[64:128, :, 0:64], 0.0).then_inc(sem("wst_ready"), 1)
                dve.wait_ge(sem("xt_tr"), 4 * (1 + 2 * l))
                dve.wait_ge(sem("cex_ready"), 2 * (l + 1))
                norm_scale(1 + 2 * l, xres)
                if l == 0:
                    lo_upto(end_pair("vm") + 1)
                norm_lo(1 + 2 * l)
                lo_upto(end_pair(f"ssm_u{l}") + 1)
                c = chunk(f"ssm_u{l}")
                dve.wait_ge(pair_used, FIRST[c] + PAIRS[c])
                dve.tensor_copy(uT[:, :, :], PJ[BUF[c]][:, 0, :]).then_inc(sem("u_ready"), 1)
                lo_upto(end_pair(f"ssm_u{l}") + 3)

                def qk_norm_rope(i, nm):
                    c = chunk(f"{nm}{l}")
                    pj = PJ[BUF[c]]
                    lo_upto(end_pair(f"{nm}{l}") + 3)
                    dve.wait_ge(sem("hsq_ready"), 4 * l + 2 * i + 2)
                    if i or l:
                        dve.wait_ge(sem("hr_ready"), 2 * l + i)
                    for t in range(TT):
                        m = dve.tensor_reduce(hss[:, 8 * t:8 * t + 8], hsq[:, t, :].rearrange("p (g d) -> p g d", g=8), AX.X, ALU.add)
                        if t == 0:
                            steps[0] += 1
                            m.then_inc(sem("dve_chain"), 1)
                            dve.wait_ge(sem("dve_chain"), steps[0])
                    m.then_inc(sem("hss_ready"), 1)
                    lo_upto(end_pair(f"{nm}{l}") + 5)
                    dve.wait_ge(sem("hr_ready"), 2 * l + i + 1)
                    for t in range(TT):
                        g8 = pj[:, t, :].rearrange("p (g d) -> p g d", g=8)
                        dve.tensor_tensor(qn[:, t, :].rearrange("p (g d) -> p g d", g=8), g8,
                                          wide(hr[:, i, 8 * t:8 * t + 8], QKD, 2), ALU.mult).then_inc(sem("qn_ready"), 1)
                    dve.wait_ge(sem("qn_ready"), 2 * (2 * l + i + 1))
                    for t in range(TT):
                        q8 = qn[:, t, :].rearrange("p (g d) -> p g d", g=8)
                        t2 = hsq[:, t, :].rearrange("p (g d) -> p g d", g=8)
                        o8 = xn[:, t, 512 * i:512 * i + 512].rearrange("p (g d) -> p g d", g=8)
                        cg, sg = (wide(ropeq[:, 2 * i + j, t, :], 8) for j in range(2))
                        dve.tensor_tensor(t2, q8, sg, ALU.mult).then_inc(sem("dve_chain"), 1)
                        dve.tensor_tensor(q8, q8, cg, ALU.mult).then_inc(sem("dve_chain"), 1)
                        steps[0] += 2
                        dve.wait_ge(sem("dve_chain"), steps[0])
                        dve.tensor_tensor(o8[:, :, 0:32], q8[:, :, 0:32], t2[:, :, 32:64], ALU.subtract).then_inc(sem("rope_ready"), 1)
                        dve.tensor_tensor(o8[:, :, 32:64], q8[:, :, 32:64], t2[:, :, 0:32], ALU.add).then_inc(sem("rope_ready"), 1)

                def ssm_scan(s):
                    dve.wait_ge(sem("pre_rot"), 2 * (ST * l + s + 1))
                    r = sp_[:, 3, 8 * l + s:8 * l + s + 1].to_broadcast([P, TOK])
                    for c in range(2):
                        dve.tensor_tensor_scan(bu[:, s, c, :], r, bu[:, s, c, :], 0.0, ALU.mult, ALU.add).then_inc(sem("scanned"), 1)
                    if s in POOL_POST:
                        return
                    dve.wait_ge(sem("scanned"), 2 * (ST * l + s + 1))
                    post_rotate(dve, l, s, md[:, 1:3, :, :])

                def batch_max(b):
                    t, heads = DB[b]
                    k = len(heads)
                    dve.wait_ge(sem("da_sc"), 3 * l + b + 1)
                    for c, bank in enumerate(DBANKS[b]):
                        link(dve.tensor_reduce(st_[:, b, c, 0:k], bank[:, :].rearrange("p (h n) -> p h n", h=k), AX.X, ALU.max))
                    dve.tensor_scalar(st_[:, b, 2:4, 0:k], st_[:, b, 0:2, 0:k], -(QKD ** -0.5), None, ALU.mult).then_inc(sem("da_nb"), 1)

                def combine(b):
                    k = len(DB[b][1])
                    dve.wait_ge(sem("da_exp"), 16 * l + EXPS[b])
                    link(dve.reciprocal(st_[:, b, 6:8, 0:k], st_[:, b, 4:6, 0:k]))
                    link(dve.scalar_tensor_tensor(out=st_[:, b, 7, 0:k], in0=st_[:, b, 7, 0:k], scalar=nlam[:, l:l + 1],
                                                  in1=st_[:, b, 4, 0:k], op0=ALU.mult, op1=ALU.mult))
                    p1 = sm[:, b % 2, 1, :].rearrange("p (h n) -> p h n", h=k)
                    link(dve.tensor_tensor(p1, p1, wide(st_[:, b, 7, 0:k], 512 // k, 2), ALU.mult))
                    dve.tensor_tensor(sm[:, b % 2, 1, :], sm[:, b % 2, 1, :], sm[:, b % 2, 0, :], ALU.add).then_inc(sem("da_w"), 1)

                def out_scale(t):
                    dve.wait_ge(sem("da_pv"), 3 * l + (1 if t == 0 else 3))
                    for b in ((0,) if t == 0 else (1, 2)):
                        k = len(DB[b][1])
                        a = DB[b][1][0] * VD
                        o = xn[:, t, a:a + k * VD].rearrange("p (h n) -> p h n", h=k)
                        i = PJ[buf(f"gmlp{l}")][:, t, a:a + k * VD].rearrange("p (h n) -> p h n", h=k)
                        m = dve.tensor_tensor(o, i, wide(st_[:, b, 6, 0:k], VD, 2), ALU.mult)
                        if b == 1:
                            link(m)
                    m.then_inc(sem("da_o"), 1)

                qk_norm_rope(0, "q")
                lo_upto(end_pair(f"q{l}") + 6)
                ssm_scan(0)
                qk_norm_rope(1, "k")
                lo_upto(end_pair(f"k{l}") + 6)
                ssm_scan(1)
                ssm_scan(2)
                lo_upto(end_pair(f"v{l}") + 3)
                ssm_scan(3)
                lo_upto(end_pair(f"gmlp{l}"))
                batch_max(0)
                batch_max(1)
                ssm_scan(4)
                combine(0)
                c = chunk(f"gmlp{l}")
                dve.wait_ge(sem("gr_ready"), l + 1)
                dve.wait_ge(sem("qk_tr"), 2 * (l + 1))
                for t in range(TT):
                    dve.scalar_tensor_tensor(out=xn[:, t, 768:1024], in0=PJ[BUF[c]][:, t, 256:512], scalar=gr[:, l, t:t + 1],
                                             in1=row("vg", 256 * l, 256), op0=ALU.mult, op1=ALU.mult).then_inc(sem("vn_ready"), 1)
                    dve.tensor_copy(ug[:, t, :], PJ[BUF[c]][:, t, 0:256]).then_inc(sem("ug_ready"), 1)

                ssm_scan(5)
                combine(1)
                batch_max(2)
                out_scale(0)
                combine(2)
                ssm_scan(6)
                out_scale(1)
                ssm_scan(7)
                lo_upto(end_pair(f"gmlp{l}") + RING)
                dve.wait_ge(sem("sgu_done"), l + 1)
                for h in range(4):
                    dve.scalar_tensor_tensor(out=xn[:, :, 512 + h * 64:576 + h * 64],
                                             in0=T0[:, h * P:(h + 1) * P].rearrange("p (t d) -> p t d", t=TT),
                                             scalar=col("bs", 4 * l + h, 1), in1=ug[:, :, h * 64:(h + 1) * 64],
                                             op0=ALU.add, op1=ALU.mult).then_inc(sem("sgu_ready"), 1)
                dve.wait_ge(sem("y_done"), l + 1)
                for f in range(2):
                    dve.scalar_tensor_tensor(out=md[:, 1, f, :], in0=uT[:, f, :], scalar=col("dskip", 2 * l + f, 1),
                                             in1=T1[:, f * TOK:(f + 1) * TOK], op0=ALU.mult, op1=ALU.add).then_inc(sem("ypre_ready"), 1)
                dve.wait_ge(sem("osq_ready"), 2 * (l + 1))
                dve.wait_ge(sem("hr_ready"), 2 * (l + 1))
                dve.tensor_reduce(hss[:, 0:8], hsq[:, :, :].rearrange("p t (g d) -> p (t g) d", g=4), AX.X, ALU.add)\
                   .then_inc(sem("oss_ready"), 1)
                dve.wait_ge(sem("mix_tr"), 2 * l + 1)
                dve.wait_ge(sem("mix_hi"), 4 * l + 1)
                dve.tensor_tensor(xtl[:, 2:4, :], S0[:, :].rearrange("p (f d) -> p f d", f=2), xth[:, 2:4, :].bitcast(F32),
                                  ALU.subtract).then_inc(sem("mix_lo"), 1)
                dve.wait_ge(sem("or_ready"), l + 1)
                a8 = xn[:, :, 0:512]
                for t in range(TT):
                    a4 = xn[:, t, 0:512].rearrange("p (g d) -> p g d", g=4)
                    link(dve.tensor_tensor(a4, a4, wide(hr[:, 0, 4 * t:4 * t + 4], VD, 2), ALU.mult))
                    dve.tensor_tensor(a4, a4, wide(row("sub", VD * l, VD), 4), ALU.mult).then_inc(sem("diff_ready"), 1)
                dve.wait_ge(sem("mix_hi"), 4 * l + 3)
                for i, bank in enumerate((S1, T0)):
                    dve.tensor_tensor(xtl[:, 4 + 2 * i:6 + 2 * i, :], bank[:, :].rearrange("p (f d) -> p f d", f=2),
                                      xth[:, 4 + 2 * i:6 + 2 * i, :].bitcast(F32), ALU.subtract).then_inc(sem("mix_lo"), 1)
                dve.wait_ge(sem("tanh_ready"), 2 * (l + 1))
                dve.scalar_tensor_tensor(out=md[:, 2, :, :], in0=md[:, 1, :, :], scalar=1.0, in1=md[:, 0, :, :],
                                         op0=ALU.add, op1=ALU.mult).then_inc(sem("glu_prod"), 1)
                dve.wait_ge(sem("mix_hi"), 4 * (l + 1))
                dve.scalar_tensor_tensor(out=xtl[:, 0:2, :], in0=md[:, 2, :, :], scalar=0.5, in1=xth[:, 0:2, :].bitcast(F32),
                                         op0=ALU.mult, op1=ALU.subtract).then_inc(sem("mix_lo"), 1)

                def residual(nm, i, ahead):
                    c = chunk(nm)
                    lo_upto(end_pair(nm) + ahead)
                    dve.wait_ge(pair_used, FIRST[c] + PAIRS[c])
                    for t in range(TT):
                        dve.tensor_tensor(xres[:, t, 512 * i:512 * i + 512], PJ[BUF[c]][:, t, :],
                                          xres[:, t, 512 * i:512 * i + 512], ALU.add).then_inc(sem("resid"), 1)
                residual(f"out{l}_0", 0, 1)
                residual(f"out{l}_1", 1, RING)
                norm_scale(2 + 2 * l, xres)
                norm_lo(2 + 2 * l)

                def unit_taps(j):
                    c = chunk(f"up{l}_{j}")
                    n0 = 4 * (UNITS * l + j)
                    for tap, sh in ((1, 1), (0, 2)):
                        for i in range(4):
                            k = conv_col(l, j, i)
                            if tap == 1:
                                dve.wait_ge(sem("conv_a"), n0 + i // 2 * 2 + 2)
                            else:
                                dve.wait_ge(sem("conv_m"), n0 + i + 1)
                            dve.scalar_tensor_tensor(
                                out=acc[:, j % 2, i, sh:TOK],
                                in0=PJ[BUF[c]][:, i // 2, (i % 2) * TOK:(i % 2 + 1) * TOK - sh],
                                scalar=colv[:, k + tap:k + tap + 1], in1=acc[:, j % 2, i, sh:TOK],
                                op0=ALU.mult, op1=ALU.add).then_inc(sem("conv_m" if tap == 1 else "conv_d"), 1)

                def unit_lo(j):
                    dve.wait_ge(sem("ht_hi"), UNITS * l + j + 1)
                    dve.tensor_tensor(htl[:, 2 * j:2 * j + 2, :], gtd[:, j % 2, :, :], hth[:, 2 * j:2 * j + 2, :].bitcast(F32),
                                      ALU.subtract).then_inc(sem("ht_lo"), 1)

                for j in range(UNITS + 1):
                    if j < UNITS:
                        lo_upto(end_pair(f"up{l}_{j}") + 3)
                        unit_taps(j)
                        lo_upto(end_pair(f"up{l}_{j}") + 4)
                    if j > 0:
                        unit_lo(j - 1)
                residual(f"down{l}_0", 0, 1)
                residual(f"down{l}_1", 1, RING)
            if upto == 1:
                return

            norm_scale(5, xres)
            norm_lo(5)
            lo_upto(end_pair("mq") + 1)
            aco, asi = (cs(z).rearrange("p (t d) -> p t d", t=TT) for z in ("acos", "asin"))
            for i, (g, tb) in enumerate((("qn2", aco), ("qn2", asi), ("kn2", aco), ("kn2", asi))):
                dve.tensor_tensor(tabq[:, i, :, :], tb, wide(row(g), TT), ALU.mult).then_inc(sem("tabq_ready"), 1)
            lo_upto(end_pair("bq") + 1)

            def head_norm_rope(heads, squares_, source, sq_sem, n_sq, which, temp, outs, sems_):
                w = heads * HD
                dve.wait_ge(sem(sq_sem), n_sq)
                for t in range(TT):
                    m = dve.tensor_reduce(hss[:, heads * t:heads * t + heads], squares_(t).rearrange("p (g d) -> p g d", g=heads),
                                          AX.X, ALU.add)
                    if t == 0:
                        link(m)
                m.then_inc(sem("bhss_ready"), 1)
                dve.wait_ge(sem("bhr_ready"), which + 1)
                dve.wait_ge(sem("tabq_ready"), 4)
                for t in range(TT):
                    g8 = source(t).rearrange("p (g d) -> p g d", g=heads)
                    x8 = temp(t, 0).rearrange("p (g d) -> p g d", g=heads)
                    dve.tensor_tensor(x8, g8, wide(hr[:, which, heads * t:heads * t + heads], HD, 2), ALU.mult).then_inc(sem(sems_[0]), 1)
                dve.wait_ge(sem(sems_[0]), 2)
                for t in range(TT):
                    x8 = temp(t, 0).rearrange("p (g d) -> p g d", g=heads)
                    t8 = temp(t, 1).rearrange("p (g d) -> p g d", g=heads)
                    link(dve.tensor_tensor(t8, x8, wide(tabq[:, 2 * which + 1, t, :], heads), ALU.mult))
                    link(dve.tensor_tensor(x8, x8, wide(tabq[:, 2 * which, t, :], heads), ALU.mult))
                    x16 = temp(t, 0).rearrange("p (g d) -> p g d", g=2 * heads)
                    t16 = temp(t, 1).rearrange("p (g d) -> p g d", g=2 * heads)
                    for o in outs(t, x16, t16):
                        o16, xx, tt_ = o
                        dve.tensor_tensor(o16[:, :, 0:16], xx[:, :, 0:16], tt_[:, :, 16:32], ALU.subtract).then_inc(sem(sems_[1]), 1)
                        dve.tensor_tensor(o16[:, :, 16:32], xx[:, :, 16:32], tt_[:, :, 0:16], ALU.add).then_inc(sem(sems_[1]), 1)

            head_norm_rope(BH, lambda t: sm2[:, t, 0:512], lambda t: PJ[buf("bq")][:, t, :], "bsq_ready", 2, 0,
                           lambda t, i: xn[:, t, 512 * i:512 * i + 512],
                           lambda t, x, z: [(rt[:, t, :].rearrange("p (g d) -> p g d", g=16), x, z)],
                           ("bqn_ready", "brope_ready"))
            lo_upto(end_pair("bkv") + 1)

            def twice(t, x, z):
                out_ = []
                for h in range(2):
                    for c in range(2):
                        a = 256 + P * h + HD * c
                        out_.append((xn[:, t, a:a + HD].rearrange("p (g d) -> p g d", g=2), x[:, 2 * h:2 * h + 2, :], z[:, 2 * h:2 * h + 2, :]))
                return out_

            dve.wait_ge(sem("brope_ready"), 4)
            dve.wait_ge(sem("bv_ready"), 2)
            head_norm_rope(2, lambda t: pT2[:, t, 0, :], lambda t: PJ[buf("bkv")][:, t, 0:P], "bksq_ready", 2, 1,
                           lambda t, i: xn[:, t, P * i:P * i + P], twice, ("bkn_ready", "bkrope_ready"))

            def silu(nm, th):
                i = SILU_ORDER.index(nm)
                for t in range(TT):
                    dve.wait_ge(sem("th_ready"), 2 * i + t + 1)
                    dve.scalar_tensor_tensor(out=gat[:, i, t, :], in0=th[:, t, 0:512], scalar=1.0, in1=PJ[buf(nm)][:, t, :],
                                             op0=ALU.add, op1=ALU.mult).then_inc(sem("silu_ready"), 1)

            lo_upto(end_pair("gb") + 2)
            silu("gb", sm2)
            lo_upto(end_pair("gm") + 2)
            silu("gm", sm2)

            def rot_terms(c):
                nm = A_CHUNKS[c]
                dve.wait_ge(pair_used, end_pair(nm))
                if c:
                    dve.wait_ge(sem("a_rope"), 4 * c)
                else:
                    dve.wait_ge(sem("b_tr"), 2)
                for t in range(TT):
                    g8 = PJ[buf(nm)][:, t, :].rearrange("p (g d) -> p g d", g=8)
                    for i, tb in enumerate((cosv, sinv)):
                        o8 = xn[:, t, i * 512:(i + 1) * 512].rearrange("p (g d) -> p g d", g=8)
                        dve.tensor_tensor(o8, g8, wide(tb[:, t, :], 8), ALU.mult).then_inc(sem("rot_terms"), 1)

            for c, nm in enumerate(A_CHUNKS):
                for j in range(4):
                    n = 4 * c + j
                    lo_upto(F2 + n + 3)
                    if j == 0 and 1 <= c <= 6:
                        rot_terms(c - 1)
                    for k in bm_slots(n):
                        if k < len(BM):
                            br, h, t = BM[k]
                            dve.wait_ge(sem("bm_sc"), k + 1)
                            if k >= 4:
                                dve.wait_ge(sem("bm_out"), k - 3)
                            link(dve.tensor_reduce(sx[:, k % 4, 0:1], S0[:, 0:TOK], AX.X, ALU.max))
                            dve.tensor_scalar(sx[:, k % 4, 1:2], sx[:, k % 4, 0:1], -((HD if br == "b" else MD) ** -0.5), None,
                                              ALU.mult).then_inc(sem("bm_nb"), 1)
                        if k >= 1 and k - 1 < len(BM):
                            dve.wait_ge(sem("bm_exp"), k)
                            dve.reciprocal(sx[:, (k - 1) % 4, 3:4], sx[:, (k - 1) % 4, 2:3]).then_inc(sem("bm_rl"), 1)
                        if k >= 2:
                            k2 = k - 2
                            br, h, t = BM[k2]
                            w = HD if br == "b" else MD
                            o = gat[:, "bm".index(br), t, h * w:(h + 1) * w]
                            dve.wait_ge(sem("bm_pv"), k2 + 1)
                            dve.wait_ge(sem("bm_rl"), k2 + 1)
                            dve.scalar_tensor_tensor(out=o, in0=T1[:, 0:w], scalar=sx[:, k2 % 4, 3:4], in1=o,
                                                     op0=ALU.mult, op1=ALU.mult).then_inc(sem("bm_out"), 1)
            lo_upto(F3 + 2)
            silu("ga", rt)
            dve.wait_ge(sem("ma_landed"), 16)
            for n in range(24):
                lo_upto(F3 + n + 3)
                if n % 4 == 0 and n:
                    gate_sum(dve, n // 4 - 1)
                for k in a_slots(n):
                    if k < AH * TT:
                        h, t = divmod(k, TT)
                        dve.wait_ge(sem("a_sc"), k + 1)
                        if k >= 2:
                            dve.wait_ge(sem("a_ptr"), k - 1)
                        if k >= 4:
                            dve.wait_ge(sem("a_out"), k - 3)
                        mk = ma[:, t * TOK:].rearrange("p (g n) -> p g n", n=TOK)[:, 0:3 - t:2 - t, :]
                        dve.tensor_tensor_reduce(sm2[:, k % 2, 0:512].rearrange("p (g n) -> p g n", g=2),
                                                 S0[:, :].rearrange("p (g n) -> p g n", g=2), mk, 1.0, BIG, ALU.add, ALU.max,
                                                 sx[:, k % 4, 4:5]).then_inc(sem("a_max"), 1)
                        dve.tensor_tensor_reduce(sm2[:, k % 2, 512:768], S1[:, 0:TOK], ma[:, 3 * TOK:4 * TOK], 1.0, BIG, ALU.add,
                                                 ALU.max, sx[:, k % 4, 5:6]).then_inc(sem("a_max"), 1)
                        dve.wait_ge(sem("a_max"), 2 * k + 2)
                        link(dve.tensor_tensor(sx[:, k % 4, 0:1], sx[:, k % 4, 4:5], sx[:, k % 4, 5:6], ALU.max))
                        dve.tensor_scalar(sx[:, k % 4, 1:2], sx[:, k % 4, 0:1], -(HD ** -0.5), None, ALU.mult).then_inc(sem("a_nb"), 1)
                    if k >= 1 and k - 1 < AH * TT:
                        dve.wait_ge(sem("a_exp"), k)
                        dve.reciprocal(sx[:, (k - 1) % 4, 3:4], sx[:, (k - 1) % 4, 2:3]).then_inc(sem("a_rl"), 1)
                    if k >= 2:
                        h, t = divmod(k - 2, TT)
                        o = gat[:, 2, t, h * HD:(h + 1) * HD]
                        dve.wait_ge(sem("apv_done"), k - 1)
                        dve.wait_ge(sem("a_rl"), k - 1)
                        dve.scalar_tensor_tensor(out=o, in0=S1[:, TOK:TOK + HD], scalar=sx[:, (k - 2) % 4, 3:4], in1=o,
                                                 op0=ALU.mult, op1=ALU.mult).then_inc(sem("a_out"), 1)
            gate_sum(dve, 5)
            lo_upto(F3 + 24 + RING)
            for i in range(6):
                dve.wait_ge(sem("o_hi"), i + 1)
                dve.scalar_tensor_tensor(out=otl[:, 2 * i:2 * i + 2, :], in0=OBANKS[i % 4][:, :].rearrange("p (f n) -> p f n", f=2),
                                         scalar=0.5, in1=oth[:, 2 * i:2 * i + 2, :].bitcast(F32),
                                         op0=ALU.mult, op1=ALU.subtract).then_inc(sem("o_lo"), 1)
            for i, b in enumerate(BRANCH_ORDER):
                nm = "br" + b
                n = int(b[1])
                lo_upto(min(end_pair(nm) + 2, FIRST[chunk("wo0")] + 3))
                dve.wait_ge(pair_used, end_pair(nm))
                dve.wait_ge(sem("gate_ready"), 6)
                at_ = "abm".index(b[0]) * D + 512 * n
                for t in range(TT):
                    g = gt[:, t, at_:at_ + 512]
                    o = merged[:, t, 512 * n:512 * n + 512] if b[0] == "a" else g
                    dve.scalar_tensor_tensor(out=o, in0=g, scalar=1.0, in1=PJ[buf(nm)][:, t, :],
                                             op0=ALU.add, op1=ALU.mult).then_inc(sem("y_gated"), 1)
            for i in range(4):
                dve.wait_ge(sem("m_hi"), i + 1)
                dve.scalar_tensor_tensor(out=xtl[:, 2 * i:2 * i + 2, :], in0=AUX[i][:, :].rearrange("p (f n) -> p f n", f=2),
                                         scalar=0.5, in1=xth[:, 2 * i:2 * i + 2, :].bitcast(F32),
                                         op0=ALU.mult, op1=ALU.subtract).then_inc(sem("m_lo"), 1)
            for i in range(2):
                nm = f"wo{i}"
                lo_upto(end_pair(nm) + 1)
                dve.wait_ge(sem("ssq_ready"), 4 * 6 + 2 * i + 2)
                for t in range(TT):
                    dve.tensor_copy(xn[:, t, 512 * i:512 * i + 512], PJ[buf(nm)][:, t, :]).then_inc(sem("wo_ev"), 1)
            dve.wait_ge(sem("rstd_ready"), 7)
            dve.wait_ge(sem("gpost_landed"), 16)
            dve.wait_ge(sem("wo_ev"), 4)
            for t in range(TT):
                link(dve.scalar_tensor_tensor(out=xn[:, t, :], in0=xn[:, t, :], scalar=rstd[:, 6, t:t + 1], in1=gpost[:, :],
                                              op0=ALU.mult, op1=ALU.mult))
                dve.tensor_tensor(xn[:, t, :], xn[:, t, :], xres[:, t, :], ALU.add).then_inc(sem("y_ready"), 1)

def conv_col(l, j, i):
    tile = 2 * j + i % 2 + (FT if i >= 2 else 0)
    return COL["conv"][0] + (l * 2 * FT + tile) * 4


def rope_table(pos, half, width):
    inv = 10000.0 ** (-np.arange(half, dtype=np.float64) / half)
    a = pos[:, None] * inv[None, :]
    a = np.concatenate([a, a], axis=1)
    return np.cos(a), np.sin(a)


def by_partition(a):
    return np.ascontiguousarray(a.reshape(TT, P, -1).transpose(1, 0, 2).reshape(P, -1))


def constants():
    pos = np.arange(TOK)
    cos, sin = rope_table(pos, 32, 64)
    rc, rs = rope_table(pos // 64, 16, 32)
    cc, cs_ = rope_table(pos % 64, 16, 32)
    own = pos[:, None] // 64
    diff = np.where(pos[None, :] // 64 <= own, 0.0, NEG)
    parts = [np.eye(P), by_partition(cos), by_partition(sin), by_partition(np.concatenate([rc, cc], 1)),
             by_partition(np.concatenate([rs, cs_], 1)), diff[0:128, 0:128], diff[128:256, 0:256]]
    return np.concatenate(parts, axis=1).astype(np.float32)


def window_masks():
    q, k = np.arange(TOK)[:, None], np.arange(TOK)[None, :]
    near = np.abs(q - k) <= 64
    parts = [near[0:P], near[P:]] + [((q - k) % d == 0)[0:P] for d in (4, 16)]
    return np.where(np.concatenate(parts, axis=1), 0.0, NEG).astype(np.float32)


def layout(i):
    def cut(w, n):
        return w.reshape(w.shape[0] // P, P, w.shape[1])

    tiles = {}
    for l in range(LAYERS):
        w = i["w_in"][l]
        at = 0
        for nm, n in (("ssm_u", 256), ("gmlp", 512), ("q", 512), ("k", 512), ("v", 512)):
            tiles[f"{nm}{l}"] = w[:, at:at + n]
            at += n
        for j in range(2):
            tiles[f"out{l}_{j}"] = i["w_out"][l][:, 512 * j:512 * j + 512]
            tiles[f"down{l}_{j}"] = i["w_down"][l][:, 512 * j:512 * j + 512]
        for j in range(UNITS):
            up = i["w_up"][l]
            tiles[f"up{l}_{j}"] = np.concatenate([up[:, 256 * j:256 * j + 256], up[:, FF + 256 * j:FF + 256 * j + 256]], 1)
    w = i["w_in_2"][0]
    at = 0
    for nm, n in [(f"a{c}{g}", 512) for c in "qkv" for g in range(NG)] + \
            [("bq", 512), ("bkv", 256), ("mq", 512), ("ga", 512), ("gb", 512), ("gm", 512)] + [(f"mg{j}", 512) for j in range(6)]:
        tiles[nm] = w[:, at:at + n]
        at += n
    tiles["km"], tiles["vm"] = i["w_mem_kv_2"][0][:, 0:512], i["w_mem_kv_2"][0][:, 512:1024]
    for j in range(2):
        for b in "abm":
            tiles[f"br{b}{j}"] = i[f"w_br_{b}_2"][0][:, 512 * j:512 * j + 512]
        tiles[f"wo{j}"] = i["w_out_2"][0][:, 512 * j:512 * j + 512]
    weights = np.empty((NPAIRS, P, 1024), np.float32)
    for (nm, k, n), first, pairs in zip(CHUNKS, FIRST, PAIRS):
        per = 1024 // n
        weights[first:first + pairs] = tiles[nm].reshape(pairs, per, P, n).transpose(0, 2, 1, 3).reshape(pairs, P, 1024)

    cols = np.zeros((P, NCOL), np.float32)

    def put(name, a, at=0):
        a = a.reshape(-1, P).T
        cols[:, COL[name][0] + at:COL[name][0] + at + a.shape[1]] = a

    put("are", i["ssm_a_re"])
    put("aim", i["ssm_a_im"])
    put("ldt", np.repeat(i["ssm_log_dt"].reshape(-1), STATE))
    put("gattn", i["attn_norm_g"])
    put("gffn", i["ffn_norm_g"])
    put("dskip", i["ssm_d"])
    put("bglu", i["ssm_b_glu"])
    put("bs", i["gmlp_b_s"])
    put("gpre", i["g_pre_2"])
    put("gmem", i["g_mem_2"])
    conv = np.concatenate([i["conv_w"], i["conv_b"][:, None, :]], axis=1)
    put("conv", conv.reshape(LAYERS, 4, 2 * FT, P).transpose(0, 2, 1, 3))
    rows = np.zeros((1, NROW), np.float32)
    for name, src in (("vg", "gmlp_v_g"), ("qg", "q_norm_g"), ("kg", "k_norm_g"), ("sub", "subln_g"),
                      ("qn2", "q_norm_2"), ("kn2", "k_norm_2")):
        a, b = ROW[name]
        rows[0, a:b] = i[src].reshape(-1)
    bexp = np.zeros((LAYERS, P, 2, 2, P), np.float32)
    cexp = np.zeros((LAYERS, P, 2, ST, 32), np.float32)
    for c, (b, m) in enumerate((("ssm_b_re", "ssm_c_re"), ("ssm_b_im", "ssm_c_im"))):
        for g in range(GROUPS):
            s, half, ch = g // 2, (g % 2) * STATE, (g % 8) * GCH
            bexp[:, ch:ch + GCH, c, s // 4, half:half + STATE] = i[b][:, g].transpose(0, 2, 1)
            cexp[:, half:half + STATE, c, s, ch % 32:ch % 32 + GCH] = i[m][:, g].transpose(0, 2, 1)
    return {
        "weights": weights, "x": i["x"].reshape(TOK, D), "mem": i["mem_2"].reshape(TOK, D), "cols": cols, "rows": rows,
        "lams": np.concatenate([i[f"lambda_{z}"].reshape(1, -1) for z in ("q1", "k1", "q2", "k2")], axis=1),
        "bmerge": np.concatenate([i["b_merge_2"].reshape(1, -1), i["g_post_2"].reshape(1, -1)], axis=1),
        "consts": constants(), "amask": window_masks(), "bexp": bexp, "cexp": cexp,
        "wst": np.ascontiguousarray(i["gmlp_w_s"].transpose(0, 3, 1, 2)),
        "wglu": np.ascontiguousarray(i["ssm_w_glu"].reshape(LAYERS, 2, P, 256).transpose(0, 2, 1, 3)),
    }


def kernel(**inputs):
    import concourse.bacc as bacc
    from concourse.bass_utils import run_bass_kernel_spmd

    nc = bacc.Bacc("TRN2", target_bir_lowering=False, num_devices=1)
    arrays = {f"{k}_in": np.ascontiguousarray(v) for k, v in layout({k: np.asarray(v) for k, v in inputs.items()}).items()}
    args = {k[:-3]: nc.dram_tensor(k, a.shape, mybir.dt.from_np(a.dtype), kind="ExternalInput").ap() for k, a in arrays.items()}
    out = nc.dram_tensor("y_out", (TOK, D), F32, kind="ExternalOutput").ap()
    build(nc, out=out, **args)
    r = run_bass_kernel_spmd(nc, [arrays], core_ids=[0])
    return r.results[0]["y_out"].reshape(1, TOK, D)
```

```python
from contextlib import ExitStack
import math

import numpy as np
import concourse.bass as bass
from concourse import mybir

P = 128
TOK, TT = 256, 2
D, KD = 1024, 8
LAYERS = 2
GROUPS, GCH, STATE = 16, 16, 64
ST = GROUPS * STATE // P
QKD, VD, DH = 64, 128, 4
FF = 2816
FT = FF // P
UNITS = FT // 2
HD, AH, NG, BH, MH, MD = 64, 8, 3, 8, 4, 128
EPS = 1e-6
NEG = -1e30
BIG = -3.0e38
RAW, RING = 5, 5

F32, F32R = mybir.dt.float32, mybir.dt.float32r
ALU, ACT, AX = mybir.AluOpType, mybir.ActivationFunctionType, mybir.AxisListType
LAMBDA_INIT = [0.8 - 0.6 * math.exp(-0.3 * l) for l in range(LAYERS)]

CHUNKS = [("km", 8, 512), ("vm", 8, 512)]
for _l in range(LAYERS):
    CHUNKS += [(f"ssm_u{_l}", 8, 256), (f"q{_l}", 8, 512), (f"k{_l}", 8, 512), (f"gmlp{_l}", 8, 512),
               (f"v{_l}", 8, 512), (f"out{_l}_0", 8, 512), (f"out{_l}_1", 8, 512)]
    CHUNKS += [(f"up{_l}_{j}", 8, 512) for j in range(UNITS)]
    CHUNKS += [(f"down{_l}_0", FT, 512), (f"down{_l}_1", FT, 512)]
CHUNKS += [("mq", 8, 512), ("bq", 8, 512), ("gb", 8, 512), ("bkv", 8, 256), ("gm", 8, 512)]
CHUNKS += [(f"a{w}{g}", 8, 512) for w in "qkv" for g in range(NG)] + [("ga", 8, 512)]
CHUNKS += [(f"mg{i}", 8, 512) for i in range(6)]
CHUNKS += [(f"br{b}{n}", 4, 512) for n in range(2) for b in "bma"] + [("wo0", 8, 512), ("wo1", 8, 512)]
NAMES = [c[0] for c in CHUNKS]
PAIRS = [k * n // 1024 for _, k, n in CHUNKS]
FIRST = [sum(PAIRS[:i]) for i in range(len(CHUNKS))]
NPAIRS = sum(PAIRS)


OUT_PAIRS = (1, 2, 3, 0)


def chunk(name):
    return NAMES.index(name)


def end_pair(name):
    c = chunk(name)
    return FIRST[c] + PAIRS[c]


BRANCH_ORDER = [b + str(n) for n in range(2) for b in "bma"]
A_CHUNKS = [f"a{w}{g}" for w in "qkv" for g in range(NG)] + ["ga"]
SILU_ORDER = ["gb", "gm", "ga"]
EMPTIED = {"km": [("mem_ev", 2)], "vm": [("mem_ev", 4)], "mq": [("mq_ev", 2)], "bq": [("bqn_ready", 2)],
           "bkv": [("bkn_ready", 2), ("bv_ready", 2)]}
for _l in range(LAYERS):
    EMPTIED[f"ssm_u{_l}"] = [("u_ready", _l + 1)]
    EMPTIED[f"q{_l}"] = [("qn_ready", 4 * _l + 2)]
    EMPTIED[f"k{_l}"] = [("qn_ready", 4 * _l + 4)]
    EMPTIED[f"v{_l}"] = [("v_ready", 2 * _l + 2)]
    EMPTIED[f"gmlp{_l}"] = [("vn_ready", 2 * _l + 2), ("ug_ready", 2 * _l + 2)]
    for _n in range(2):
        EMPTIED[f"out{_l}_{_n}"] = [("resid", 8 * _l + 2 * _n + 2)]
        EMPTIED[f"down{_l}_{_n}"] = [("resid", 8 * _l + 4 + 2 * _n + 2)]
    for _j in range(UNITS):
        EMPTIED[f"up{_l}_{_j}"] = [("conv_d", 4 * (UNITS * _l + _j + 1))]
for _n in range(6):
    EMPTIED[A_CHUNKS[_n]] = [("rot_terms", 4 * _n + 4)]
    EMPTIED[f"mg{_n}"] = [("gate_sum", 2 * _n + 2)]
    EMPTIED["br" + BRANCH_ORDER[_n]] = [("y_gated", 2 * _n + 2)]
for _n in range(NG):
    EMPTIED[f"av{_n}"] = [("av_ready", 2 * _n + 2)]
    EMPTIED[SILU_ORDER[_n]] = [("silu_ready", 2 * _n + 2)]
BUF = []
for _n in NAMES:
    BUF.append(1 - BUF[-1] if BUF else 0)


def buf(name):
    return BUF[chunk(name)]


def spans(*items):
    at, out = 0, {}
    for name, n in items:
        out[name] = (at, at + n)
        at += n
    return out, at


COL, NCOL = spans(("are", 16), ("aim", 16), ("ldt", 16), ("gattn", 16), ("gffn", 16), ("dskip", 4),
                  ("bglu", 4), ("bs", 8), ("gpre", 8), ("gmem", 8), ("conv", LAYERS * 2 * FT * 4))
ROW, NROW = spans(("vg", 512), ("qg", 128), ("kg", 128), ("sub", 256), ("qn2", 64), ("kn2", 64))
LAM, NLAM = spans(("lq1", 128), ("lk1", 128), ("lq2", 128), ("lk2", 128))
CST, NCST = spans(("ident", 128), ("cos", 128), ("sin", 128), ("acos", 128), ("asin", 128),
                  ("mdiff", 384))


def build(nc, weights, x, mem, cols, rows, lams, bmerge, consts, amask, bexp, cexp, wst, wglu, out):
    with ExitStack() as ctx:
        def sbt(stack, name, shape, dt=F32):
            return stack.enter_context(nc.sbuf_tensor(name, shape, dt))

        sems = {}

        def sem(name):
            if name not in sems:
                sems[name] = ctx.enter_context(nc.semaphore(name))
            return sems[name]

        raw = sbt(ctx, "raw", [P, RAW, 1024])
        whi = sbt(ctx, "whi", [P, RING, 1024], F32R)
        wlo = sbt(ctx, "wlo", [P, RING, 1024], F32R)
        xres = sbt(ctx, "xres", [P, TT, D])
        xn = sbt(ctx, "xn", [P, TT, D])
        xth = sbt(ctx, "xth", [P, KD, TOK], F32R)
        xtl = sbt(ctx, "xtl", [P, KD, TOK], F32R)
        kmT = sbt(ctx, "kmT", [P, MH, TOK])
        vm = sbt(ctx, "vm", [P, TT, 512])
        colv = sbt(ctx, "colv", [P, NCOL])
        rowv = sbt(ctx, "rowv", [P, NROW])
        cst = sbt(ctx, "cst", [P, NCST])
        ssq = sbt(ctx, "ssq", [P, 8, 4])
        ssm1 = sbt(ctx, "ssm1", [P, 8, 2])
        rstd = sbt(ctx, "rstd", [P, 8, 2])
        mhalf = sbt(ctx, "mhalf", [P, 16])
        sqs = sbt(ctx, "sqs", [P, 512], mybir.dt.bfloat16)
        gss = sbt(ctx, "gss", [P, LAYERS, TT])
        gr = sbt(ctx, "gr", [P, LAYERS, TT])
        hss = sbt(ctx, "hss", [P, 16])
        hr = sbt(ctx, "hr", [P, 2, 16])
        sqs2 = sbt(ctx, "sqs2", [P, 64])
        hb = sbt(ctx, "hb", [P, 4])
        nlam = sbt(ctx, "nlam", [P, LAYERS])
        lamv = sbt(ctx, "lamv", [P, 8])

        def col(name, i=0, n=None):
            a, b = COL[name]
            return colv[:, a + i:(a + i + n) if n else b]

        def row(name, i=0, n=None):
            a, b = ROW[name]
            return rowv[:, a + i:(a + i + n) if n else b]

        def cs(name):
            a, b = CST[name]
            return cst[:, a:b]

        ident = cs("ident")

        def wide(ap, n, dim=1):
            a = ap.unsqueeze(dim)
            shape = list(a.shape)
            shape[dim] = n
            return a.to_broadcast(shape)

        one = ExitStack()
        ctx.enter_context(one)
        bex = sbt(one, "bex", [P, 2, 2, P])
        cex = sbt(one, "cex", [P, 2, ST, 32])
        sp_ = sbt(one, "sp_", [P, 24, 16])
        ropeq = sbt(one, "ropeq", [P, 4, TT, QKD])
        identb = sbt(one, "identb", [P, P], mybir.dt.bfloat16)
        maskb = sbt(one, "maskb", [P, TT, 512], mybir.dt.bfloat16)
        tab = sbt(one, "tab", [P, 2, ST, TOK])
        wglus = sbt(one, "wglus", [P, 2, 256])
        wsts = sbt(one, "wsts", [P, 4, P])
        pw = sbt(one, "pw", [P, 5, ST])
        pow16 = sbt(one, "pow16", [P, 2, ST, 16])
        pow1 = sbt(one, "pow1", [P, 2, ST, 16])
        tq = sbt(one, "tq", [P, 4, ST, 8])
        mix = ExitStack()
        one.enter_context(mix)
        bu = sbt(mix, "bu", [P, ST, 2, TOK])
        mp = sbt(mix, "mp", [P, 2, 2, TOK])
        md = sbt(mix, "md", [P, 3, 2, TOK])
        uT = sbt(mix, "uT", [P, 2, TOK])
        qT = sbt(mix, "qT", [P, DH, TOK])
        kT = sbt(mix, "kT", [P, DH, TOK])
        v_sb = sbt(mix, "v_sb", [P, TT, 512])
        qn = sbt(mix, "qn", [P, TT, 512])
        hsq = sbt(mix, "hsq", [P, TT, 512])
        ug = sbt(mix, "ug", [P, TT, 256])
        sm = sbt(mix, "sm", [P, 2, 2, 512])
        pT = sbt(mix, "pT", [P, 2, 4, P])
        st_ = sbt(mix, "st_", [P, 3, 8, 4])
        mix.close()
        ffs = ExitStack()
        one.enter_context(ffs)
        hth = sbt(ffs, "hth", [P, FT, TOK], F32R)
        htl = sbt(ffs, "htl", [P, FT, TOK], F32R)
        acc = sbt(ffs, "acc", [P, 2, 4, TOK])
        gtd = sbt(ffs, "gtd", [P, 2, 2, TOK])
        ffs.close()
        one.close()

        two = ExitStack()
        ctx.enter_context(two)
        sm2 = sbt(two, "sm2", [P, 2, NG * TOK])
        pT2 = sbt(two, "pT2", [P, 2, 2 * NG, P])
        rt = sbt(two, "rt", [P, TT, 512])
        brow = rt
        gat = sbt(two, "gat", [P, 3, TT, 512])
        ma = sbt(two, "ma", [P, 4 * TOK])
        sx = sbt(two, "sx", [P, 4, 8])
        tabq = sbt(two, "tabq", [P, 4, TT, HD])
        bm = ExitStack()
        two.enter_context(bm)
        bqT = sbt(bm, "bqT", [P, 4, TOK])
        bkT = sbt(bm, "bkT", [P, 2, TOK])
        bv = sbt(bm, "bv", [P, TT, P])
        mqT = sbt(bm, "mqT", [P, MH, TOK])
        bm.close()
        gt = sbt(two, "gt", [P, TT, 3 * D])
        att = ExitStack()
        two.enter_context(att)
        aqT = sbt(att, "aqT", [P, 2, NG, 4, TOK])
        va = sbt(att, "va", [P, NG, TT, 512])
        att.close()
        oth = sbt(two, "oth", [P, 12, TOK], F32R)
        otl = sbt(two, "otl", [P, 12, TOK], F32R)
        merged = sbt(two, "merged", [P, TT, D])
        gpost = sbt(two, "gpost", [P, D])
        two.close()

        PJ = [ctx.enter_context(nc.psum_tensor(f"PJ{i}", [P, TT, 512], F32)) for i in range(2)]
        S0, S1, T0, T1 = (ctx.enter_context(nc.psum_tensor(n, [P, 512], F32)) for n in ("S0", "S1", "T0", "T1"))
        AUX = [S0, S1, T0, T1]
        OBANKS = [S0, T0, T1, S1]

        raw_landed = [sem(f"raw_landed{i}") for i in range(RAW)]
        hi_ready, lo_ready, pair_used = sem("hi_ready"), sem("lo_ready"), sem("pair_used")
        block = ctx.enter_context(nc.Block())

        NORM_GAIN = [("gmem", 0), ("gattn", 0), ("gffn", 0), ("gattn", 8), ("gffn", 8), ("gpre", 0)]

        def md_vn(h):
            return xn[:, :, 768 + h * 64:768 + (h + 1) * 64]

        def md_g(k):
            return md[:, 0, k, :]

        def merge_tanh(act, i):
            act.wait_ge(sem("gate_sum"), 2 * i + 2)
            act.activation(gt[:, :, 512 * i:512 * i + 512], gt[:, :, 512 * i:512 * i + 512], ACT.Tanh,
                           scale=0.5).then_inc(sem("gate_ready"), 1)

        def gate_sum(dve, i):
            nm = f"mg{i}"
            dve.wait_ge(pair_used, end_pair(nm))
            dve.wait_ge(sem(f"brow_landed{i % 2}"), 16 * (i // 2 + 1))
            for t in range(TT):
                dve.tensor_tensor(gt[:, t, 512 * i:512 * i + 512], PJ[buf(nm)][:, t, :], brow[:, i % 2, :],
                                  ALU.add).then_inc(sem("gate_sum"), 1)

        def table_base(eng, link, l):
            lo8 = slice(8 * l, 8 * l + 8)
            link(eng.tensor_copy(pw[:, 0, :], sp_[:, 8, lo8]))
            link(eng.tensor_copy(pw[:, 1, :], sp_[:, 6, lo8]))

        def table_factor(eng, link, tt_):
            link(eng.memset(tt_[:, 0, :, 0:1], 1.0))
            link(eng.memset(tt_[:, 1, :, 0:1], 0.0))
            n = 1
            while n < 16:
                known = tt_[:, :, :, 0:n]
                C, S = (wide(wide(pw[:, i, :], n, 2), 2) for i in range(2))
                link(eng.tensor_tensor(tq[:, 0:2, :, 0:n], known, C, ALU.mult), False)
                link(eng.tensor_tensor(tq[:, 2:4, :, 0:n], known, S, ALU.mult), False)
                link(eng.tensor_tensor(pw[:, 2:4, :], pw[:, 0:2, :], wide(pw[:, 0, :], 2), ALU.mult), False)
                link(eng.tensor_tensor(pw[:, 4, :], pw[:, 1, :], pw[:, 1, :], ALU.mult))
                link(eng.tensor_tensor(tt_[:, 0, :, n:2 * n], tq[:, 0, :, 0:n], tq[:, 3, :, 0:n], ALU.subtract), False)
                link(eng.tensor_tensor(tt_[:, 1, :, n:2 * n], tq[:, 1, :, 0:n], tq[:, 2, :, 0:n], ALU.add), False)
                link(eng.tensor_tensor(pw[:, 0, :], pw[:, 2, :], pw[:, 4, :], ALU.subtract), False)
                link(eng.tensor_tensor(pw[:, 1, :], pw[:, 3, :], pw[:, 3, :], ALU.add))
                n *= 2

        def table_product(eng, s, tmp, ready, n):
            av = [wide(pow16[:, i, s:s + 2, :], 16, 3) for i in range(2)]
            bv_ = [wide(pow1[:, i, s:s + 2, :], 16, 2) for i in range(2)]
            o = [tab[:, i, s:s + 2, :].rearrange("p s (a b) -> p s a b", a=16) for i in range(2)]
            for k, first, second, op in ((0, (av[0], bv_[0]), (av[1], bv_[1]), ALU.subtract),
                                         (1, (av[1], bv_[0]), (av[0], bv_[1]), ALU.add)):
                eng.tensor_tensor(o[k], *first, ALU.mult).then_inc(sem(ready + "_p"), 1)
                eng.tensor_tensor(tmp[:, k], *second, ALU.mult).then_inc(sem(ready + "_p"), 1)
                eng.wait_ge(sem(ready + "_p"), 4 * n + 2 * k + 2)
                eng.tensor_tensor(o[k], o[k], tmp[:, k], op).then_inc(sem(ready), 1)
            eng.wait_ge(sem(ready), 2 * n + 2)

        def fold_coefficient(eng, link, l, cf):
            eng.wait_ge(sem("cex_landed"), 16 * (l + 1))
            cr, ci, nci, ncr = (wide(sp_[:, r, 8 * l:8 * l + 8], 32, 2) for r in (9, 10, 11, 12))
            re, im = cex[:, 0, :, :], cex[:, 1, :, :]
            for o, (i_, k) in enumerate(((re, cr), (im, nci), (re, nci), (im, ncr))):
                link(eng.tensor_tensor(cf[:, o, :, :], i_, k, ALU.mult))
            eng.tensor_tensor(re, cf[:, 0, :, :], cf[:, 1, :, :], ALU.add).then_inc(sem("cex_ready"), 1)
            eng.tensor_tensor(im, cf[:, 2, :, :], cf[:, 3, :, :], ALU.add).then_inc(sem("cex_ready"), 1)

        @block.sync
        def _(sp):
            def small(dst, src, s):
                sp.dma_start(dst, src).then_inc(sem(s), 16)

            for t in range(TT):
                small(xn[:, t, :], mem[t * P:(t + 1) * P, :], f"mem_landed{t}")
            small(cst[:], consts, "cst_landed")
            small(colv[:], cols, "col_landed")
            for p in range(NPAIRS):
                if p >= RAW:
                    sp.wait_ge(lo_ready, p - RAW + 1)
                sp.dma_start(raw[:, p % RAW, :], weights[p]).then_inc(raw_landed[p % RAW], 16)
                if p == 2:
                    small(xres[:], x.rearrange("(t p) d -> p t d", p=P), "x_landed")
                if p == 3:
                    small(rowv[:], rows.to_broadcast([P, NROW]), "row_landed")
                    small(bu[:, 0, :, :].rearrange("p c t -> p (c t)"), lams.to_broadcast([P, NLAM]), "lam_landed")
                    small(bex[:], bexp[0], "bex_landed")
                    small(cex[:], cexp[0], "cex_landed")
                    small(wsts[:], wst[0], "wst_landed")
                    small(wglus[:], wglu[0], "wglu_landed")
                if p == FIRST[chunk("up0_0")] + 6:
                    for s in ("y_done", "glu_done", "sgu_done"):
                        sp.wait_ge(sem(s), 1)
                    small(bex[:], bexp[1], "bex_landed")
                    small(cex[:], cexp[1], "cex_landed")
                    small(wsts[:], wst[1], "wst_landed")
                    small(wglus[:], wglu[1], "wglu_landed")
                if p == FIRST[chunk("gb")]:
                    sp.wait_ge(pair_used, end_pair("down1_1"))
                    small(ma[:], amask, "ma_landed")
                for i in range(6):
                    if p == (FIRST[chunk("mg1")] + 3 if i < 2 else FIRST[chunk(f"mg{i}")] + 2):
                        if i >= 2:
                            sp.wait_ge(sem("gate_sum"), 2 * i - 2)
                        else:
                            sp.wait_ge(sem("silu_ready"), 6)
                        small(brow[:, i % 2, :], bmerge[:, 512 * i:512 * i + 512].to_broadcast([P, 512]), f"brow_landed{i % 2}")
            sp.wait_ge(sem("apv_done"), 16)
            small(gpost[:], bmerge[:, 3 * D:4 * D].to_broadcast([P, D]), "gpost_landed")
            for t in range(TT):
                for i in range(2):
                    sp.wait_ge(sem("y_ready"), 2 * t + i + 1)
                    sp.dma_start(out[t * P:(t + 1) * P, 512 * i:512 * i + 512], xn[:, t, 512 * i:512 * i + 512])\
                      .then_inc(sem("out_stored"), 16)
            sp.wait_ge(sem("out_stored"), 64)

        POOL_POST = (2, 3, 4, 5, 6)

        def post_rotate(eng, l, s, products):
            mine = [x for x in range(ST) if (x in POOL_POST) == (s in POOL_POST)]
            name = "state_ready_pool" if s in POOL_POST else "state_ready"
            before = len(mine) * l + mine.index(s)
            if before:
                eng.wait_ge(sem(name), 2 * before)
            cc, ss = wide(tab[:, 0, s, :], 2), wide(tab[:, 1, s, :], 2)
            eng.tensor_tensor(products[:, 0, :, :], bu[:, s, :, :], cc, ALU.mult).then_inc(sem(name + "_p"), 1)
            eng.tensor_tensor(products[:, 1, :, :], bu[:, s, :, :], ss, ALU.mult).then_inc(sem(name + "_p"), 1)
            eng.wait_ge(sem(name + "_p"), 2 * before + 2)
            eng.tensor_tensor(bu[:, s, 0, :], products[:, 0, 0, :], products[:, 1, 1, :], ALU.subtract).then_inc(sem(name), 1)
            eng.tensor_tensor(bu[:, s, 1, :], products[:, 0, 1, :], products[:, 1, 0, :], ALU.add).then_inc(sem(name), 1)

        DB = [(0, (0, 1, 2, 3)), (1, (0, 1)), (1, (2, 3))]
        DBANKS = [(S0, S1), (T0, T1), (S0, S1)]
        EXPS = [8, 12, 16]

        BM = [("b", h, t) for h in range(BH) for t in range(TT)] + [("m", h, t) for h in range(MH) for t in range(TT)]
        F2, F3 = FIRST[chunk("aq0")], FIRST[chunk("mg0")]

        def bm_slots(n):
            return [k for k in range(len(BM) + 2) if 1 + 3 * k // 2 == n]

        def a_slots(n):
            return [k for k in range(AH * TT + 2) if 4 * k // 3 == n]

        @block.tensor
        def _(pe):
            def last_pairs(name, j0, ks, xh, xl):
                c = chunk(name)
                for t in range(TT):
                    for j in range(j0, PAIRS[c]):
                        p = FIRST[c] + j
                        if t == 0:
                            pe.wait_ge(hi_ready, p + 1)
                            pe.wait_ge(lo_ready, p + 1)
                        for kk in range(2):
                            k = 2 * ks[j] + kk
                            wh, wl = (w[:, p % RING, kk * 512:(kk + 1) * 512] for w in (whi, wlo))
                            o = PJ[BUF[c]][:, t, :]
                            h, lw = xh[:, k, t * P:(t + 1) * P], xl[:, k, t * P:(t + 1) * P]
                            last = j == PAIRS[c] - 1 and kk == 1
                            pe.matmul(o, h, wh, start=(j == 0 and kk == 0), stop=False, skip_group_check=True)
                            pe.matmul(o, h, wl, start=False, stop=False, skip_group_check=True)
                            m = pe.matmul(o, lw, wh, start=False, stop=last, skip_group_check=True)
                        if t == 1:
                            m.then_inc(pair_used, 1)
                    if t == 0:
                        m.then_inc(sem("tile0_done"), 1)

            def pair_products(p, kt0, banks, fm, xh, xl, cw, is_first, is_last):
                r = p % RING
                n_k = 1024 // cw
                pe.wait_ge(hi_ready, p + 1)
                pe.wait_ge(lo_ready, p + 1)
                for kk in range(n_k):
                    k = kt0 + kk
                    first, last = is_first and kk == 0, is_last and kk == n_k - 1
                    wh, wl = whi[:, r, kk * cw:(kk + 1) * cw], wlo[:, r, kk * cw:(kk + 1) * cw]
                    if fm:
                        for f in range(cw // P):
                            o = banks[f // 2][:, (f % 2) * TOK:(f % 2 + 1) * TOK]
                            a, b = wh[:, f * P:(f + 1) * P], wl[:, f * P:(f + 1) * P]
                            pe.matmul(o, a, xh[:, k, :], start=(first and f % 2 == 0), stop=False, skip_group_check=True)
                            pe.matmul(o, a, xl[:, k, :], start=False, stop=False, skip_group_check=True)
                            m = pe.matmul(o, b, xh[:, k, :], start=False, stop=last, skip_group_check=True)
                    else:
                        for t in range(TT):
                            o = banks[t][:, 0:cw]
                            h, lw = xh[:, k, t * P:(t + 1) * P], xl[:, k, t * P:(t + 1) * P]
                            pe.matmul(o, h, wh, start=first, stop=False, skip_group_check=True)
                            pe.matmul(o, h, wl, start=False, stop=False, skip_group_check=True)
                            m = pe.matmul(o, lw, wh, start=False, stop=last, skip_group_check=True)
                return m

            def project(name, fm=False, xh=xth, xl=xtl, ready=None, pairs=None, order=None):
                c = chunk(name)
                _, n_k, cw = CHUNKS[c]
                banks = [PJ[BUF[c]][:, 0, :], PJ[BUF[c]][:, 1, :]]
                before = [i for i in range(c) if BUF[i] == BUF[c]]
                per = 1024 // cw
                for j in (range(PAIRS[c]) if pairs is None else pairs):
                    if j == 0 and before:
                        for s, n in EMPTIED[NAMES[before[-1]]]:
                            pe.wait_ge(sem(s), n)
                    if ready:
                        pe.wait_ge(ready[0], ready[1] + (j + 1) * ready[2])
                    m = pair_products(FIRST[c] + j, (order[j] if order else j) * per, banks, fm, xh, xl, cw,
                                      j == 0, j == PAIRS[c] - 1)
                    m.then_inc(pair_used, 1)

            def norm_transposes(n):
                if n == 0:
                    pe.wait_ge(sem("cst_landed"), 16)
                if n >= 1:
                    pe.wait_ge(sem("xt_lo"), 8 * n)
                if n >= 2:
                    aux_free_before_norm(n)
                for t in range(TT):
                    pe.wait_ge(sem("xn_ready"), 2 * n + t + 1)
                    for f in range(KD):
                        o = AUX[f // 2][:, (f % 2) * TOK + t * P:(f % 2) * TOK + (t + 1) * P]
                        m = pe.transpose(o, xn[:, t, f * P:(f + 1) * P], ident)
                        if t == 1 and f % 2 == 1:
                            m.then_inc(sem("xt_tr"), 1)

            def aux_free_before_norm(n):
                if n in (2, 4):
                    l = n // 2 - 1
                    pe.wait_ge(sem("mix_lo"), 4 * (l + 1))

            norm_transposes(0)
            project("km", fm=True, ready=(sem("xt_lo"), 0, 2))
            project("vm")
            norm_transposes(1)

            for l in range(LAYERS):
                if l > 0:
                    norm_transposes(1 + 2 * l)
                xt = (sem("xt_lo"), 8 * (1 + 2 * l), 4)
                project(f"ssm_u{l}", fm=True, ready=xt)
                pe.wait_ge(sem("bex_landed"), 16 * (l + 1))
                pe.wait_ge(sem("u_ready"), l + 1)
                pe.wait_ge(sem("xt_lo"), 8 * (2 + 2 * l))
                for s in range(ST):
                    if s >= 4:
                        pe.wait_ge(sem("bu_ready"), ST * l + s - 3)
                    q = slice(32 * (s % 4), 32 * (s % 4) + 32)
                    for c in range(2):
                        m = pe.matmul(AUX[s % 4][:, c * TOK:(c + 1) * TOK], bex[q, c, s // 4, :], uT[q, s // 4, :],
                                      start=(c == 0), stop=True, skip_group_check=True)
                    m.then_inc(sem("bu_done"), 1)
                    if s % 2:
                        project(f"q{l}", pairs=[s // 2])
                project(f"k{l}")

                def head_transposes(which, banks):
                    pe.wait_ge(sem("bu_ready"), ST * (l + 1))
                    pe.wait_ge(sem("rope_ready"), 4 * (2 * l + which + 1))
                    for h in range(DH):
                        for t in range(TT):
                            o = banks[h // 2][:, (h % 2) * TOK + t * P:(h % 2) * TOK + (t + 1) * P]
                            m = pe.transpose(o, xn[:, t, which * 512 + h * P:which * 512 + (h + 1) * P], ident)
                    m.then_inc(sem("qk_tr"), 1)

                head_transposes(0, (S0, S1))
                project(f"gmlp{l}")
                project(f"v{l}", pairs=[0])
                head_transposes(1, (T0, T1))
                project(f"v{l}", pairs=[1])

                def scores(b):
                    t, heads = DB[b]
                    n = P * (t + 1)
                    if b == 2:
                        pe.wait_ge(sem("da_exp"), 16 * l + EXPS[0])
                    for c, bank in enumerate(DBANKS[b]):
                        pe.matmul(bank[:, :], identb[:, :], maskb[:, t, :], start=True, stop=False, skip_group_check=True)
                    for i, h in enumerate(heads):
                        for c, bank in enumerate(DBANKS[b]):
                            m = pe.matmul(bank[:, i * n:(i + 1) * n], qT[c * QKD:(c + 1) * QKD, h, t * P:(t + 1) * P],
                                          kT[c * QKD:(c + 1) * QKD, h, 0:n], start=False, stop=True, skip_group_check=True)
                    m.then_inc(sem("da_sc"), 1)

                def pt_bank(b):
                    return S1 if b == 2 else PJ[buf(f"gmlp{l}")][:, b, :]

                def prob_transposes(b):
                    pe.wait_ge(sem("da_w"), 8 * l + (4, 6, 8)[b])
                    if b == 2:
                        pe.wait_ge(sem("da_exp"), 16 * (l + 1))
                    for i in range(4):
                        m = pe.transpose(pt_bank(b)[:, i * P:(i + 1) * P], sm[:, b % 2, 1, i * P:(i + 1) * P], ident)
                    m.then_inc(sem("da_tr"), 1)

                def values(b):
                    t, heads = DB[b]
                    pe.wait_ge(sem("da_pt"), 3 * l + b + 1)
                    for i, h in enumerate(heads):
                        for k in range(t + 1):
                            m = pe.matmul(PJ[buf(f"v{l}")][:, t, h * VD:(h + 1) * VD], pT[:, b % 2, i * (t + 1) + k, :],
                                          v_sb[:, k, h * VD:(h + 1) * VD], start=(k == 0), stop=(k == t), skip_group_check=True)
                    m.then_inc(sem("da_pv"), 1)

                pe.wait_ge(sem("qk_ev"), 4 * (l + 1))
                if l == 0:
                    pe.wait_ge(sem("maskb_ready"), 3)
                scores(0)
                scores(1)
                project(f"v{l}", pairs=[2, 3])
                scores(2)
                for s, n in EMPTIED[f"gmlp{l}"]:
                    pe.wait_ge(sem(s), n)
                prob_transposes(0)
                pe.wait_ge(sem("wst_ready"), l + 1)
                pe.wait_ge(sem("da_exp"), 16 * l + EXPS[1])
                for h in range(4):
                    m = pe.matmul(T0[:, h * P:(h + 1) * P], wsts[:, h, :], md_vn(h), start=(h == 0), stop=True,
                                  skip_group_check=True)
                m.then_inc(sem("sgu_done"), 1)
                for s, n in EMPTIED[f"v{l}"]:
                    pe.wait_ge(sem(s), n)
                values(0)
                prob_transposes(1)

                def c_products(ct):
                    pe.wait_ge(sem("cex_ready"), 2 * (l + 1))
                    for j in range(4):
                        s = 4 * ct + j
                        mine = [x for x in range(ST) if (x in POOL_POST) == (s in POOL_POST)]
                        pe.wait_ge(sem("state_ready_pool" if s in POOL_POST else "state_ready"), 2 * (len(mine) * l + mine.index(s) + 1))
                        for c in range(2):
                            m = pe.matmul(T1[32 * j:32 * j + 32, ct * TOK:(ct + 1) * TOK], cex[:, c, s, :], bu[:, s, c, :],
                                          start=(c == 0), stop=(c == 1), skip_group_check=True)
                    return m

                c_products(0)
                values(1)
                pe.wait_ge(sem("da_exp"), 16 * (l + 1))
                pe.wait_ge(sem("sgu_ready"), 4 * (l + 1))
                for f in range(2):
                    for t in range(TT):
                        m = pe.transpose(S0[:, f * TOK + t * P:f * TOK + (t + 1) * P], xn[:, t, 512 + f * P:512 + (f + 1) * P], ident)
                m.then_inc(sem("mix_tr"), 1)
                prob_transposes(2)
                values(2)
                out_terms = dict(ready=(sem("mix_lo"), 4 * l, 1), order=OUT_PAIRS)
                project(f"out{l}_0", pairs=[0], **out_terms)
                c_products(1).then_inc(sem("y_done"), 1)
                pe.wait_ge(sem("diff_ready"), 8 * (l + 1))
                for f in range(4):
                    for t in range(TT):
                        bank = (S1, T0)[f // 2]
                        m = pe.transpose(bank[:, (f % 2) * TOK + t * P:(f % 2) * TOK + (t + 1) * P],
                                         xn[:, t, f * P:(f + 1) * P], ident)
                m.then_inc(sem("mix_tr"), 1)
                pe.wait_ge(sem("wglu_landed"), 16 * (l + 1))
                pe.wait_ge(sem("gelu_ready"), 2 * (l + 1))
                for f in range(2):
                    for k in range(2):
                        m = pe.matmul(S0[:, f * TOK:(f + 1) * TOK], wglus[:, k, f * P:(f + 1) * P], md_g(k),
                                      start=(f == 0 and k == 0), stop=(k == 1), skip_group_check=True)
                m.then_inc(sem("glu_done"), 1)
                project(f"out{l}_0", pairs=[1, 2, 3], **out_terms)
                before = [i for i in range(chunk(f"out{l}_1")) if BUF[i] == buf(f"out{l}_1")][-1]
                for s, n in EMPTIED[NAMES[before]]:
                    pe.wait_ge(sem(s), n)
                last_pairs(f"out{l}_1", 0, OUT_PAIRS, xth, xtl)
                norm_transposes(2 + 2 * l)
                xt = (sem("xt_lo"), 8 * (2 + 2 * l), 2)
                for j in range(UNITS):
                    project(f"up{l}_{j}", fm=True, ready=xt)
                for i in range(2):
                    project(f"down{l}_{i}", xh=hth, xl=htl, ready=None if i else (sem("ht_lo"), UNITS * l, 1),
                            pairs=range(FT // 2 - 4 * i))
                last_pairs(f"down{l}_1", FT // 2 - 4, range(FT // 2), hth, htl)

            norm_transposes(5)
            project("mq", fm=True, ready=(sem("xt_lo"), 40, 2))
            project("bq")
            project("gb")
            pe.wait_ge(sem("brope_ready"), 4)
            for f in range(4):
                for t in range(TT):
                    m = pe.transpose((T0, T1)[f // 2][:, (f % 2) * TOK + t * P:(f % 2) * TOK + (t + 1) * P],
                                     rt[:, t, f * P:(f + 1) * P], ident)
            m.then_inc(sem("b_tr"), 1)
            project("bkv")
            project("gm")
            pe.wait_ge(sem("bkrope_ready"), 16)
            for f in range(2):
                for t in range(TT):
                    m = pe.transpose(S0[:, f * TOK + t * P:f * TOK + (t + 1) * P], xn[:, t, 256 + f * P:256 + (f + 1) * P], ident)
            m.then_inc(sem("b_tr"), 1)

            def bm_scores(k):
                br, h, t = BM[k]
                if k:
                    pe.wait_ge(sem("bm_exp"), k)
                if br == "b":
                    a, b = (h % 2) * HD, (h % 2 + 1) * HD
                    m = pe.matmul(S0[:, 0:TOK], bqT[a:b, h // 2, t * P:(t + 1) * P], bkT[a:b, h // 4, :], start=True, stop=True)
                else:
                    m = pe.matmul(S0[:, 0:TOK], mqT[:, h, t * P:(t + 1) * P], kmT[:, h, :], start=True, stop=True)
                m.then_inc(sem("bm_sc"), 1)

            def bm_transposes(k):
                pe.wait_ge(sem("bm_exp"), k + 1)
                if k:
                    pe.wait_ge(sem("bm_pt"), k)
                for i in range(2):
                    m = pe.transpose(T0[:, i * P:(i + 1) * P], sm2[:, k % 2, i * P:(i + 1) * P], ident)
                m.then_inc(sem("bm_tr"), 1)

            def bm_values(k):
                br, h, t = BM[k]
                pe.wait_ge(sem("bm_pt"), k + 1)
                if k:
                    pe.wait_ge(sem("bm_out"), k)
                for i in range(2):
                    v = bv[:, i, (h // 4) * HD:(h // 4 + 1) * HD] if br == "b" else vm[:, i, h * MD:(h + 1) * MD]
                    m = pe.matmul(T1[:, 0:HD if br == "b" else MD], pT2[:, k % 2, i, :], v, start=(i == 0), stop=(i == 1))
                m.then_inc(sem("bm_pv"), 1)

            pe.wait_ge(sem("b_ev"), 3)
            pe.wait_ge(sem("bv_ready"), 2)
            pe.wait_ge(sem("mq_ev"), 2)
            for c, nm in enumerate(A_CHUNKS):
                for j in range(4):
                    project(nm, pairs=[j])
                    if 1 <= c <= 6 and j >= 2:
                        rnd = 2 * (c - 1) + j - 2
                        pe.wait_ge(sem("a_rope"), 4 * c)
                        if rnd:
                            pe.wait_ge(sem("a_ev"), rnd)
                        for i in range(2):
                            f = 2 * (j - 2) + i
                            for t in range(TT):
                                m = pe.transpose(S1[:, i * TOK + t * P:i * TOK + (t + 1) * P], rt[:, t, f * P:(f + 1) * P], ident)
                        m.then_inc(sem("a_tr"), 1)
                    for k in bm_slots(4 * c + j):
                        if k < len(BM):
                            bm_scores(k)
                        if 1 <= k <= len(BM):
                            bm_transposes(k - 1)
                        if k >= 2:
                            bm_values(k - 2)

            def a_scores(k):
                h, t = divmod(k, TT)
                a, b = (h % 2) * HD, (h % 2 + 1) * HD
                if k:
                    pe.wait_ge(sem("a_max"), 2 * k)
                if k >= 3:
                    pe.wait_ge(sem("a_out"), k - 2)
                for g in range(NG):
                    o = (S0, S0, S1)[g][:, (g % 2) * TOK:(g % 2 + 1) * TOK]
                    m = pe.matmul(o, aqT[a:b, 0, g, h // 2, t * P:(t + 1) * P], aqT[a:b, 1, g, h // 2, :],
                                  start=(g != 1), stop=True, skip_group_check=True)
                m.then_inc(sem("a_sc"), 1)

            def a_transposes(k):
                pe.wait_ge(sem("a_exp"), k + 1)
                if k:
                    pe.wait_ge(sem("a_pt"), 2 * k)
                for i in range(2 * NG):
                    m = pe.transpose((T0, T1)[i // 4][:, (i % 4) * P:(i % 4 + 1) * P], sm2[:, k % 2, i * P:(i + 1) * P], ident)
                m.then_inc(sem("a_ptr"), 1)

            def a_values(k):
                h, t = divmod(k, TT)
                pe.wait_ge(sem("a_pt"), 2 * k + 2)
                if k:
                    pe.wait_ge(sem("a_out"), k)
                pe.wait_ge(sem("a_max"), 2 * min(k + 2, AH * TT))
                for i in range(2 * NG):
                    m = pe.matmul(S1[:, TOK:TOK + HD], pT2[:, k % 2, i, :], va[:, i // 2, i % 2, h * HD:(h + 1) * HD],
                                  start=(i == 0), stop=(i == 2 * NG - 1))
                m.then_inc(sem("apv_done"), 1)

            for n in range(24):
                project(f"mg{n // 4}", pairs=[n % 4])
                for k in a_slots(n):
                    if k == 0:
                        pe.wait_ge(sem("a_ev"), 12)
                        pe.wait_ge(sem("av_ready"), 6)
                        pe.wait_ge(sem("bm_out"), len(BM))
                    if k >= 2:
                        a_values(k - 2)
                    if k < AH * TT:
                        a_scores(k)
                    if 1 <= k <= AH * TT:
                        a_transposes(k - 1)
            pe.wait_ge(sem("a_pt"), 2 * AH * TT)

            def output_transposes(i):
                b, f = i // 2, i % 2 * 2
                if i == 3:
                    pe.wait_ge(sem("a_out"), AH * TT)
                if i >= 4:
                    pe.wait_ge(sem("o_lo"), i - 3)
                for q in range(2):
                    for t in range(TT):
                        m = pe.transpose(OBANKS[i % 4][:, q * TOK + t * P:q * TOK + (t + 1) * P],
                                         gat[:, b, t, (f + q) * P:(f + q + 1) * P], ident)
                m.then_inc(sem("o_tr"), 1)

            for i in range(4):
                output_transposes(i)
            for nm in BRANCH_ORDER:
                b = "bma".index(nm[0])
                project("br" + nm, xh=oth[:, 4 * b:4 * b + 4, :], xl=otl[:, 4 * b:4 * b + 4, :],
                        ready=(sem("o_lo"), 2 * b, 1))
                if nm == "b0":
                    output_transposes(4)
                    output_transposes(5)
            for f in range(KD):
                if f % 2 == 0:
                    pe.wait_ge(sem("o_lo"), 6)
                if f < 4:
                    pe.wait_ge(sem("merged_ready"), 2)
                else:
                    pe.wait_ge(sem("merged_ready_dve"), 2)
                for t in range(TT):
                    m = pe.transpose(AUX[f // 2][:, (f % 2) * TOK + t * P:(f % 2) * TOK + (t + 1) * P],
                                     merged[:, t, f * P:(f + 1) * P], ident)
                if f % 2:
                    m.then_inc(sem("m_tr"), 1)
            project("wo0", ready=(sem("m_lo"), 0, 1))
            last_pairs("wo1", 0, range(4), xth, xtl)

        @block.scalar
        def _(act):
            at = [0]

            def hi_upto(n):
                while at[0] < min(n, NPAIRS):
                    p = at[0]
                    act.wait_ge(raw_landed[p % RAW], 16 * (p // RAW + 1))
                    if p >= RING:
                        act.wait_ge(pair_used, p - RING + 1)
                    act.activation(whi[:, p % RING, :], raw[:, p % RAW, :], ACT.Copy).then_inc(hi_ready, 1)
                    at[0] += 1

            n_sq = [0]

            def squares(n, src, t, half):
                if n_sq[0]:
                    act.wait_ge(sem("ssq_ready"), n_sq[0])
                n_sq[0] += 1
                act.activation(sqs[:, :], src[:, t, half * 512:(half + 1) * 512], ACT.Square,
                               accum_out=ssq[:, n, 2 * t + half:2 * t + half + 1]).then_inc(sem("ssq_ready"), 1)

            def norm_hi(n):
                g, o = NORM_GAIN[n]
                for f in range(KD):
                    if f % 2 == 0:
                        act.wait_ge(sem("xt_tr"), 4 * n + f // 2 + 1)
                    act.activation(xth[:, f, :], AUX[f // 2][:, (f % 2) * TOK:(f % 2 + 1) * TOK], ACT.Copy,
                                   scale=col(g, o + f, 1)).then_inc(sem("xt_hi"), 1)

            for t in range(TT):
                act.wait_ge(sem(f"mem_landed{t}"), 16)
                for half in range(2):
                    squares(0, xn, t, half)
            hi_upto(2)
            act.wait_ge(sem("col_landed"), 16)
            norm_hi(0)
            hi_upto(4)
            act.activation(sp_[:, 0, :], col("ldt"), ACT.Exp).then_inc(sem("par_a"), 1)
            hi_upto(5)
            act.wait_ge(sem("x_landed"), 16)
            for t in range(TT):
                for half in range(2):
                    squares(1, xres, t, half)
            act.wait_ge(sem("par_d"), 1)
            act.activation(sp_[:, 3, :], sp_[:, 1, :], ACT.Exp).then_inc(sem("par_a"), 1)
            act.activation(lamv[:, 2:4], lamv[:, 0:2], ACT.Exp).then_inc(sem("par_a"), 1)
            act.activation(lamv[:, 6:8], lamv[:, 4:6], ACT.Exp).then_inc(sem("par_a"), 1)
            act.activation(sp_[:, 6, :], sp_[:, 5, :], ACT.Sin).then_inc(sem("par_a"), 1)
            act.activation(sp_[:, 7, :], sp_[:, 5, :], ACT.Sin, scale=0.5).then_inc(sem("par_a"), 1)
            hi_upto(end_pair("km") + 4)
            for t in range(TT):
                act.wait_ge(pair_used, end_pair("km"))
                act.copy(kmT[:, 2 * t:2 * t + 2, :], PJ[0][:, t, :]).then_inc(sem("mem_ev"), 1)
            hi_upto(end_pair("vm") + 4)
            for t in range(TT):
                act.wait_ge(pair_used, end_pair("vm"))
                act.copy(vm[:, t, :], PJ[1][:, t, :]).then_inc(sem("mem_ev"), 1)

            for l in range(LAYERS):
                act.wait_ge(pair_used, FIRST[chunk(f"ssm_u{l}")])
                norm_hi(1 + 2 * l)
                hi_upto(end_pair(f"ssm_u{l}") + 2)
                if l == 0:
                    act.wait_ge(sem("par_d"), 1)
                for s in range(ST):
                    act.wait_ge(sem("bu_done"), ST * l + s + 1)
                    act.copy(bu[:, s, :, :], AUX[s % 4][:, :]).then_inc(sem("bu_ready"), 1)
                    if s % 2:
                        hi_upto(end_pair(f"ssm_u{l}") + 3 + s // 2)
                for i, nm in enumerate("qk"):
                    c = chunk(f"{nm}{l}")
                    hi_upto(end_pair(f"{nm}{l}") + 4)
                    act.wait_ge(pair_used, FIRST[c] + PAIRS[c])
                    for t in range(TT):
                        if t == 0 and (i or l):
                            act.wait_ge(sem("hss_ready"), 2 * (2 * l + i))
                            act.wait_ge(sem("rope_ready"), 4 * (2 * l + i))
                        act.activation(hsq[:, t, :], PJ[BUF[c]][:, t, :], ACT.Square).then_inc(sem("hsq_ready"), 1)
                    if i == 1:
                        hi_upto(end_pair(f"k{l}") + 5)
                        act.wait_ge(sem("qk_tr"), 2 * l + 1)
                        act.copy(qT[:, 0:2, :], S0[:, :]).then_inc(sem("qk_ev"), 1)
                        act.copy(qT[:, 2:4, :], S1[:, :]).then_inc(sem("qk_ev"), 1)
                c = chunk(f"gmlp{l}")
                hi_upto(end_pair(f"gmlp{l}") + 4)
                act.wait_ge(pair_used, FIRST[c] + PAIRS[c])
                act.wait_ge(sem("ssq_ready"), n_sq[0])
                for t in range(TT):
                    if t:
                        act.wait_ge(sem("gss_ready"), 2 * l + 1)
                    act.activation(sqs[:, 0:256], PJ[BUF[c]][:, t, 256:512], ACT.Square,
                                   accum_out=gss[:, l, t:t + 1]).then_inc(sem("gss_ready"), 1)
                for t in range(TT):
                    act.copy(ug[:, t, :], PJ[BUF[c]][:, t, 0:256]).then_inc(sem("ug_ready"), 1)
                act.wait_ge(sem("qk_tr"), 2 * l + 2)
                act.copy(kT[:, 0:2, :], T0[:, :]).then_inc(sem("qk_ev"), 1)
                act.copy(kT[:, 2:4, :], T1[:, :]).then_inc(sem("qk_ev"), 1)

                def exps(b):
                    t, heads = DB[b]
                    n = P * (t + 1)
                    act.wait_ge(sem("da_nb"), 3 * l + b + 1)
                    if b == 2:
                        act.wait_ge(sem("da_tr"), 3 * l + 1)
                    for c, bank in enumerate(DBANKS[b]):
                        for i in range(len(heads)):
                            act.activation(sm[:, b % 2, c, i * n:(i + 1) * n], bank[:, i * n:(i + 1) * n], ACT.Exp,
                                           bias=st_[:, b, 2 + c, i:i + 1], scale=QKD ** -0.5,
                                           accum_out=st_[:, b, 4 + c, i:i + 1]).then_inc(sem("da_exp"), 1)

                def prob_evac(b):
                    act.wait_ge(sem("da_tr"), 3 * l + b + 1)
                    if b == 2:
                        act.wait_ge(sem("da_pv"), 3 * l + 1)
                    act.copy(pT[:, b % 2, :, :], S1[:, :] if b == 2 else PJ[buf(f"gmlp{l}")][:, b, :]).then_inc(sem("da_pt"), 1)

                hi_upto(end_pair(f"v{l}"))
                exps(0)
                exps(1)
                c = chunk(f"v{l}")
                act.wait_ge(pair_used, FIRST[c] + PAIRS[c])
                for t in range(TT):
                    act.copy(v_sb[:, t, :], PJ[BUF[c]][:, t, :]).then_inc(sem("v_ready"), 1)
                prob_evac(0)
                hi_upto(end_pair(f"v{l}") + 2)
                exps(2)
                prob_evac(1)

                def attention_squares(t):
                    act.wait_ge(sem("da_o"), 2 * l + t + 1)
                    act.activation(hsq[:, t, :], xn[:, t, 0:512], ACT.Square).then_inc(sem("osq_ready"), 1)

                attention_squares(0)
                act.wait_ge(sem("mix_tr"), 2 * l + 1)
                act.wait_ge(pair_used, end_pair(f"v{l}"))
                act.copy(xth[:, 2:4, :], S0[:, :]).then_inc(sem("mix_hi"), 1)
                prob_evac(2)
                hi_upto(end_pair(f"v{l}") + 3)
                attention_squares(1)
                hi_upto(end_pair(f"v{l}") + RING)
                act.wait_ge(sem("ypre_ready"), 2 * (l + 1))
                for f in range(2):
                    act.activation(md[:, 0, f, :], md[:, 1, f, :], ACT.Gelu_apprx_tanh).then_inc(sem("gelu_ready"), 1)
                act.wait_ge(sem("mix_tr"), 2 * l + 2)
                act.copy(xth[:, 4:6, :], S1[:, :]).then_inc(sem("mix_hi"), 1)
                act.copy(xth[:, 6:8, :], T0[:, :]).then_inc(sem("mix_hi"), 1)
                act.wait_ge(sem("glu_done"), l + 1)
                for f in range(2):
                    act.activation(md[:, 1, f, :], S0[:, f * TOK:(f + 1) * TOK], ACT.Tanh, scale=0.5,
                                   bias=hb[:, 2 * l + f:2 * l + f + 1]).then_inc(sem("tanh_ready"), 1)
                act.wait_ge(sem("glu_prod"), l + 1)
                act.activation(xth[:, 0:2, :], md[:, 2, :, :], ACT.Copy, scale=0.5).then_inc(sem("mix_hi"), 1)
                for i in range(2):
                    nm = f"out{l}_{i}"
                    hi_upto(end_pair(nm) + (4 if i == 0 else 1))
                    for t in range(TT):
                        act.wait_ge(sem("resid"), 8 * l + 2 * i + t + 1)
                        squares(2 + 2 * l, xres, t, i)
                hi_upto(end_pair(nm) + 3)
                act.wait_ge(pair_used, end_pair(f"out{l}_1"))
                norm_hi(2 + 2 * l)

                def unit_first(j):
                    c = chunk(f"up{l}_{j}")
                    act.wait_ge(pair_used, FIRST[c] + PAIRS[c])
                    if UNITS * l + j >= 2:
                        act.wait_ge(sem("gated"), UNITS * l + j - 1)
                    for i in range(4):
                        k = conv_col(l, j, i)
                        act.activation(acc[:, j % 2, i, :], PJ[BUF[c]][:, i // 2, (i % 2) * TOK:(i % 2 + 1) * TOK],
                                       ACT.Identity, scale=colv[:, k + 2:k + 3], bias=colv[:, k + 3:k + 4]).then_inc(sem("conv_a"), 1)

                def unit_gelu(j):
                    act.wait_ge(sem("conv_d"), 4 * (UNITS * l + j + 1))
                    act.activation(acc[:, j % 2, 0:2, :], acc[:, j % 2, 0:2, :], ACT.Gelu_apprx_tanh).then_inc(sem("ffn_gelu"), 1)

                def unit_hi(j):
                    act.wait_ge(sem("gated"), UNITS * l + j + 1)
                    act.copy(hth[:, 2 * j:2 * j + 2, :], gtd[:, j % 2, :, :]).then_inc(sem("ht_hi"), 1)

                for j in range(UNITS + 1):
                    if j < UNITS:
                        hi_upto(end_pair(f"up{l}_{j}") + 3)
                        unit_first(j)
                        hi_upto(end_pair(f"up{l}_{j}") + 4)
                    if j > 0:
                        unit_hi(j - 1)
                        if j < UNITS:
                            hi_upto(end_pair(f"up{l}_{j}") + 5)
                    if j < UNITS:
                        unit_gelu(j)
                for i in range(2):
                    nm = f"down{l}_{i}"
                    hi_upto(end_pair(nm) + (4 if i == 0 else 1))
                    for t in range(TT):
                        act.wait_ge(sem("resid"), 8 * l + 4 + 2 * i + t + 1)
                        squares(3 + 2 * l, xres, t, i)
                hi_upto(end_pair(nm) + 3)

            act.wait_ge(pair_used, FIRST[chunk("mq")])
            norm_hi(5)
            hi_upto(end_pair("mq") + 4)
            act.wait_ge(pair_used, end_pair("mq"))
            for t in range(TT):
                act.copy(mqT[:, 2 * t:2 * t + 2, :], PJ[buf("mq")][:, t, :]).then_inc(sem("mq_ev"), 1)
            hi_upto(end_pair("bq") + 4)
            act.wait_ge(pair_used, end_pair("bq"))
            for t in range(TT):
                act.activation(sm2[:, t, 0:512], PJ[buf("bq")][:, t, :], ACT.Square).then_inc(sem("bsq_ready"), 1)

            def gate_tanh(nm, th):
                i = SILU_ORDER.index(nm)
                act.wait_ge(pair_used, end_pair(nm))
                if i == 1:
                    act.wait_ge(sem("silu_ready"), 2)
                for t in range(TT):
                    act.activation(th[:, t, 0:512], PJ[buf(nm)][:, t, :], ACT.Tanh, scale=0.5).then_inc(sem("th_ready"), 1)

            hi_upto(end_pair("gb") + 3)
            act.wait_ge(sem("bhss_ready"), 1)
            gate_tanh("gb", sm2)
            act.wait_ge(sem("b_tr"), 1)
            act.copy(bqT[:, 0:2, :], T0[:, :]).then_inc(sem("b_ev"), 1)
            act.copy(bqT[:, 2:4, :], T1[:, :]).then_inc(sem("b_ev"), 1)
            hi_upto(end_pair("bkv") + 4)
            act.wait_ge(pair_used, end_pair("bkv"))
            for t in range(TT):
                act.activation(pT2[:, t, 0, :], PJ[buf("bkv")][:, t, 0:P], ACT.Square).then_inc(sem("bksq_ready"), 1)
                act.copy(bv[:, t, :], PJ[buf("bkv")][:, t, P:2 * P]).then_inc(sem("bv_ready"), 1)
            hi_upto(end_pair("gm") + 3)
            gate_tanh("gm", sm2)
            act.wait_ge(sem("b_tr"), 2)
            act.copy(bkT[:, :, :], S0[:, :]).then_inc(sem("b_ev"), 1)
            for c, nm in enumerate(A_CHUNKS):
                for j in range(4):
                    n = 4 * c + j
                    hi_upto(F2 + n + 3)
                    if j == 1 and c >= 7:
                        g = c - 7
                        act.wait_ge(pair_used, end_pair(f"av{g}"))
                        for t in range(TT):
                            act.copy(va[:, g, t, :], PJ[buf(f"av{g}")][:, t, :]).then_inc(sem("av_ready"), 1)
                    if 1 <= c <= 6 and j >= 2:
                        rnd = 2 * (c - 1) + j - 2
                        act.wait_ge(sem("a_tr"), rnd + 1)
                        w, g = divmod(c - 1, NG)
                        act.copy(aqT[:, w, g, 2 * (j - 2):2 * (j - 2) + 2, :], S1[:, :]).then_inc(sem("a_ev"), 1)
                    for k in bm_slots(n):
                        if k < len(BM):
                            br, h, t = BM[k]
                            act.wait_ge(sem("bm_nb"), k + 1)
                            if k == 0:
                                act.wait_ge(sem("silu_ready"), 4)
                            if k >= 2:
                                act.wait_ge(sem("bm_tr"), k - 1)
                            act.activation(sm2[:, k % 2, 0:TOK], S0[:, 0:TOK], ACT.Exp, bias=sx[:, k % 4, 1:2],
                                           scale=(HD if br == "b" else MD) ** -0.5,
                                           accum_out=sx[:, k % 4, 2:3]).then_inc(sem("bm_exp"), 1)
                        if 1 <= k <= len(BM):
                            act.wait_ge(sem("bm_tr"), k)
                            if k >= 3:
                                act.wait_ge(sem("bm_pv"), k - 2)
                            act.copy(pT2[:, (k - 1) % 2, 0:2, :], T0[:, 0:TOK]).then_inc(sem("bm_pt"), 1)
            hi_upto(F3 + 2)
            act.wait_ge(sem("a_tr"), 12)
            gate_tanh("ga", rt)
            for n in range(24):
                hi_upto(F3 + n + 3)
                for k in a_slots(n):
                    if k < AH * TT:
                        act.wait_ge(sem("a_nb"), k + 1)
                        act.activation(sm2[:, k % 2, :], sm2[:, k % 2, :], ACT.Exp, bias=sx[:, k % 4, 1:2], scale=HD ** -0.5,
                                       accum_out=sx[:, k % 4, 2:3]).then_inc(sem("a_exp"), 1)
                    if 1 <= k <= AH * TT:
                        act.wait_ge(sem("a_ptr"), k)
                        if k >= 3:
                            act.wait_ge(sem("apv_done"), k - 2)
                        act.copy(pT2[:, (k - 1) % 2, 0:4, :], T0[:, :]).then_inc(sem("a_pt"), 1)
                        act.copy(pT2[:, (k - 1) % 2, 4:6, :], T1[:, 0:TOK]).then_inc(sem("a_pt"), 1)
                if n % 4 == 1 and n > 4:
                    merge_tanh(act, n // 4 - 1)
            for i in range(6):
                act.wait_ge(sem("o_tr"), i + 1)
                act.activation(oth[:, 2 * i:2 * i + 2, :], OBANKS[i % 4][:, :], ACT.Copy, scale=0.5).then_inc(sem("o_hi"), 1)
                if i == 3:
                    hi_upto(F3 + 24 + 3)
                    merge_tanh(act, 5)
            hi_upto(F3 + 24 + RING)
            hi_upto(FIRST[chunk("wo0")] + 3)
            for i in range(4):
                act.wait_ge(sem("m_tr"), i + 1)
                act.activation(xth[:, 2 * i:2 * i + 2, :], AUX[i][:, :], ACT.Copy, scale=0.5).then_inc(sem("m_hi"), 1)
            for i in range(2):
                nm = f"wo{i}"
                hi_upto(end_pair(nm) + 4)
                for t in range(TT):
                    if (i, t) == (1, 0):
                        act.wait_ge(sem("tile0_done"), 2 * LAYERS + 1)
                    else:
                        act.wait_ge(pair_used, end_pair(nm))
                    act.wait_ge(sem("ssq_ready"), n_sq[0])
                    n_sq[0] += 1
                    act.activation(sqs[:, :], PJ[buf(nm)][:, t, :], ACT.Square,
                                   accum_out=ssq[:, 6, 2 * t + i:2 * t + i + 1]).then_inc(sem("ssq_ready"), 1)

        @block.gpsimd
        def _(pool):
            pool.memset(mhalf[:], -0.5).then_inc(sem("mhalf_ready"), 1)
            pool.wait_ge(sem("mhalf_ready"), 1)

            steps = [0]

            def link(ins, wait=True):
                steps[0] += 1
                ins.then_inc(sem("pool_chain"), 1)
                if wait:
                    pool.wait_ge(sem("pool_chain"), steps[0])

            def power(out_, in_, n, width, signal):
                link(pool.tensor_scalar(out_, in_, 1.0 / width, EPS, ALU.mult, ALU.add))
                pool.tensor_tensor(out_, out_, mhalf[:, 0:n], ALU.pow).then_inc(sem(signal), 1)

            def norm_rstd(n):
                for t in range(TT):
                    pool.wait_ge(sem("ssq_ready"), 4 * n + (2 if n < 2 else 3) if t == 0 else 4 * n + 4)
                    link(pool.tensor_tensor(ssm1[:, n, t:t + 1], ssq[:, n, 2 * t:2 * t + 1], ssq[:, n, 2 * t + 1:2 * t + 2], ALU.add))
                    power(rstd[:, n, t:t + 1], ssm1[:, n, t:t + 1], 1, D, "rstd_ready")

            GR_AFTER = (4, 6)
            HR_AFTER = ((0, 3), (3, 5))
            def pre_rotate(l, s):
                pool.wait_ge(sem("bu_ready"), ST * l + s + 1)
                if ST * l + s:
                    pool.wait_ge(sem("pre_rot"), 2 * (ST * l + s))
                if l == 0 and s == ST // 2:
                    pool.wait_ge(sem("tab_ready_dve"), ST // 2)
                if l and s == 0:
                    pool.wait_ge(sem("state_ready_pool"), 2 * len(POOL_POST) * l)
                cc, ss = wide(tab[:, 0, s, :], 2), wide(tab[:, 1, s, :], 2)
                pool.tensor_tensor(mp[:, 0, :, :], bu[:, s, :, :], cc, ALU.mult).then_inc(sem("pool_chain"), 1)
                pool.tensor_tensor(mp[:, 1, :, :], bu[:, s, :, :], ss, ALU.mult).then_inc(sem("pool_chain"), 1)
                steps[0] += 2
                pool.wait_ge(sem("pool_chain"), steps[0])
                pool.tensor_tensor(bu[:, s, 0, :], mp[:, 0, 0, :], mp[:, 1, 1, :], ALU.add).then_inc(sem("pre_rot"), 1)
                pool.tensor_tensor(bu[:, s, 1, :], mp[:, 0, 1, :], mp[:, 1, 0, :], ALU.subtract).then_inc(sem("pre_rot"), 1)

            norm_rstd(0)
            norm_rstd(1)
            pool.wait_ge(sem("par_done"), 1)
            fold_coefficient(pool, link, 0, v_sb[:, :, :].rearrange("p t (o a b) -> p (t o) a b", o=2, b=32))
            pool.wait_ge(sem("cex_ready"), 2)
            pool.wait_ge(sem("factors_ready"), 1)
            for s in range(0, ST // 2, 2):
                table_product(pool, s, v_sb[:, :, :].rearrange("p k (c a b) -> p k c a b", c=2, a=16),
                              "tab_ready", s // 2)
            for l in range(LAYERS):
                if l > 0:
                    norm_rstd(1 + 2 * l)

                for s in range(ST):
                    pre_rotate(l, s)
                    if s in HR_AFTER[l]:
                        which = HR_AFTER[l].index(s)
                        for t in range(TT):
                            pool.wait_ge(sem("hss_ready"), 2 * (2 * l + which) + t + 1)
                            power(hr[:, which, 8 * t:8 * t + 8], hss[:, 8 * t:8 * t + 8], 8, QKD, "hr_ready")
                    if s == GR_AFTER[l]:
                        pool.wait_ge(sem("gss_ready"), 2 * (l + 1))
                        power(gr[:, l, :], gss[:, l, :], 2, 256, "gr_ready")
                for s in POOL_POST:
                    pool.wait_ge(sem("scanned"), 2 * (ST * l + s + 1))
                    pool.wait_ge(sem("pre_rot"), 2 * ST * (l + 1))
                    post_rotate(pool, l, s, mp)
                pool.wait_ge(sem("oss_ready"), l + 1)
                power(hr[:, 0, 0:8], hss[:, 0:8], 8, VD, "or_ready")
                norm_rstd(2 + 2 * l)
                for j in range(UNITS):
                    pool.wait_ge(sem("ffn_gelu"), UNITS * l + j + 1)
                    if j >= 2 or l:
                        pool.wait_ge(sem("ht_lo"), UNITS * l + j - 1)
                    pool.tensor_tensor(gtd[:, j % 2, :, :], acc[:, j % 2, 0:2, :], acc[:, j % 2, 2:4, :],
                                       ALU.mult).then_inc(sem("gated"), 1)
                    if l + 1 < LAYERS:
                        if j == 1:
                            table_base(pool, link, l + 1)
                            table_factor(pool, link, pow1)
                        if j == 2:
                            table_factor(pool, link, pow16)
                        if 3 <= j < 3 + ST // 2:
                            table_product(pool, 2 * (j - 3), xn[:, 0, :].rearrange("p (k c a b) -> p k c a b", k=2, c=2, a=16),
                                          "tab_ready", ST // 4 + j - 3)
                        if j == 3 + ST // 2:
                            fold_coefficient(pool, link, l + 1, xn[:, 0, :].rearrange("p (o a b) -> p o a b", o=4, b=32))

            norm_rstd(5)
            pool.wait_ge(sem("bhss_ready"), 1)
            power(hr[:, 0, 0:16], hss[:, 0:16], 16, HD, "bhr_ready")
            pool.wait_ge(sem("bhss_ready"), 2)
            power(hr[:, 1, 0:4], hss[:, 0:4], 4, HD, "bhr_ready")
            for c in range(6):
                if c:
                    pool.wait_ge(sem("a_tr"), 2 * c)
                else:
                    pool.wait_ge(sem("b_tr"), 1)
                for t in range(TT):
                    pool.wait_ge(sem("rot_terms"), 4 * c + 2 * t + 2)
                    c8, s8 = (xn[:, t, i * 512:(i + 1) * 512].rearrange("p (g d) -> p g d", g=8) for i in range(2))
                    o8 = rt[:, t, :].rearrange("p (g d) -> p g d", g=8)
                    pool.tensor_tensor(o8[:, :, 0:32], c8[:, :, 0:32], s8[:, :, 32:64], ALU.subtract).then_inc(sem("a_rope"), 1)
                    pool.tensor_tensor(o8[:, :, 32:64], c8[:, :, 32:64], s8[:, :, 0:32], ALU.add).then_inc(sem("a_rope"), 1)
            for i in range(6):
                b, n = BRANCH_ORDER[i][0], int(BRANCH_ORDER[i][1])
                if b == "b" or i == 5:
                    continue
                for t in range(TT):
                    pool.wait_ge(sem("y_gated"), 2 * i + t + 1)
                    m = merged[:, t, 512 * n:512 * n + 512]
                    at = ("abm".index(b)) * D + 512 * n
                    if b == "a":
                        pool.wait_ge(sem("merged_m"), 2 * n + t + 1)
                    pool.tensor_tensor(m, m, gt[:, t, at:at + 512], ALU.add).then_inc(sem("merged_m" if b == "m" else "merged_ready"), 1)
            norm_rstd(6)

        @block.vector
        def _(dve):
            at = [0]
            steps = [0]

            def link(ins, wait=True):
                steps[0] += 1
                ins.then_inc(sem("dve_chain"), 1)
                if wait:
                    dve.wait_ge(sem("dve_chain"), steps[0])

            def lo_upto(n):
                while at[0] < min(n, NPAIRS):
                    p = at[0]
                    dve.wait_ge(hi_ready, p + 1)
                    dve.tensor_tensor(wlo[:, p % RING, :], raw[:, p % RAW, :], whi[:, p % RING, :].bitcast(F32),
                                      ALU.subtract).then_inc(lo_ready, 1)
                    at[0] += 1

            def norm_scale(n, src):
                for t in range(TT):
                    dve.wait_ge(sem("rstd_ready"), 2 * n + t + 1)
                    dve.tensor_scalar(xn[:, t, :], src[:, t, :], rstd[:, n, t:t + 1], None, ALU.mult).then_inc(sem("xn_ready"), 1)

            def norm_lo(n):
                g, o = NORM_GAIN[n]
                for f in range(KD):
                    dve.wait_ge(sem("xt_hi"), KD * n + f // 2 * 2 + 2)
                    dve.scalar_tensor_tensor(out=xtl[:, f, :], in0=AUX[f // 2][:, (f % 2) * TOK:(f % 2 + 1) * TOK],
                                             scalar=col(g, o + f, 1), in1=xth[:, f, :].bitcast(F32),
                                             op0=ALU.mult, op1=ALU.subtract).then_inc(sem("xt_lo"), 1)

            norm_scale(0, xn)
            lo_upto(2)
            dve.wait_ge(sem("col_landed"), 16)
            norm_lo(0)
            lo_upto(4)
            v = [sp_[:, i, :] for i in range(24)]
            dve.wait_ge(sem("row_landed"), 16)
            dve.wait_ge(sem("par_a"), 1)
            link(dve.tensor_tensor(v[1], col("are"), v[0], ALU.mult))
            link(dve.tensor_tensor(v[2], col("aim"), v[0], ALU.mult))
            link(dve.tensor_scalar(v[4], v[2], 1.0 / (2 * math.pi), None, ALU.mult))
            link(dve.tensor_scalar(v[4], v[4], 12582912.0, None, ALU.add))
            link(dve.tensor_scalar(v[4], v[4], -12582912.0, None, ALU.add))
            c1 = 6.28125
            c2 = round((2 * math.pi - c1) * 2 ** 21) / 2 ** 21
            c3 = 2 * math.pi - c1 - c2
            src_ = v[2]
            for cc in (c1, c2, c3):
                link(dve.scalar_tensor_tensor(out=v[5], in0=v[4], scalar=-cc, in1=src_, op0=ALU.mult, op1=ALU.add))
                src_ = v[5]
            link(dve.tensor_scalar(v[5], v[5], 3.1415925, -3.1415925, ALU.min, ALU.max))
            dve.wait_ge(sem("lam_landed"), 16)
            lamrow = bu[:, 0, :, :].rearrange("p c t -> p (c t)")
            for l in range(LAYERS):
                for i, (a, b) in enumerate((("lq1", "lk1"), ("lq2", "lk2"))):
                    ra, rb = (lamrow[:, LAM[z][0] + 64 * l:LAM[z][0] + 64 * l + 64] for z in (a, b))
                    link(dve.tensor_tensor_reduce(sqs2[:, :], ra, rb, 1.0, 0.0,
                                                  ALU.mult, ALU.add, lamv[:, 4 * i + l:4 * i + l + 1]))
            dve.sem_inc(sem("par_d"), 1)
            lo_upto(6)
            dve.wait_ge(sem("cst_landed"), 16)
            dve.tensor_copy(identb[:, :], ident).then_inc(sem("maskb_ready"), 1)
            for t, k in ((0, 4), (1, 2)):
                dve.tensor_copy(maskb[:, t, :].rearrange("p (h n) -> p h n", h=k),
                                wide(cs("mdiff")[:, 0:128] if t == 0 else cs("mdiff")[:, 128:384], k)).then_inc(sem("maskb_ready"), 1)
            cosv = cs("cos").rearrange("p (t d) -> p t d", t=TT)
            sinv = cs("sin").rearrange("p (t d) -> p t d", t=TT)
            for l in range(LAYERS):
                link(dve.tensor_scalar(row("sub", VD * l, VD), row("sub", VD * l, VD), 1.0 - LAMBDA_INIT[l], None, ALU.mult))
            dve.wait_ge(sem("col_landed"), 16)
            link(dve.tensor_scalar(hb[:, :], col("bglu"), 0.5, None, ALU.mult))
            lo_upto(7)
            dve.wait_ge(sem("par_a"), 6)
            for l in range(LAYERS):
                link(dve.tensor_tensor(nlam[:, l:l + 1], lamv[:, 6 + l:7 + l], lamv[:, 2 + l:3 + l], ALU.subtract))
                link(dve.tensor_scalar(nlam[:, l:l + 1], nlam[:, l:l + 1], -LAMBDA_INIT[l], None, ALU.add))
            are, aim = col("are"), col("aim")
            link(dve.tensor_tensor(v[13], v[7], v[7], ALU.mult))
            link(dve.tensor_scalar(v[8], v[13], -2.0, 1.0, ALU.mult, ALU.add))
            link(dve.tensor_tensor(v[14], v[3], v[8], ALU.mult))
            link(dve.tensor_tensor(v[15], v[3], v[6], ALU.mult))
            link(dve.tensor_scalar(v[14], v[14], -1.0, None, ALU.add))
            link(dve.tensor_tensor(v[16], are, are, ALU.mult))
            link(dve.tensor_tensor(v[17], aim, aim, ALU.mult))
            link(dve.tensor_tensor(v[16], v[16], v[17], ALU.add))
            link(dve.reciprocal(v[16], v[16]))
            link(dve.tensor_tensor(v[17], v[14], are, ALU.mult))
            link(dve.tensor_tensor(v[18], v[15], aim, ALU.mult))
            link(dve.tensor_tensor(v[17], v[17], v[18], ALU.add))
            link(dve.tensor_tensor(v[9], v[17], v[16], ALU.mult))
            link(dve.tensor_tensor(v[17], v[15], are, ALU.mult))
            link(dve.tensor_tensor(v[18], v[14], aim, ALU.mult))
            link(dve.tensor_tensor(v[17], v[17], v[18], ALU.subtract))
            link(dve.tensor_tensor(v[10], v[17], v[16], ALU.mult))
            link(dve.tensor_scalar(v[11], v[10], -1.0, None, ALU.mult))
            link(dve.tensor_scalar(v[12], v[9], -1.0, None, ALU.mult))
            dve.sem_inc(sem("par_done"), 1)
            norm_scale(1, xres)
            table_base(dve, link, 0)
            lo_upto(9)
            table_factor(dve, link, pow1)
            lo_upto(end_pair("vm") + 3)

            for l in range(LAYERS):
                if l:
                    dve.wait_ge(sem("xt_tr"), 4 * (1 + 2 * l))
                    dve.wait_ge(sem("cex_ready"), 2 * (l + 1))
                    norm_scale(1 + 2 * l, xres)
                norm_lo(1 + 2 * l)
                if l == 0:
                    lo_upto(end_pair(f"ssm_u{l}"))
                    table_factor(dve, link, pow16)
                    dve.sem_inc(sem("factors_ready"), 1)
                lo_upto(end_pair(f"ssm_u{l}") + 1)
                c = chunk(f"ssm_u{l}")
                dve.wait_ge(pair_used, FIRST[c] + PAIRS[c])
                dve.tensor_copy(uT[:, :, :], PJ[BUF[c]][:, 0, :]).then_inc(sem("u_ready"), 1)
                lo_upto(end_pair(f"ssm_u{l}") + 3)
                for i, (g, tb_) in enumerate((("qg", cosv), ("qg", sinv), ("kg", cosv), ("kg", sinv))):
                    link(dve.tensor_tensor(ropeq[:, i, :, :], tb_, wide(row(g, 64 * l, 64), TT), ALU.mult))
                dve.wait_ge(sem("wst_landed"), 16 * (l + 1))
                dve.memset(wsts[64:128, :, 0:64], 0.0).then_inc(sem("wst_ready"), 1)
                if l == 0:
                    lo_upto(end_pair(f"ssm_u{l}") + 5)
                    tmp = pT[:, :, :, :].rearrange("p k i n -> p k (i n)").rearrange("p k (c a b) -> p k c a b", c=2, a=16)
                    for n in range(ST // 4):
                        table_product(dve, ST // 2 + 2 * n, tmp, "tab_ready_dve", n)
                        lo_upto(end_pair(f"ssm_u{l}") + 6 + n)

                def qk_sums(i, nm):
                    c = chunk(f"{nm}{l}")
                    pj = PJ[BUF[c]]
                    lo_upto(end_pair(f"{nm}{l}") + 3)
                    dve.wait_ge(sem("hsq_ready"), 4 * l + 2 * i + 2)
                    if i or l:
                        dve.wait_ge(sem("hr_ready"), 2 * (2 * l + i))
                    for t in range(TT):
                        dve.tensor_reduce(hss[:, 8 * t:8 * t + 8], hsq[:, t, :].rearrange("p (g d) -> p g d", g=8), AX.X,
                                          ALU.add).then_inc(sem("hss_ready"), 1)
                    lo_upto(end_pair(f"{nm}{l}") + 5)

                def qk_rope(i, nm):
                    pj = PJ[buf(f"{nm}{l}")]
                    for t in range(TT):
                        dve.wait_ge(sem("hr_ready"), 2 * (2 * l + i) + t + 1)
                        g8 = pj[:, t, :].rearrange("p (g d) -> p g d", g=8)
                        dve.tensor_tensor(qn[:, t, :].rearrange("p (g d) -> p g d", g=8), g8,
                                          wide(hr[:, i, 8 * t:8 * t + 8], QKD, 2), ALU.mult).then_inc(sem("qn_ready"), 1)
                    dve.wait_ge(sem("qn_ready"), 2 * (2 * l + i + 1))
                    for t in range(TT):
                        q8 = qn[:, t, :].rearrange("p (g d) -> p g d", g=8)
                        t2 = hsq[:, t, :].rearrange("p (g d) -> p g d", g=8)
                        o8 = xn[:, t, 512 * i:512 * i + 512].rearrange("p (g d) -> p g d", g=8)
                        cg, sg = (wide(ropeq[:, 2 * i + j, t, :], 8) for j in range(2))
                        dve.tensor_tensor(t2, q8, sg, ALU.mult).then_inc(sem("dve_chain"), 1)
                        dve.tensor_tensor(q8, q8, cg, ALU.mult).then_inc(sem("dve_chain"), 1)
                        steps[0] += 2
                        dve.wait_ge(sem("dve_chain"), steps[0])
                        dve.tensor_tensor(o8[:, :, 0:32], q8[:, :, 0:32], t2[:, :, 32:64], ALU.subtract).then_inc(sem("rope_ready"), 1)
                        dve.tensor_tensor(o8[:, :, 32:64], q8[:, :, 32:64], t2[:, :, 0:32], ALU.add).then_inc(sem("rope_ready"), 1)

                def ssm_scan(s):
                    dve.wait_ge(sem("pre_rot"), 2 * (ST * l + s + 1))
                    r = sp_[:, 3, 8 * l + s:8 * l + s + 1].to_broadcast([P, TOK])
                    for c in range(2):
                        dve.tensor_tensor_scan(bu[:, s, c, :], r, bu[:, s, c, :], 0.0, ALU.mult, ALU.add).then_inc(sem("scanned"), 1)
                    if s in POOL_POST:
                        return
                    dve.wait_ge(sem("scanned"), 2 * (ST * l + s + 1))
                    post_rotate(dve, l, s, md[:, 1:3, :, :])

                def batch_max(b):
                    t, heads = DB[b]
                    k = len(heads)
                    dve.wait_ge(sem("da_sc"), 3 * l + b + 1)
                    for c, bank in enumerate(DBANKS[b]):
                        link(dve.tensor_reduce(st_[:, b, c, 0:k], bank[:, :].rearrange("p (h n) -> p h n", h=k), AX.X, ALU.max))
                    dve.tensor_scalar(st_[:, b, 2:4, 0:k], st_[:, b, 0:2, 0:k], -(QKD ** -0.5), None, ALU.mult).then_inc(sem("da_nb"), 1)

                def combine(b):
                    k = len(DB[b][1])
                    dve.wait_ge(sem("da_exp"), 16 * l + EXPS[b])
                    link(dve.reciprocal(st_[:, b, 6:8, 0:k], st_[:, b, 4:6, 0:k]))
                    link(dve.scalar_tensor_tensor(out=st_[:, b, 7, 0:k], in0=st_[:, b, 7, 0:k], scalar=nlam[:, l:l + 1],
                                                  in1=st_[:, b, 4, 0:k], op0=ALU.mult, op1=ALU.mult))
                    n = 512 // k
                    for i in range(k):
                        p0, p1 = (sm[:, b % 2, c, i * n:(i + 1) * n] for c in range(2))
                        dve.scalar_tensor_tensor(out=p1, in0=p1, scalar=st_[:, b, 7, i:i + 1], in1=p0, op0=ALU.mult,
                                                 op1=ALU.add).then_inc(sem("da_w"), 1)

                def out_scale(t):
                    dve.wait_ge(sem("da_pv"), 3 * l + (1 if t == 0 else 3))
                    for b in ((0,) if t == 0 else (1, 2)):
                        k = len(DB[b][1])
                        a = DB[b][1][0] * VD
                        o = xn[:, t, a:a + k * VD].rearrange("p (h n) -> p h n", h=k)
                        i = PJ[buf(f"v{l}")][:, t, a:a + k * VD].rearrange("p (h n) -> p h n", h=k)
                        m = dve.tensor_tensor(o, i, wide(st_[:, b, 6, 0:k], VD, 2), ALU.mult)
                        if b == 1:
                            link(m)
                    m.then_inc(sem("da_o"), 1)

                qk_sums(0, "q")
                qk_rope(0, "q")
                lo_upto(end_pair(f"q{l}") + 6)
                qk_sums(1, "k")
                ssm_scan(0)
                qk_rope(1, "k")
                lo_upto(end_pair(f"gmlp{l}") + 2)
                ssm_scan(1)
                lo_upto(end_pair(f"gmlp{l}") + 3)
                c = chunk(f"gmlp{l}")
                dve.wait_ge(sem("gr_ready"), l + 1)
                dve.wait_ge(sem("ug_ready"), 2 * (l + 1))
                dve.wait_ge(sem("qk_tr"), 2 * (l + 1))
                for t in range(TT):
                    dve.scalar_tensor_tensor(out=xn[:, t, 768:1024], in0=PJ[BUF[c]][:, t, 256:512], scalar=gr[:, l, t:t + 1],
                                             in1=row("vg", 256 * l, 256), op0=ALU.mult, op1=ALU.mult).then_inc(sem("vn_ready"), 1)
                lo_upto(end_pair(f"v{l}"))
                ssm_scan(2)
                batch_max(0)
                batch_max(1)
                ssm_scan(3)
                combine(0)
                ssm_scan(4)
                combine(1)
                batch_max(2)
                ssm_scan(5)
                out_scale(0)
                dve.wait_ge(sem("sgu_done"), l + 1)
                for h in range(4):
                    dve.scalar_tensor_tensor(out=xn[:, :, 512 + h * 64:576 + h * 64],
                                             in0=T0[:, h * P:(h + 1) * P].rearrange("p (t d) -> p t d", t=TT),
                                             scalar=col("bs", 4 * l + h, 1), in1=ug[:, :, h * 64:(h + 1) * 64],
                                             op0=ALU.add, op1=ALU.mult).then_inc(sem("sgu_ready"), 1)
                combine(2)
                lo_upto(end_pair(f"v{l}") + 1)
                dve.wait_ge(sem("mix_hi"), 4 * l + 1)
                dve.tensor_tensor(xtl[:, 2:4, :], S0[:, :].rearrange("p (f d) -> p f d", f=2), xth[:, 2:4, :].bitcast(F32),
                                  ALU.subtract).then_inc(sem("mix_lo"), 1)
                ssm_scan(6)
                out_scale(1)
                dve.wait_ge(sem("osq_ready"), 2 * (l + 1))
                dve.wait_ge(sem("hr_ready"), 4 * (l + 1))
                dve.tensor_reduce(hss[:, 0:8], hsq[:, :, :].rearrange("p t (g d) -> p (t g) d", g=4), AX.X, ALU.add)\
                   .then_inc(sem("oss_ready"), 1)
                ssm_scan(7)
                dve.wait_ge(sem("or_ready"), l + 1)
                for t in range(TT):
                    a4 = xn[:, t, 0:512].rearrange("p (g d) -> p g d", g=4)
                    for h in range(DH):
                        dve.scalar_tensor_tensor(out=a4[:, h, :], in0=a4[:, h, :], scalar=hr[:, 0, 4 * t + h:4 * t + h + 1],
                                                 in1=row("sub", VD * l, VD), op0=ALU.mult, op1=ALU.mult).then_inc(sem("diff_ready"), 1)
                lo_upto(end_pair(f"v{l}") + 2)
                dve.wait_ge(sem("y_done"), l + 1)
                for f in range(2):
                    dve.scalar_tensor_tensor(out=md[:, 1, f, :], in0=uT[:, f, :], scalar=col("dskip", 2 * l + f, 1),
                                             in1=T1[:, f * TOK:(f + 1) * TOK], op0=ALU.mult, op1=ALU.add).then_inc(sem("ypre_ready"), 1)
                lo_upto(end_pair(f"v{l}") + 3)
                dve.wait_ge(sem("mix_hi"), 4 * l + 3)
                for i, bank in enumerate((S1, T0)):
                    dve.tensor_tensor(xtl[:, 4 + 2 * i:6 + 2 * i, :], bank[:, :].rearrange("p (f d) -> p f d", f=2),
                                      xth[:, 4 + 2 * i:6 + 2 * i, :].bitcast(F32), ALU.subtract).then_inc(sem("mix_lo"), 1)
                lo_upto(end_pair(f"v{l}") + RING)
                dve.wait_ge(sem("tanh_ready"), 2 * (l + 1))
                dve.scalar_tensor_tensor(out=md[:, 2, :, :], in0=md[:, 1, :, :], scalar=1.0, in1=md[:, 0, :, :],
                                         op0=ALU.add, op1=ALU.mult).then_inc(sem("glu_prod"), 1)
                dve.wait_ge(sem("mix_hi"), 4 * (l + 1))
                dve.scalar_tensor_tensor(out=xtl[:, 0:2, :], in0=md[:, 2, :, :], scalar=0.5, in1=xth[:, 0:2, :].bitcast(F32),
                                         op0=ALU.mult, op1=ALU.subtract).then_inc(sem("mix_lo"), 1)

                def residual(nm, i, ahead):
                    c = chunk(nm)
                    lo_upto(end_pair(nm) + ahead)
                    for t in range(TT):
                        if i == 1 and t == 0:
                            dve.wait_ge(sem("tile0_done"), 2 * l + (2 if nm[0] == "d" else 1))
                        else:
                            dve.wait_ge(pair_used, FIRST[c] + PAIRS[c])
                        dve.tensor_tensor(xres[:, t, 512 * i:512 * i + 512], PJ[BUF[c]][:, t, :],
                                          xres[:, t, 512 * i:512 * i + 512], ALU.add).then_inc(sem("resid"), 1)
                residual(f"out{l}_0", 0, 4)
                residual(f"out{l}_1", 1, 1)
                norm_scale(2 + 2 * l, xres)
                norm_lo(2 + 2 * l)

                def unit_taps(j):
                    c = chunk(f"up{l}_{j}")
                    n0 = 4 * (UNITS * l + j)
                    for tap, sh in ((1, 1), (0, 2)):
                        for i in range(4):
                            k = conv_col(l, j, i)
                            if tap == 1:
                                dve.wait_ge(sem("conv_a"), n0 + i // 2 * 2 + 2)
                            else:
                                dve.wait_ge(sem("conv_m"), n0 + i + 1)
                            dve.scalar_tensor_tensor(
                                out=acc[:, j % 2, i, sh:TOK],
                                in0=PJ[BUF[c]][:, i // 2, (i % 2) * TOK:(i % 2 + 1) * TOK - sh],
                                scalar=colv[:, k + tap:k + tap + 1], in1=acc[:, j % 2, i, sh:TOK],
                                op0=ALU.mult, op1=ALU.add).then_inc(sem("conv_m" if tap == 1 else "conv_d"), 1)

                def unit_lo(j):
                    dve.wait_ge(sem("ht_hi"), UNITS * l + j + 1)
                    dve.tensor_tensor(htl[:, 2 * j:2 * j + 2, :], gtd[:, j % 2, :, :], hth[:, 2 * j:2 * j + 2, :].bitcast(F32),
                                      ALU.subtract).then_inc(sem("ht_lo"), 1)

                for j in range(UNITS + 1):
                    if j < UNITS:
                        lo_upto(end_pair(f"up{l}_{j}") + 3)
                        unit_taps(j)
                        lo_upto(end_pair(f"up{l}_{j}") + 4)
                    if j > 0:
                        unit_lo(j - 1)
                residual(f"down{l}_0", 0, 4)
                residual(f"down{l}_1", 1, 1)

            norm_scale(5, xres)
            norm_lo(5)
            lo_upto(end_pair("mq") + 2)
            aco, asi = (cs(z).rearrange("p (t d) -> p t d", t=TT) for z in ("acos", "asin"))
            for i, (g, tb) in enumerate((("qn2", aco), ("qn2", asi), ("kn2", aco), ("kn2", asi))):
                dve.tensor_tensor(tabq[:, i, :, :], tb, wide(row(g), TT), ALU.mult).then_inc(sem("tabq_ready"), 1)
            lo_upto(end_pair("bq") + 3)

            def head_norm_rope(heads, squares_, source, sq_sem, n_sq, which, temp, outs, sems_, lo_ahead):
                w = heads * HD
                dve.wait_ge(sem(sq_sem), n_sq)
                for t in range(TT):
                    m = dve.tensor_reduce(hss[:, heads * t:heads * t + heads], squares_(t).rearrange("p (g d) -> p g d", g=heads),
                                          AX.X, ALU.add)
                    if t == 0:
                        link(m)
                m.then_inc(sem("bhss_ready"), 1)
                lo_upto(lo_ahead)
                dve.wait_ge(sem("bhr_ready"), which + 1)
                dve.wait_ge(sem("tabq_ready"), 4)
                for t in range(TT):
                    g8 = source(t).rearrange("p (g d) -> p g d", g=heads)
                    x8 = temp(t, 0).rearrange("p (g d) -> p g d", g=heads)
                    dve.tensor_tensor(x8, g8, wide(hr[:, which, heads * t:heads * t + heads], HD, 2), ALU.mult).then_inc(sem(sems_[0]), 1)
                dve.wait_ge(sem(sems_[0]), 2)
                for t in range(TT):
                    x8 = temp(t, 0).rearrange("p (g d) -> p g d", g=heads)
                    t8 = temp(t, 1).rearrange("p (g d) -> p g d", g=heads)
                    link(dve.tensor_tensor(t8, x8, wide(tabq[:, 2 * which + 1, t, :], heads), ALU.mult))
                    link(dve.tensor_tensor(x8, x8, wide(tabq[:, 2 * which, t, :], heads), ALU.mult))
                    x16 = temp(t, 0).rearrange("p (g d) -> p g d", g=2 * heads)
                    t16 = temp(t, 1).rearrange("p (g d) -> p g d", g=2 * heads)
                    for o in outs(t, x16, t16):
                        o16, xx, tt_ = o
                        dve.tensor_tensor(o16[:, :, 0:16], xx[:, :, 0:16], tt_[:, :, 16:32], ALU.subtract).then_inc(sem(sems_[1]), 1)
                        dve.tensor_tensor(o16[:, :, 16:32], xx[:, :, 16:32], tt_[:, :, 0:16], ALU.add).then_inc(sem(sems_[1]), 1)

            head_norm_rope(BH, lambda t: sm2[:, t, 0:512], lambda t: PJ[buf("bq")][:, t, :], "bsq_ready", 2, 0,
                           lambda t, i: xn[:, t, 512 * i:512 * i + 512],
                           lambda t, x, z: [(rt[:, t, :].rearrange("p (g d) -> p g d", g=16), x, z)],
                           ("bqn_ready", "brope_ready"), end_pair("bq") + RING)

            def twice(t, x, z):
                out_ = []
                for h in range(2):
                    for c in range(2):
                        a = 256 + P * h + HD * c
                        out_.append((xn[:, t, a:a + HD].rearrange("p (g d) -> p g d", g=2), x[:, 2 * h:2 * h + 2, :], z[:, 2 * h:2 * h + 2, :]))
                return out_

            def silu(nm, th):
                i = SILU_ORDER.index(nm)
                for t in range(TT):
                    dve.wait_ge(sem("th_ready"), 2 * i + t + 1)
                    dve.scalar_tensor_tensor(out=gat[:, i, t, :], in0=th[:, t, 0:512], scalar=1.0, in1=PJ[buf(nm)][:, t, :],
                                             op0=ALU.add, op1=ALU.mult).then_inc(sem("silu_ready"), 1)

            lo_upto(end_pair("gb") + 3)
            silu("gb", sm2)
            lo_upto(end_pair("bkv") + 3)
            dve.wait_ge(sem("brope_ready"), 4)
            dve.wait_ge(sem("bv_ready"), 2)
            head_norm_rope(2, lambda t: pT2[:, t, 0, :], lambda t: PJ[buf("bkv")][:, t, 0:P], "bksq_ready", 2, 1,
                           lambda t, i: xn[:, t, P * i:P * i + P], twice, ("bkn_ready", "bkrope_ready"), end_pair("bkv") + RING)

            lo_upto(end_pair("gm") + 3)
            silu("gm", sm2)

            def rot_terms(c):
                nm = A_CHUNKS[c]
                dve.wait_ge(pair_used, end_pair(nm))
                if c:
                    dve.wait_ge(sem("a_rope"), 4 * c)
                else:
                    dve.wait_ge(sem("b_tr"), 2)
                for t in range(TT):
                    g8 = PJ[buf(nm)][:, t, :].rearrange("p (g d) -> p g d", g=8)
                    for i, tb in enumerate((cosv, sinv)):
                        o8 = xn[:, t, i * 512:(i + 1) * 512].rearrange("p (g d) -> p g d", g=8)
                        dve.tensor_tensor(o8, g8, wide(tb[:, t, :], 8), ALU.mult).then_inc(sem("rot_terms"), 1)

            for c, nm in enumerate(A_CHUNKS):
                for j in range(4):
                    n = 4 * c + j
                    lo_upto(F2 + n + 3)
                    if j == 0 and 1 <= c <= 6:
                        rot_terms(c - 1)
                    for k in bm_slots(n):
                        if k < len(BM):
                            br, h, t = BM[k]
                            dve.wait_ge(sem("bm_sc"), k + 1)
                            if k >= 4:
                                dve.wait_ge(sem("bm_out"), k - 3)
                            link(dve.tensor_reduce(sx[:, k % 4, 0:1], S0[:, 0:TOK], AX.X, ALU.max))
                            dve.tensor_scalar(sx[:, k % 4, 1:2], sx[:, k % 4, 0:1], -((HD if br == "b" else MD) ** -0.5), None,
                                              ALU.mult).then_inc(sem("bm_nb"), 1)
                        if k >= 1 and k - 1 < len(BM):
                            dve.wait_ge(sem("bm_exp"), k)
                            dve.reciprocal(sx[:, (k - 1) % 4, 3:4], sx[:, (k - 1) % 4, 2:3]).then_inc(sem("bm_rl"), 1)
                        if k >= 2:
                            k2 = k - 2
                            br, h, t = BM[k2]
                            w = HD if br == "b" else MD
                            o = gat[:, "bm".index(br), t, h * w:(h + 1) * w]
                            dve.wait_ge(sem("bm_pv"), k2 + 1)
                            dve.wait_ge(sem("bm_rl"), k2 + 1)
                            dve.scalar_tensor_tensor(out=o, in0=T1[:, 0:w], scalar=sx[:, k2 % 4, 3:4], in1=o,
                                                     op0=ALU.mult, op1=ALU.mult).then_inc(sem("bm_out"), 1)
            lo_upto(F3 + 2)
            silu("ga", rt)
            dve.wait_ge(sem("ma_landed"), 16)
            for n in range(24):
                lo_upto(F3 + n + 3)
                if n % 4 == 0 and n:
                    gate_sum(dve, n // 4 - 1)
                for k in a_slots(n):
                    if k < AH * TT:
                        h, t = divmod(k, TT)
                        dve.wait_ge(sem("a_sc"), k + 1)
                        if k >= 2:
                            dve.wait_ge(sem("a_ptr"), k - 1)
                        if k >= 4:
                            dve.wait_ge(sem("a_out"), k - 3)
                        mk = ma[:, t * TOK:].rearrange("p (g n) -> p g n", n=TOK)[:, 0:3 - t:2 - t, :]
                        dve.tensor_tensor_reduce(sm2[:, k % 2, 0:512].rearrange("p (g n) -> p g n", g=2),
                                                 S0[:, :].rearrange("p (g n) -> p g n", g=2), mk, 1.0, BIG, ALU.add, ALU.max,
                                                 sx[:, k % 4, 4:5]).then_inc(sem("a_max"), 1)
                        dve.tensor_tensor_reduce(sm2[:, k % 2, 512:768], S1[:, 0:TOK], ma[:, 3 * TOK:4 * TOK], 1.0, BIG, ALU.add,
                                                 ALU.max, sx[:, k % 4, 5:6]).then_inc(sem("a_max"), 1)
                        dve.wait_ge(sem("a_max"), 2 * k + 2)
                        link(dve.tensor_tensor(sx[:, k % 4, 0:1], sx[:, k % 4, 4:5], sx[:, k % 4, 5:6], ALU.max))
                        dve.tensor_scalar(sx[:, k % 4, 1:2], sx[:, k % 4, 0:1], -(HD ** -0.5), None, ALU.mult).then_inc(sem("a_nb"), 1)
                    if k >= 1 and k - 1 < AH * TT:
                        dve.wait_ge(sem("a_exp"), k)
                        dve.reciprocal(sx[:, (k - 1) % 4, 3:4], sx[:, (k - 1) % 4, 2:3]).then_inc(sem("a_rl"), 1)
                    if k >= 2:
                        h, t = divmod(k - 2, TT)
                        o = gat[:, 2, t, h * HD:(h + 1) * HD]
                        dve.wait_ge(sem("apv_done"), k - 1)
                        dve.wait_ge(sem("a_rl"), k - 1)
                        dve.scalar_tensor_tensor(out=o, in0=S1[:, TOK:TOK + HD], scalar=sx[:, (k - 2) % 4, 3:4], in1=o,
                                                 op0=ALU.mult, op1=ALU.mult).then_inc(sem("a_out"), 1)
            gate_sum(dve, 5)
            for i in range(6):
                if i == 4:
                    lo_upto(F3 + 24 + RING)
                dve.wait_ge(sem("o_hi"), i + 1)
                dve.scalar_tensor_tensor(out=otl[:, 2 * i:2 * i + 2, :], in0=OBANKS[i % 4][:, :].rearrange("p (f n) -> p f n", f=2),
                                         scalar=0.5, in1=oth[:, 2 * i:2 * i + 2, :].bitcast(F32),
                                         op0=ALU.mult, op1=ALU.subtract).then_inc(sem("o_lo"), 1)
            for i, b in enumerate(BRANCH_ORDER):
                nm = "br" + b
                n = int(b[1])
                lo_upto(min(end_pair(nm) + 3, FIRST[chunk("wo0")] + 3))
                dve.wait_ge(pair_used, end_pair(nm))
                dve.wait_ge(sem("gate_ready"), 6)
                at_ = "abm".index(b[0]) * D + 512 * n
                for t in range(TT):
                    g = gt[:, t, at_:at_ + 512]
                    o = merged[:, t, 512 * n:512 * n + 512] if b[0] == "b" else g
                    dve.scalar_tensor_tensor(out=o, in0=g, scalar=1.0, in1=PJ[buf(nm)][:, t, :],
                                             op0=ALU.add, op1=ALU.mult).then_inc(sem("y_gated"), 1)
                if i == 5:
                    for t in range(TT):
                        dve.wait_ge(sem("y_gated"), 2 * i + t + 1)
                        dve.wait_ge(sem("merged_m"), 2 * n + t + 1)
                        m = merged[:, t, 512 * n:512 * n + 512]
                        dve.tensor_tensor(m, m, gt[:, t, at_:at_ + 512], ALU.add).then_inc(sem("merged_ready_dve"), 1)
            for i in range(4):
                dve.wait_ge(sem("m_hi"), i + 1)
                dve.scalar_tensor_tensor(out=xtl[:, 2 * i:2 * i + 2, :], in0=AUX[i][:, :].rearrange("p (f n) -> p f n", f=2),
                                         scalar=0.5, in1=xth[:, 2 * i:2 * i + 2, :].bitcast(F32),
                                         op0=ALU.mult, op1=ALU.subtract).then_inc(sem("m_lo"), 1)
            lo_upto(NPAIRS)
            dve.wait_ge(sem("gpost_landed"), 16)
            for t in range(TT):
                dve.wait_ge(sem("rstd_ready"), 12 + t + 1)
                for i in range(2):
                    half = slice(512 * i, 512 * i + 512)
                    dve.scalar_tensor_tensor(out=xn[:, t, half], in0=PJ[buf(f"wo{i}")][:, t, :], scalar=rstd[:, 6, t:t + 1],
                                             in1=gpost[:, half], op0=ALU.mult, op1=ALU.mult).then_inc(sem("wo_scaled"), 1)
                for i in range(2):
                    half = slice(512 * i, 512 * i + 512)
                    dve.wait_ge(sem("wo_scaled"), 2 * t + i + 1)
                    dve.tensor_tensor(xn[:, t, half], xn[:, t, half], xres[:, t, half], ALU.add).then_inc(sem("y_ready"), 1)

def conv_col(l, j, i):
    tile = 2 * j + i % 2 + (FT if i >= 2 else 0)
    return COL["conv"][0] + (l * 2 * FT + tile) * 4


def rope_table(pos, half, width):
    inv = 10000.0 ** (-np.arange(half, dtype=np.float64) / half)
    a = pos[:, None] * inv[None, :]
    a = np.concatenate([a, a], axis=1)
    return np.cos(a), np.sin(a)


def by_partition(a):
    return np.ascontiguousarray(a.reshape(TT, P, -1).transpose(1, 0, 2).reshape(P, -1))


def constants():
    pos = np.arange(TOK)
    cos, sin = rope_table(pos, 32, 64)
    rc, rs = rope_table(pos // 64, 16, 32)
    cc, cs_ = rope_table(pos % 64, 16, 32)
    own = pos[:, None] // 64
    diff = np.where(pos[None, :] // 64 <= own, 0.0, NEG)
    parts = [np.eye(P), by_partition(cos), by_partition(sin), by_partition(np.concatenate([rc, cc], 1)),
             by_partition(np.concatenate([rs, cs_], 1)), diff[0:128, 0:128], diff[128:256, 0:256]]
    return np.concatenate(parts, axis=1).astype(np.float32)


def window_masks():
    q, k = np.arange(TOK)[:, None], np.arange(TOK)[None, :]
    near = np.abs(q - k) <= 64
    parts = [near[0:P], near[P:]] + [((q - k) % d == 0)[0:P] for d in (4, 16)]
    return np.where(np.concatenate(parts, axis=1), 0.0, NEG).astype(np.float32)


def layout(i):
    def cut(w, n):
        return w.reshape(w.shape[0] // P, P, w.shape[1])

    tiles = {}
    for l in range(LAYERS):
        w = i["w_in"][l]
        at = 0
        for nm, n in (("ssm_u", 256), ("gmlp", 512), ("q", 512), ("k", 512), ("v", 512)):
            tiles[f"{nm}{l}"] = w[:, at:at + n]
            at += n
        for j in range(2):
            w_out = i["w_out"][l][:, 512 * j:512 * j + 512].reshape(4, D // 4, 512)
            tiles[f"out{l}_{j}"] = np.concatenate([w_out[k] for k in OUT_PAIRS], 0)
            tiles[f"down{l}_{j}"] = i["w_down"][l][:, 512 * j:512 * j + 512]
        for j in range(UNITS):
            up = i["w_up"][l]
            tiles[f"up{l}_{j}"] = np.concatenate([up[:, 256 * j:256 * j + 256], up[:, FF + 256 * j:FF + 256 * j + 256]], 1)
    w = i["w_in_2"][0]
    at = 0
    for nm, n in [(f"a{c}{g}", 512) for c in "qkv" for g in range(NG)] + \
            [("bq", 512), ("bkv", 256), ("mq", 512), ("ga", 512), ("gb", 512), ("gm", 512)] + [(f"mg{j}", 512) for j in range(6)]:
        tiles[nm] = w[:, at:at + n]
        at += n
    tiles["km"], tiles["vm"] = i["w_mem_kv_2"][0][:, 0:512], i["w_mem_kv_2"][0][:, 512:1024]
    for j in range(2):
        for b in "abm":
            tiles[f"br{b}{j}"] = i[f"w_br_{b}_2"][0][:, 512 * j:512 * j + 512]
        tiles[f"wo{j}"] = i["w_out_2"][0][:, 512 * j:512 * j + 512]
    weights = np.empty((NPAIRS, P, 1024), np.float32)
    for (nm, k, n), first, pairs in zip(CHUNKS, FIRST, PAIRS):
        per = 1024 // n
        weights[first:first + pairs] = tiles[nm].reshape(pairs, per, P, n).transpose(0, 2, 1, 3).reshape(pairs, P, 1024)

    cols = np.zeros((P, NCOL), np.float32)

    def put(name, a, at=0):
        a = a.reshape(-1, P).T
        cols[:, COL[name][0] + at:COL[name][0] + at + a.shape[1]] = a

    put("are", i["ssm_a_re"])
    put("aim", i["ssm_a_im"])
    put("ldt", np.repeat(i["ssm_log_dt"].reshape(-1), STATE))
    put("gattn", i["attn_norm_g"])
    put("gffn", i["ffn_norm_g"])
    put("dskip", i["ssm_d"])
    put("bglu", i["ssm_b_glu"])
    put("bs", i["gmlp_b_s"])
    put("gpre", i["g_pre_2"])
    put("gmem", i["g_mem_2"])
    conv = np.concatenate([i["conv_w"], i["conv_b"][:, None, :]], axis=1)
    put("conv", conv.reshape(LAYERS, 4, 2 * FT, P).transpose(0, 2, 1, 3))
    rows = np.zeros((1, NROW), np.float32)
    for name, src in (("vg", "gmlp_v_g"), ("qg", "q_norm_g"), ("kg", "k_norm_g"), ("sub", "subln_g"),
                      ("qn2", "q_norm_2"), ("kn2", "k_norm_2")):
        a, b = ROW[name]
        rows[0, a:b] = i[src].reshape(-1)
    bexp = np.zeros((LAYERS, P, 2, 2, P), np.float32)
    cexp = np.zeros((LAYERS, P, 2, ST, 32), np.float32)
    for c, (b, m) in enumerate((("ssm_b_re", "ssm_c_re"), ("ssm_b_im", "ssm_c_im"))):
        for g in range(GROUPS):
            s, half, ch = g // 2, (g % 2) * STATE, (g % 8) * GCH
            bexp[:, ch:ch + GCH, c, s // 4, half:half + STATE] = i[b][:, g].transpose(0, 2, 1)
            cexp[:, half:half + STATE, c, s, ch % 32:ch % 32 + GCH] = i[m][:, g].transpose(0, 2, 1)
    return {
        "weights": weights, "x": i["x"].reshape(TOK, D), "mem": i["mem_2"].reshape(TOK, D), "cols": cols, "rows": rows,
        "lams": np.concatenate([i[f"lambda_{z}"].reshape(1, -1) for z in ("q1", "k1", "q2", "k2")], axis=1),
        "bmerge": np.concatenate([i["b_merge_2"].reshape(1, -1), i["g_post_2"].reshape(1, -1)], axis=1),
        "consts": constants(), "amask": window_masks(), "bexp": bexp, "cexp": cexp,
        "wst": np.ascontiguousarray(i["gmlp_w_s"].transpose(0, 3, 1, 2)),
        "wglu": np.ascontiguousarray(i["ssm_w_glu"].reshape(LAYERS, 2, P, 256).transpose(0, 2, 1, 3)),
    }


def kernel(**inputs):
    import concourse.bacc as bacc
    from concourse.bass_utils import run_bass_kernel_spmd

    nc = bacc.Bacc("TRN2", target_bir_lowering=False, num_devices=1)
    arrays = {f"{k}_in": np.ascontiguousarray(v) for k, v in layout({k: np.asarray(v) for k, v in inputs.items()}).items()}
    args = {k[:-3]: nc.dram_tensor(k, a.shape, mybir.dt.from_np(a.dtype), kind="ExternalInput").ap() for k, a in arrays.items()}
    out = nc.dram_tensor("y_out", (TOK, D), F32, kind="ExternalOutput").ap()
    build(nc, out=out, **args)
    r = run_bass_kernel_spmd(nc, [arrays], core_ids=[0])
    return r.results[0]["y_out"].reshape(1, TOK, D)
```
